# Optimizing a Trainium2 kernel written in Bass

```python
import math
import jax, jax.numpy as jnp
from jax import lax
import numpy as np

D_MODEL = 1024
BATCH = 1
SEQ = 256
DEPTH = 2

CHUNK = 64
RET_HEADS = 4
RET_DK = 128
RET_DV = 256
CA_HEADS = 8
CA_DH = 64
CA_LEFT_CHUNKS = 8
REL_CLIP = 256
DA_HEADS = 4
DA_DH = 64
Q_BLOCK = 128
FFN_HIDDEN = -(-8 * D_MODEL // (3 * 256)) * 256
ROPE_THETA = 10000.0
LN_EPS = 1e-5
NEG_INF = -1e30
DEEPNORM_ALPHA = (2.0 * DEPTH) ** 0.25
DEEPNORM_BETA = (8.0 * DEPTH) ** -0.25
N_BRANCHES = 3

RET_QK_W = RET_HEADS * RET_DK
RET_V_W = RET_HEADS * RET_DV
CA_W = CA_HEADS * CA_DH
DA_QK_W = 2 * DA_HEADS * DA_DH
DA_V_W = DA_HEADS * 2 * DA_DH
IN_WIDTHS = (RET_QK_W, RET_QK_W, RET_V_W, RET_V_W, CA_W, CA_W, CA_W, DA_QK_W, DA_QK_W, DA_V_W, N_BRANCHES * D_MODEL)
IN_IS_VALUE = (False, False, True, False, False, False, True, False, False, True, False)
IN_TOTAL = sum(IN_WIDTHS)


def _layer_norm(x, g, b):
    xf = x.astype(jnp.float32)
    mu = jnp.mean(xf, axis=-1, keepdims=True)
    var = jnp.mean(jnp.square(xf - mu), axis=-1, keepdims=True)
    return ((xf - mu) * lax.rsqrt(var + LN_EPS) * g.astype(jnp.float32) + b.astype(jnp.float32)).astype(x.dtype)

def _rms_norm(x, g):
    xf = x.astype(jnp.float32)
    y = xf * lax.rsqrt(jnp.mean(xf * xf, axis=-1, keepdims=True) + LN_EPS) * g.astype(jnp.float32)
    return y.astype(x.dtype)

def _rotary(x):
    S, d = x.shape[1], x.shape[-1]
    inv_freq = ROPE_THETA ** (-jnp.arange(0, d, 2, dtype=jnp.float32) / d)
    ang = jnp.arange(S, dtype=jnp.float32)[:, None] * inv_freq[None, :]
    cos = jnp.cos(ang)[None, :, None, :].astype(x.dtype)
    sin = jnp.sin(ang)[None, :, None, :].astype(x.dtype)
    x1, x2 = x[..., : d // 2], x[..., d // 2:]
    return jnp.concatenate([x1 * cos - x2 * sin, x2 * cos + x1 * sin], axis=-1)

def _retention(q, k, v, gate, norm_g):
    B, S, H, dk = q.shape
    dv = v.shape[-1]
    nc = S // CHUNK
    q = _rotary(q)
    k = _rotary(k) * (dk ** -0.5)
    log_gamma = jnp.log1p(-jnp.exp2(-5.0 - jnp.arange(H, dtype=jnp.float32)))
    pos = jnp.arange(CHUNK, dtype=jnp.float32)
    intra_decay = jnp.exp(log_gamma[:, None, None] * jnp.abs(pos[:, None] - pos[None, :]))
    q_decay = jnp.exp(log_gamma[None, :] * (pos[:, None] + 1.0))
    k_decay = jnp.exp(log_gamma[None, :] * (CHUNK - 1.0 - pos[:, None]))
    chunk_decay = jnp.exp(log_gamma * CHUNK)

    qc = q.reshape(B, nc, CHUNK, H, dk)
    kc = k.reshape(B, nc, CHUNK, H, dk)
    vc = v.reshape(B, nc, CHUNK, H, dv)
    scores = jnp.einsum('bcnhd,bcmhd->bchnm', qc, kc) * intra_decay.astype(q.dtype)
    o_intra = jnp.einsum('bchnm,bcmhe->bcnhe', scores, vc)

    def step(state, xs):
        q_i, k_i, v_i = xs
        o = jnp.einsum('bnhd,bhde->bnhe', q_i.astype(jnp.float32) * q_decay[None, :, :, None], state)
        kv = jnp.einsum('bmhd,bmhe->bhde', k_i.astype(jnp.float32) * k_decay[None, :, :, None], v_i.astype(jnp.float32))
        state = state * chunk_decay[None, :, None, None] + kv
        return state, o

    state0 = jnp.zeros((B, H, dk, dv), jnp.float32)
    _, o_inter = lax.scan(step, state0, (jnp.swapaxes(qc, 0, 1), jnp.swapaxes(kc, 0, 1), jnp.swapaxes(vc, 0, 1)))
    o = (o_intra.astype(jnp.float32) + jnp.swapaxes(o_inter, 0, 1)).astype(v.dtype)
    o = _rms_norm(o, norm_g).reshape(B, S, H * dv)
    return jax.nn.silu(gate) * o

def _chunk_attention(q, k, v, rel_bias):
    B, S, H, d = q.shape
    nc = S // CHUNK
    pad = CA_LEFT_CHUNKS * CHUNK
    band = pad + CHUNK
    k_pad = jnp.pad(k, ((0, 0), (pad, 0), (0, 0), (0, 0)))
    v_pad = jnp.pad(v, ((0, 0), (pad, 0), (0, 0), (0, 0)))
    qpos = jnp.arange(CHUNK)
    kpos = jnp.arange(band)
    rel = qpos[:, None] + pad - kpos[None, :]
    idx = jnp.clip(rel, -REL_CLIP, REL_CLIP) + REL_CLIP
    bias = rel_bias[:, idx].astype(jnp.float32)
    q = q * (d ** -0.5)

    def one_chunk(i):
        start = i * CHUNK
        q_i = lax.dynamic_slice_in_dim(q, start, CHUNK, axis=1)
        k_i = lax.dynamic_slice_in_dim(k_pad, start, band, axis=1)
        v_i = lax.dynamic_slice_in_dim(v_pad, start, band, axis=1)
        s = jnp.einsum('bqhd,bkhd->bhqk', q_i, k_i).astype(jnp.float32) + bias[None]
        valid = (start - pad + kpos) >= 0
        s = jnp.where(valid[None, None, None, :], s, NEG_INF)
        p = jax.nn.softmax(s, axis=-1).astype(v.dtype)
        return jnp.einsum('bhqk,bkhd->bqhd', p, v_i)

    o = lax.map(one_chunk, jnp.arange(nc))
    return jnp.transpose(o, (1, 0, 2, 3, 4)).reshape(B, S, H * d)

def _diff_attention(q, k, v, lam, lambda_init, norm_g):
    B, S, H2, d = q.shape
    H = H2 // 2
    q = _rotary(q) * (d ** -0.5)
    k = _rotary(k)
    nb = S // Q_BLOCK
    key_chunk = jnp.arange(S) // CHUNK

    def one_block(i):
        start = i * Q_BLOCK
        q_i = lax.dynamic_slice_in_dim(q, start, Q_BLOCK, axis=1)
        s = jnp.einsum('bqgd,bkgd->bgqk', q_i, k).astype(jnp.float32)
        query_chunk = (start + jnp.arange(Q_BLOCK)) // CHUNK
        allowed = key_chunk[None, :] <= query_chunk[:, None]
        s = jnp.where(allowed[None, None], s, NEG_INF)
        p = jax.nn.softmax(s, axis=-1).reshape(B, H, 2, Q_BLOCK, S)
        p = p[:, :, 0] - lam * p[:, :, 1]
        return jnp.einsum('bhqk,bkhe->bqhe', p.astype(v.dtype), v)

    o = lax.map(one_block, jnp.arange(nb))
    o = jnp.transpose(o, (1, 0, 2, 3, 4)).reshape(B, S, H, 2 * d)
    o = _rms_norm(o, norm_g) * (1.0 - lambda_init)
    return o.reshape(B, S, H * 2 * d)

def first_inputs(seed: int = 0) -> dict:
    key = jax.random.key(seed)
    ks = jax.random.split(key, 24)

    def nrm(k, shape, scale):
        return jax.random.normal(k, shape, jnp.float32) * scale

    beta = DEEPNORM_BETA
    col_scale = jnp.concatenate([
        jnp.full((w,), beta if is_v else 1.0, jnp.float32) for w, is_v in zip(IN_WIDTHS, IN_IS_VALUE)])
    x = nrm(ks[0], (BATCH, SEQ, D_MODEL), 1.0)
    w_in = nrm(ks[1], (DEPTH, D_MODEL, IN_TOTAL), D_MODEL ** -0.5) * col_scale
    ret_norm_g = 1.0 + nrm(ks[2], (DEPTH, RET_DV), 0.02)
    ca_rel_bias = nrm(ks[3], (DEPTH, CA_HEADS, 2 * REL_CLIP + 1), 0.1)
    da_lambda_q1 = nrm(ks[4], (DEPTH, DA_DH), 0.1)
    da_lambda_k1 = nrm(ks[5], (DEPTH, DA_DH), 0.1)
    da_lambda_q2 = nrm(ks[6], (DEPTH, DA_DH), 0.1)
    da_lambda_k2 = nrm(ks[7], (DEPTH, DA_DH), 0.1)
    da_norm_g = 1.0 + nrm(ks[8], (DEPTH, 2 * DA_DH), 0.02)
    w_branch_a = nrm(ks[9], (DEPTH, RET_V_W, D_MODEL), RET_V_W ** -0.5 * beta)
    w_branch_b = nrm(ks[10], (DEPTH, CA_W, D_MODEL), CA_W ** -0.5 * beta)
    w_branch_c = nrm(ks[11], (DEPTH, DA_V_W, D_MODEL), DA_V_W ** -0.5 * beta)
    b_merge = nrm(ks[12], (DEPTH, N_BRANCHES * D_MODEL), 0.1)
    w_out = nrm(ks[13], (DEPTH, D_MODEL, D_MODEL), D_MODEL ** -0.5 * beta)
    ln1_g = 1.0 + nrm(ks[14], (DEPTH, D_MODEL), 0.02)
    ln1_b = nrm(ks[15], (DEPTH, D_MODEL), 0.02)
    w_ffn_in = nrm(ks[16], (DEPTH, D_MODEL, 2 * FFN_HIDDEN), D_MODEL ** -0.5 * beta)
    w_ffn_out = nrm(ks[17], (DEPTH, FFN_HIDDEN, D_MODEL), FFN_HIDDEN ** -0.5 * beta)
    ln2_g = 1.0 + nrm(ks[18], (DEPTH, D_MODEL), 0.02)
    ln2_b = nrm(ks[19], (DEPTH, D_MODEL), 0.02)
    return {
        "x": x, "w_in": w_in, "ret_norm_g": ret_norm_g, "ca_rel_bias": ca_rel_bias,
        "da_lambda_q1": da_lambda_q1, "da_lambda_k1": da_lambda_k1,
        "da_lambda_q2": da_lambda_q2, "da_lambda_k2": da_lambda_k2, "da_norm_g": da_norm_g,
        "w_branch_a": w_branch_a, "w_branch_b": w_branch_b, "w_branch_c": w_branch_c,
        "b_merge": b_merge, "w_out": w_out, "ln1_g": ln1_g, "ln1_b": ln1_b,
        "w_ffn_in": w_ffn_in, "w_ffn_out": w_ffn_out, "ln2_g": ln2_g, "ln2_b": ln2_b,
    }

def first_block(x, w_in, ret_norm_g, ca_rel_bias, da_lambda_q1, da_lambda_k1, da_lambda_q2, da_lambda_k2,
              da_norm_g, w_branch_a, w_branch_b, w_branch_c, b_merge, w_out, ln1_g, ln1_b,
              w_ffn_in, w_ffn_out, ln2_g, ln2_b):
    B, S, D = x.shape
    splits = [int(s) for s in np.cumsum(IN_WIDTHS)[:-1]]
    for l in range(DEPTH):
        h = jnp.einsum('bsd,de->bse', x, w_in[l])
        rq, rk, rv, rg, cq, ck, cv, dq, dk, dv, gates = jnp.split(h, splits, axis=-1)

        o_a = _retention(rq.reshape(B, S, RET_HEADS, RET_DK), rk.reshape(B, S, RET_HEADS, RET_DK),
                         rv.reshape(B, S, RET_HEADS, RET_DV), rg, ret_norm_g[l])
        o_b = _chunk_attention(cq.reshape(B, S, CA_HEADS, CA_DH), ck.reshape(B, S, CA_HEADS, CA_DH),
                               cv.reshape(B, S, CA_HEADS, CA_DH), ca_rel_bias[l])
        lambda_init = 0.8 - 0.6 * math.exp(-0.3 * l)
        lam = (jnp.exp(jnp.sum(da_lambda_q1[l].astype(jnp.float32) * da_lambda_k1[l].astype(jnp.float32)))
               - jnp.exp(jnp.sum(da_lambda_q2[l].astype(jnp.float32) * da_lambda_k2[l].astype(jnp.float32)))
               + lambda_init)
        o_c = _diff_attention(dq.reshape(B, S, 2 * DA_HEADS, DA_DH), dk.reshape(B, S, 2 * DA_HEADS, DA_DH),
                              dv.reshape(B, S, DA_HEADS, 2 * DA_DH), lam, lambda_init, da_norm_g[l])

        g = jax.nn.sigmoid(gates + b_merge[l]).reshape(B, S, N_BRANCHES, D)
        merged = (g[:, :, 0] * jnp.einsum('bse,ed->bsd', o_a, w_branch_a[l])
                  + g[:, :, 1] * jnp.einsum('bse,ed->bsd', o_b, w_branch_b[l])
                  + g[:, :, 2] * jnp.einsum('bse,ed->bsd', o_c, w_branch_c[l]))
        mix = jnp.einsum('bsd,de->bse', merged, w_out[l])
        x = _layer_norm(DEEPNORM_ALPHA * x + mix, ln1_g[l], ln1_b[l])

        u = jnp.einsum('bsd,df->bsf', x, w_ffn_in[l])
        u_gate, u_up = jnp.split(u, 2, axis=-1)
        ffn = jnp.einsum('bsf,fd->bsd', jax.nn.silu(u_gate) * u_up, w_ffn_out[l])
        x = _layer_norm(DEEPNORM_ALPHA * x + ffn, ln2_g[l], ln2_b[l])
    return x


D_CONV = 256
CONV_GROUPS = 4
CONV_WIDTH = 3
D_GMLP = 256
GMLP_HEADS = 4
GMLP_HEAD_DIM = D_GMLP // GMLP_HEADS
GMLP_CHUNK = 128
HEAD_DIM = 64
NSA_HEADS = 8
NSA_KV_HEADS = 2
NSA_GROUP = NSA_HEADS // NSA_KV_HEADS
D_NSA = NSA_HEADS * HEAD_DIM
D_KV = NSA_KV_HEADS * HEAD_DIM
D_MIX = D_CONV + D_GMLP + D_NSA
D_IN_PROJ = 3 * D_CONV + 2 * D_GMLP + D_NSA + 6 * D_KV + 3 * NSA_HEADS
CMP_LEN = 32
CMP_STRIDE = 16
CMP_HIDDEN = 128
SEL_BLOCK = 64
N_SELECT = 16
WINDOW = 512
D_FF = 2816
ALPHA = (2 * DEPTH) ** 0.25
BETA = (8 * DEPTH) ** -0.25
NEG = -1e30


def layer_norm(x, g, b):
    xf = x.astype(jnp.float32)
    mu = jnp.mean(xf, axis=-1, keepdims=True)
    var = jnp.mean(jnp.square(xf - mu), axis=-1, keepdims=True)
    return ((xf - mu) * lax.rsqrt(var + LN_EPS) * g + b).astype(x.dtype)

def swiglu(x, w_gate, w_up, w_down):
    return (jax.nn.silu(x @ w_gate) * (x @ w_up)) @ w_down

def masked_softmax(s, mask):
    p = jax.nn.softmax(jnp.where(mask, s.astype(jnp.float32), NEG), axis=-1)
    return p * mask

def short_conv(h, b_gate, c_gate, w_conv):
    z = c_gate * h
    y = lax.conv_general_dilated(
        z, w_conv[:, None, :], window_strides=(1,),
        padding=[(CONV_WIDTH - 1, 0)],
        dimension_numbers=("NWC", "WIO", "NWC"),
        feature_group_count=D_CONV)
    return b_gate * y

def gmlp_spatial(uv, ln_g, ln_b, w_s, b_s):
    bn, s = uv.shape[:2]
    z = jax.nn.gelu(uv)
    u, v = z[..., :D_GMLP], z[..., D_GMLP:]
    v = layer_norm(v, ln_g, ln_b)
    v = v.reshape(bn, s // GMLP_CHUNK, GMLP_CHUNK, GMLP_HEADS, GMLP_HEAD_DIM)
    tril = jnp.tril(jnp.ones((GMLP_CHUNK, GMLP_CHUNK), dtype=bool))
    w = jnp.where(tril[None], w_s, 0.0)
    sv = jnp.einsum("hpq,bcqhd->bcphd", w, v) + b_s.T[:, :, None]
    return u * sv.reshape(bn, s, D_GMLP)

def compress_kv(k, pe, w1, b1, w2):
    s = k.shape[1]
    n_cmp = (s - CMP_LEN) // CMP_STRIDE + 1
    idx = np.arange(n_cmp)[:, None] * CMP_STRIDE + np.arange(CMP_LEN)[None, :]
    kb = k[:, idx]
    h = jax.nn.gelu(jnp.einsum("bnlgd,ldf->bngf", kb + pe[:, None, :], w1) + b1)
    return jnp.einsum("bngf,fe->bnge", h, w2)

def cmp_to_sel_overlap(n_cmp, n_blk):
    st = np.arange(n_cmp) * CMP_STRIDE
    bs = np.arange(n_blk) * SEL_BLOCK
    ov = np.minimum(st[:, None] + CMP_LEN, bs[None, :] + SEL_BLOCK) - np.maximum(st[:, None], bs[None, :])
    return jnp.asarray(np.clip(ov, 0, None) / CMP_LEN, dtype=jnp.float32)

def nsa_attention(q, k_cmp, v_cmp, k_slc, v_slc, k_win, v_win, gate_logits,
                  ck_pe, ck_w1, ck_b1, ck_w2, cv_pe, cv_w1, cv_b1, cv_w2):
    bn, s = q.shape[:2]
    G, R, dh = NSA_KV_HEADS, NSA_GROUP, HEAD_DIM
    q = q.reshape(bn, s, G, R, dh)
    k_cmp, v_cmp, k_slc, v_slc, k_win, v_win = [
        a.reshape(bn, s, G, dh) for a in (k_cmp, v_cmp, k_slc, v_slc, k_win, v_win)]
    scale = dh ** -0.5
    n_cmp = (s - CMP_LEN) // CMP_STRIDE + 1
    n_blk = s // SEL_BLOCK
    n_sel = min(N_SELECT, n_blk)
    t = jnp.arange(s)

    kc = compress_kv(k_cmp, ck_pe, ck_w1, ck_b1, ck_w2)
    vc = compress_kv(v_cmp, cv_pe, cv_w1, cv_b1, cv_w2)
    sc = jnp.einsum("bsgrd,bngd->bgrsn", q, kc) * scale
    cmp_end = jnp.arange(n_cmp) * CMP_STRIDE + CMP_LEN - 1
    pc = masked_softmax(sc, cmp_end[None, :] <= t[:, None])
    o_cmp = jnp.einsum("bgrsn,bngd->bsgrd", pc.astype(vc.dtype), vc)

    imp = jnp.einsum("bgrsn,nj->bgsj", pc, cmp_to_sel_overlap(n_cmp, n_blk))
    j = jnp.arange(n_blk)
    cur = (t // SEL_BLOCK)[:, None]
    valid = j[None, :] <= cur
    forced = (j[None, :] == 0) | (j[None, :] == cur) | (j[None, :] == cur - 1)
    score = jnp.where(valid, imp, NEG)
    score = jnp.where(forced, -NEG, score)
    _, sel = lax.top_k(score, n_sel)

    ks_blk = k_slc.reshape(bn, n_blk, SEL_BLOCK, G, dh).transpose(0, 3, 1, 2, 4)
    vs_blk = v_slc.reshape(bn, n_blk, SEL_BLOCK, G, dh).transpose(0, 3, 1, 2, 4)
    kw_pad = jnp.pad(k_win, ((0, 0), (WINDOW, 0), (0, 0), (0, 0)))
    vw_pad = jnp.pad(v_win, ((0, 0), (WINDOW, 0), (0, 0), (0, 0)))
    bi = jnp.arange(bn)[:, None, None, None]
    gi = jnp.arange(G)[None, :, None, None]

    def query_block(i):
        s0 = i * Q_BLOCK
        qb = lax.dynamic_slice_in_dim(q, s0, Q_BLOCK, axis=1)
        tq = s0 + jnp.arange(Q_BLOCK)
        idx = lax.dynamic_slice_in_dim(sel, s0, Q_BLOCK, axis=2)
        kg = ks_blk[bi, gi, idx]
        vg = vs_blk[bi, gi, idx]
        ss = jnp.einsum("bqgrd,bgqnkd->bgrqnk", qb, kg) * scale
        kpos = idx[..., None] * SEL_BLOCK + jnp.arange(SEL_BLOCK)
        ms = (kpos <= tq[None, None, :, None, None])[:, :, None]
        ps = masked_softmax(ss.reshape(bn, G, R, Q_BLOCK, n_sel * SEL_BLOCK),
                            ms.reshape(bn, G, 1, Q_BLOCK, n_sel * SEL_BLOCK))
        ps = ps.reshape(bn, G, R, Q_BLOCK, n_sel, SEL_BLOCK).astype(vg.dtype)
        o_s = jnp.einsum("bgrqnk,bgqnkd->bqgrd", ps, vg)
        kw = lax.dynamic_slice_in_dim(kw_pad, s0, Q_BLOCK + WINDOW, axis=1)
        vw = lax.dynamic_slice_in_dim(vw_pad, s0, Q_BLOCK + WINDOW, axis=1)
        kp = s0 - WINDOW + jnp.arange(Q_BLOCK + WINDOW)
        dist = tq[:, None] - kp[None, :]
        mw = (dist >= 0) & (dist < WINDOW) & (kp[None, :] >= 0)
        sw = jnp.einsum("bqgrd,bkgd->bgrqk", qb, kw) * scale
        pw = masked_softmax(sw, mw).astype(vw.dtype)
        o_w = jnp.einsum("bgrqk,bkgd->bqgrd", pw, vw)
        return o_s, o_w

    o_s, o_w = lax.map(query_block, jnp.arange(s // Q_BLOCK))
    o_s = o_s.transpose(1, 0, 2, 3, 4, 5).reshape(bn, s, G, R, dh)
    o_w = o_w.transpose(1, 0, 2, 3, 4, 5).reshape(bn, s, G, R, dh)

    g = jax.nn.sigmoid(gate_logits).reshape(bn, s, G, R, 3)
    o = g[..., 0, None] * o_cmp + g[..., 1, None] * o_s + g[..., 2, None] * o_w
    return o.reshape(bn, s, D_NSA)

def second_inputs(seed: int = 0) -> dict:
    key = jax.random.key(seed)
    keys = iter(jax.random.split(key, 48))
    L = DEPTH

    def nrm(shape, scale):
        return scale * jax.random.normal(next(keys), shape, jnp.float32)

    def gain(shape):
        return 1.0 + nrm(shape, 0.01)

    inp = {}
    inp["x"] = nrm((BATCH, SEQ, D_MODEL), 1.0)
    inp["ffn1_gate"] = nrm((L, D_MODEL, D_FF), D_MODEL ** -0.5)
    inp["ffn1_up"] = nrm((L, D_MODEL, D_FF), D_MODEL ** -0.5)
    inp["ffn1_down"] = nrm((L, D_FF, D_MODEL), BETA * D_FF ** -0.5)
    inp["ln1_g"] = gain((L, D_MODEL))
    inp["ln1_b"] = nrm((L, D_MODEL), 0.01)
    inp["w_in"] = nrm((L, D_MODEL, D_IN_PROJ), D_MODEL ** -0.5)
    inp["conv_w"] = nrm((L, CONV_WIDTH, D_CONV), CONV_WIDTH ** -0.5)
    inp["gmlp_ln_g"] = gain((L, D_GMLP))
    inp["gmlp_ln_b"] = nrm((L, D_GMLP), 0.01)
    inp["gmlp_w"] = nrm((L, GMLP_HEADS, GMLP_CHUNK, GMLP_CHUNK), GMLP_CHUNK ** -0.5)
    inp["gmlp_b"] = gain((L, GMLP_HEADS, GMLP_CHUNK))
    inp["ck_pe"] = nrm((L, CMP_LEN, HEAD_DIM), 0.1)
    inp["ck_w1"] = nrm((L, CMP_LEN, HEAD_DIM, CMP_HIDDEN), (CMP_LEN * HEAD_DIM) ** -0.5)
    inp["ck_b1"] = nrm((L, CMP_HIDDEN), 0.01)
    inp["ck_w2"] = nrm((L, CMP_HIDDEN, HEAD_DIM), CMP_HIDDEN ** -0.5)
    inp["cv_pe"] = nrm((L, CMP_LEN, HEAD_DIM), 0.1)
    inp["cv_w1"] = nrm((L, CMP_LEN, HEAD_DIM, CMP_HIDDEN), (CMP_LEN * HEAD_DIM) ** -0.5)
    inp["cv_b1"] = nrm((L, CMP_HIDDEN), 0.01)
    inp["cv_w2"] = nrm((L, CMP_HIDDEN, HEAD_DIM), CMP_HIDDEN ** -0.5)
    inp["w_out"] = nrm((L, D_MIX, D_MODEL), BETA * D_MIX ** -0.5)
    inp["ln2_g"] = gain((L, D_MODEL))
    inp["ln2_b"] = nrm((L, D_MODEL), 0.01)
    inp["ffn2_gate"] = nrm((L, D_MODEL, D_FF), D_MODEL ** -0.5)
    inp["ffn2_up"] = nrm((L, D_MODEL, D_FF), D_MODEL ** -0.5)
    inp["ffn2_down"] = nrm((L, D_FF, D_MODEL), BETA * D_FF ** -0.5)
    inp["ln3_g"] = gain((L, D_MODEL))
    inp["ln3_b"] = nrm((L, D_MODEL), 0.01)
    return inp

def second_block(x, ffn1_gate, ffn1_up, ffn1_down, ln1_g, ln1_b, w_in, conv_w,
              gmlp_ln_g, gmlp_ln_b, gmlp_w, gmlp_b,
              ck_pe, ck_w1, ck_b1, ck_w2, cv_pe, cv_w1, cv_b1, cv_w2,
              w_out, ln2_g, ln2_b, ffn2_gate, ffn2_up, ffn2_down, ln3_g, ln3_b):
    split_points = list(np.cumsum([D_CONV, D_CONV, D_CONV, 2 * D_GMLP, D_NSA,
                                   D_KV, D_KV, D_KV, D_KV, D_KV, D_KV]))
    split_points = [int(p) for p in split_points]
    for l in range(DEPTH):
        x = layer_norm(ALPHA * x + 0.5 * swiglu(x, ffn1_gate[l], ffn1_up[l], ffn1_down[l]),
                       ln1_g[l], ln1_b[l])
        proj = x @ w_in[l]
        (h_a, b_a, c_a, uv, q, kc, vc, ksl, vsl, kw, vw, gl) = jnp.split(proj, split_points, axis=-1)
        y_a = short_conv(h_a, b_a, c_a, conv_w[l])
        y_b = gmlp_spatial(uv, gmlp_ln_g[l], gmlp_ln_b[l], gmlp_w[l], gmlp_b[l])
        y_c = nsa_attention(q, kc, vc, ksl, vsl, kw, vw, gl,
                            ck_pe[l], ck_w1[l], ck_b1[l], ck_w2[l],
                            cv_pe[l], cv_w1[l], cv_b1[l], cv_w2[l])
        mix = jnp.concatenate([y_a, y_b, y_c], axis=-1) @ w_out[l]
        x = layer_norm(ALPHA * x + mix, ln2_g[l], ln2_b[l])
        x = layer_norm(ALPHA * x + 0.5 * swiglu(x, ffn2_gate[l], ffn2_up[l], ffn2_down[l]),
                       ln3_g[l], ln3_b[l])
    return x


_first_inputs = second_inputs


def second_inputs(seed=0):
    import zlib

    import numpy as np

    out = dict(_first_inputs(seed))
    spreads = {}
    factors = {'ln1_g': 3.685,
     'ln1_b': 3.503,
     'gmlp_ln_g': 8.0,
     'gmlp_ln_b': 8.0,
     'gmlp_b': 8.0,
     'ck_pe': 8.0,
     'ck_w1': 2.829,
     'ck_b1': 8.0,
     'ck_w2': 2.784,
     'cv_pe': 6.323,
     'cv_b1': 8.0,
     'ln2_g': 3.789,
     'ln2_b': 3.773,
     'ln3_g': 4.041,
     'ln3_b': 3.872}
    for name, (base, spread) in spreads.items():
        noise = np.random.default_rng([zlib.crc32(name.encode()), seed]).standard_normal(out[name].shape)
        drawn = base * np.exp(spread * noise) if base else spread * noise
        out[name] = __import__('jax').numpy.asarray(drawn.astype(out[name].dtype))
    for name, factor in factors.items():
        out[name] = (out[name] * factor).astype(out[name].dtype)
    return out


_narrow_inputs = second_inputs


def second_inputs(seed=0):

    out = dict(_narrow_inputs(seed))
    wider = {'gmlp_ln_g': 11.46,
     'gmlp_ln_b': 10.57,
     'gmlp_b': 7.65,
     'ck_b1': 12.0,
     'cv_pe': 4.69,
     'cv_b1': 12.0,
     'ln3_b': 3.14}
    for name, times in wider.items():
        mean = out[name].mean()
        out[name] = (mean + times * (out[name] - mean)).astype(out[name].dtype)
    return out


def setup_inputs(seed=0):
    out = dict(first_inputs(seed))
    for name, value in second_inputs(seed + 1).items():
        if name != "x":
            out[name + "_2"] = value
    return out


def reference(
    x, w_in, ret_norm_g, ca_rel_bias, da_lambda_q1, da_lambda_k1, da_lambda_q2, da_lambda_k2,
    da_norm_g, w_branch_a, w_branch_b, w_branch_c, b_merge, w_out, ln1_g, ln1_b, w_ffn_in,
    w_ffn_out, ln2_g, ln2_b, ffn1_gate_2, ffn1_up_2, ffn1_down_2, ln1_g_2, ln1_b_2, w_in_2,
    conv_w_2, gmlp_ln_g_2, gmlp_ln_b_2, gmlp_w_2, gmlp_b_2, ck_pe_2, ck_w1_2, ck_b1_2, ck_w2_2,
    cv_pe_2, cv_w1_2, cv_b1_2, cv_w2_2, w_out_2, ln2_g_2, ln2_b_2, ffn2_gate_2, ffn2_up_2,
    ffn2_down_2, ln3_g_2, ln3_b_2,
):
    x = first_block(
        x, w_in, ret_norm_g, ca_rel_bias, da_lambda_q1, da_lambda_k1, da_lambda_q2,
        da_lambda_k2, da_norm_g, w_branch_a, w_branch_b, w_branch_c, b_merge, w_out, ln1_g,
        ln1_b, w_ffn_in, w_ffn_out, ln2_g, ln2_b,
    )
    return second_block(
        x, ffn1_gate_2, ffn1_up_2, ffn1_down_2, ln1_g_2, ln1_b_2, w_in_2, conv_w_2, gmlp_ln_g_2,
        gmlp_ln_b_2, gmlp_w_2, gmlp_b_2, ck_pe_2, ck_w1_2, ck_b1_2, ck_w2_2, cv_pe_2, cv_w1_2,
        cv_b1_2, cv_w2_2, w_out_2, ln2_g_2, ln2_b_2, ffn2_gate_2, ffn2_up_2, ffn2_down_2,
        ln3_g_2, ln3_b_2,
    )


_drawn_inputs = setup_inputs


def setup_inputs(seed=0):
    import zlib

    import numpy as np

    out = dict(_drawn_inputs(seed))
    spreads = {}
    factors = {'ret_norm_g': 8.0,
     'ca_rel_bias': 8.0,
     'da_lambda_q1': 3.632,
     'da_norm_g': 8.0,
     'b_merge': 3.212,
     'ck_b1_2': 3.155}
    for name, (base, spread) in spreads.items():
        noise = np.random.default_rng([zlib.crc32(name.encode()), seed]).standard_normal(out[name].shape)
        drawn = base * np.exp(spread * noise) if base else spread * noise
        out[name] = __import__('jax').numpy.asarray(drawn.astype(out[name].dtype))
    for name, factor in factors.items():
        out[name] = (out[name] * factor).astype(out[name].dtype)
    return out
```

```python
from contextlib import ExitStack
import math

import numpy as np
import concourse.bass as bass
from concourse import mybir
from concourse.alu_op_type import AluOpType as ALU

F = mybir.dt.float32
R = mybir.dt.float32r
BF = mybir.dt.bfloat16
ACT = mybir.ActivationFunctionType
AX = mybir.AxisListType.X

DEPTH = 2
D = 1024
S = 256
FF = 2816
ALPHA = (2.0 * DEPTH) ** 0.25
EPS = 1e-5
NEG = -1e30
GC = 0.044715
GS = math.sqrt(2.0 / math.pi)

UNIT = 2048
NRAW = 3
NHL = 3

CO = {}
_at = 0
for _n, _w in (("ident", 128), ("flip", 128), ("cosR", 128), ("sinR", 256), ("cosD", 64), ("sinD", 128), ("decay", 1024),
               ("chunk", 128), ("causal", 128), ("tril", 128), ("am", 30), ("mm", 30)):
    CO[_n] = (_at, _at + _w)
    _at += _w
NCONST = _at


def constants():
    c = np.zeros((128, NCONST), np.float32)
    p = np.arange(128)

    def put(name, a):
        c[:, CO[name][0]:CO[name][1]] = a.reshape(128, -1)

    put("ident", np.eye(128))
    put("flip", np.eye(128)[:, ::-1])
    for name, d in (("R", 128), ("D", 64)):
        inv = (np.float32(10000.0) ** (-np.arange(0, d, 2, dtype=np.float32) / np.float32(d))).astype(np.float32)
        ang = (np.arange(S, dtype=np.float32)[:, None] * inv[None, :]).astype(np.float32)
        cos = np.cos(ang).astype(np.float32).reshape(2, 128, d // 2).transpose(1, 0, 2)
        sin = np.sin(ang).astype(np.float32).reshape(2, 128, d // 2).transpose(1, 0, 2)
        put("cos" + name, cos)
        put("sin" + name, np.stack([-sin, sin], axis=2))
    lg = np.log1p(-np.exp2(-5.0 - np.arange(4)))
    n = np.arange(S)
    cn, cm = n[None, :] // 64, p[:, None] // 64
    diff = n[None, :] - p[:, None]
    dec = np.zeros((128, 4, S))
    for h in range(4):
        dec[:, h] = np.where(cn >= cm, np.exp(lg[h] * np.where(cn == cm, np.abs(diff), diff)), 0.0)
    put("decay", dec * 128 ** -0.5)
    put("chunk", np.where((p[:, None] >= 64) & (p[None, :] < 64), NEG, 0.0))
    put("causal", np.where(p[:, None] > p[None, :], NEG, 0.0))
    put("tril", np.where(p[None, :] <= p[:, None], 1.0, 0.0))
    t = p[:, None, None] + 128 * np.arange(2)[None, :, None]
    ok = 16 * np.arange(15)[None, None, :] + 31 <= t
    put("am", np.where(ok, 0.0, NEG))
    put("mm", np.where(ok, 1.0, 0.0))
    return c


class Tok:

    def __init__(self, sem=None, value=0):
        self.sem, self.value, self.need = sem, value, False


def flat(ws):
    for w in ws:
        if w is None:
            continue
        if isinstance(w, Tok):
            yield w
        else:
            yield from flat(w)


class Queue:

    def __init__(self, sem):
        self.sem, self.items = sem, []

    def put(self, fn, *waits):
        tok = Tok(self.sem)
        ws = list(flat(waits))
        for w in ws:
            w.need = True
        self.items.append((fn, ws, tok, None))
        return tok

    def dma(self, fn, sem, value, *waits):
        tok = Tok(sem, value)
        ws = list(flat(waits))
        for w in ws:
            w.need = True
        self.items.append((fn, ws, tok, sem))
        return tok

    def number(self):
        n = 0
        for _, _, tok, dsem in self.items:
            if dsem is None and tok.need:
                n += 1
                tok.value = n

    def emit(self, e):
        seen = {}
        for fn, ws, tok, dsem in self.items:
            need = {}
            for w in ws:
                need[w.sem] = max(need.get(w.sem, 0), w.value)
            for s, v in need.items():
                if seen.get(s, 0) < v:
                    e.wait_ge(s, v)
                    seen[s] = v
            ins = fn(e)
            if dsem is not None:
                ins.then_inc(dsem, 16)
            elif tok.need:
                ins.then_inc(self.sem, 1)


class Buf:

    def __init__(self, ap, free=()):
        self.ap, self.ready, self._free, self.held = ap, [], list(free), False
        self.wait, self.vready = [], []

    @property
    def free(self):
        return self._free

    @free.setter
    def free(self, toks):
        self._free, self.held = toks, False

    def refill(self):
        f, self._free, self.ready = self._free, [], []
        return f


class Ring:

    def __init__(self, bufs):
        self.bufs = list(bufs)

    def take(self):
        b = next(b for b in self.bufs if not b.held)
        self.bufs.remove(b)
        self.bufs.append(b)
        b.held = True
        return b


class Program:
    def __init__(self, mem, sems, units):
        self.m = mem
        self.pe, self.act, self.dve, self.pool, self.sp = (Queue(sems[k]) for k in ("pe", "act", "dve", "pool", "sp"))
        self.sems = sems
        self.planned, self.units, self.prepped = units, [], []
        self.got = 0
        self.raw = [Buf(mem["raw"][:, i, :]) for i in range(NRAW)]
        self.rawn = [0] * NRAW
        self.hl = [Buf(mem["hl"][:, i, :, :]) for i in range(NHL)]
        self.small_at = self.small_end = 0
        self.nstage = 0
        self.dman = {}

    def small_turn(self):
        half = self.m["small"].shape[1] // 2
        self.small_end = half if self.small_end != half else 2 * half
        self.small_at = self.small_end - half

    def small(self, n):
        a = self.small_at
        self.small_at += n
        assert self.small_at <= self.small_end, self.small_at
        return self.m["small"][:, a:a + n]

    def load(self, q, name, out, src, *waits):
        n = self.dman[name] = self.dman.get(name, 0) + 1
        return q.dma(lambda e: e.dma_start(out, src), self.sems[name], 16 * n, *waits)

    def prep(self, k):
        segs, n = self.planned[k]
        r = k % NRAW
        raw, hl = self.raw[r], self.hl[k % NHL]
        waits = raw.refill()
        for view, src in segs:
            self.rawn[r] += 1
            out = view(raw.ap)
            dma = self.sp.dma(lambda e, o=out, s=src: e.dma_start(o, s), self.sems[f"raw{r}"], 16 * self.rawn[r], waits)
            waits = []
        src, hi, lo = raw.ap[:, 0:n], hl.ap[:, 0, 0:n], hl.ap[:, 1, 0:n]
        a = self.act.put(lambda e: e.activation(hi, src, ACT.Copy), dma, hl.refill())
        v = self.dve.put(lambda e: e.tensor_tensor(lo, src, hi.bitcast(F), ALU.subtract), a)
        raw.free = [v]
        hl.ready = [a, v]
        self.prepped.append(hl)

    def unit(self, segs, n):
        self.units.append((segs, n))
        if self.planned is None:
            b = Buf(self.m["hl"][:, 0, :, :])
        else:
            while len(self.prepped) < min(len(self.planned), self.got + NHL - 1):
                self.prep(len(self.prepped))
            b = self.prepped[self.got]
        self.got += 1
        return b.ap[:, 0, 0:n], b.ap[:, 1, 0:n], b


def bc(ap, axis, n):
    a = ap.unsqueeze(axis)
    shape = list(a.shape)
    shape[axis] = n
    return a.to_broadcast(shape)


def mm3(e, out, l, r, start, stop):
    e.matmul(out, l[0], r[0], start=start, stop=False)
    e.matmul(out, l[0], r[1], start=False, stop=False)
    return e.matmul(out, l[1], r[0], start=False, stop=stop)


def mix(a, b):
    a, b = iter(a), iter(b)
    for _ in a:
        next(b, None)
    for _ in b:
        pass


def script(P, I, out_ap):
    m = P.m
    pe, act, dve, pool, sp = P.pe, P.act, P.dve, P.pool, P.sp
    cst = m["const"]

    def C(name, *dims):
        a = cst[:, CO[name][0]:CO[name][1]]
        return a

    cload = P.load(sp, "const", cst[:, :], I["const"])
    identb, chunkb, causalb = m["maskb"][:, 0, :], m["maskb"][:, 1, :], m["maskb"][:, 2, :]
    ident, flip = C("ident"), C("flip")
    dve.put(lambda e: e.tensor_copy(identb, ident), cload)
    dve.put(lambda e: e.tensor_copy(chunkb, C("chunk")))
    mask_ready = dve.put(lambda e: e.tensor_copy(causalb, C("causal")))
    consts = [cload, mask_ready]

    LB = Ring([Buf(m["psum"][:, i, :]) for i in range(4)])
    AB = Ring([Buf(m["psum"][:, 4 + i, :]) for i in range(4)])
    TH = Ring([Buf(m["th"][:, i, :]) for i in range(2)])
    TM = Ring([Buf(m["tm"][:, i, :]) for i in range(3)])
    ER = Ring([Buf(m["er"][:, i, :]) for i in range(4)])
    ET = Ring([Buf(m["et"][:, i, :]) for i in range(2)])
    X = m["x"]
    XT = Buf(m["xt"])
    O1 = Buf(m["o1"])
    O2 = Buf(m["o2"])
    GB = Buf(m["gb"])
    BT = GB
    BTap = m["gb"].rearrange("p a (b c) -> p (a b) c", c=S)
    xw = [[P.load(sp, "x", X[:, :, :], I["x"][0].rearrange("(i p) d -> p i d", p=128))]] * 2

    def split(dst, sl, src, waits, scale=1.0):
        hi, lo = sl(dst[:, 0]), sl(dst[:, 1])
        a = act.put(lambda e: e.activation(hi, src, ACT.Copy, scale=scale), waits)
        if scale == 1.0:
            v = dve.put(lambda e: e.tensor_tensor(lo, src, hi.bitcast(F), ALU.subtract), a)
        else:
            v = dve.put(lambda e: e.scalar_tensor_tensor(lo, src, scale, hi.bitcast(F), ALU.mult, ALU.subtract), a)
        return [a, v]

    def transposes(ring, blocks, waits):
        b = ring.take()

        def go(e):
            for k, x in enumerate(blocks):
                i = e.transpose(b.ap[:, k * 128:(k + 1) * 128], x, ident)
            return i
        b.ready = [pe.put(go, b.refill(), waits, consts)]
        return b

    def to_T(ring, src, nk, dst, k0, waits, i):
        toks = []
        for g in range(0, nk, 4):
            n = min(4, nk - g)
            b = transposes(ring, [src[:, (g + k) * 128:(g + k + 1) * 128] for k in range(n)], waits)
            t = split(dst, lambda x, g=g, n=n: x[:, k0 + g:k0 + g + n, i * 128:(i + 1) * 128],
                      b.ap[:, 0:n * 128].rearrange("p (k t) -> p k t", k=n), b.ready)
            b.free = t
            toks += t
            last = b.ready
        return toks, last

    def wk(w, r0, kt, c0, nc):
        src = w[r0:r0 + kt * 128, c0:c0 + nc].rearrange("(k p) c -> p k c", p=128)
        return [(lambda a: a[:, 0:kt * nc].rearrange("p (k c) -> p k c", k=kt), src)], kt * nc

    def proj_N(w, c0, src, nk=8, ring=None):
        ring = ring or LB
        b = [ring.take(), ring.take()]
        fr = [x.refill() for x in b]
        per = 4
        for u in range(nk // per):
            segs, n = wk(w, u * per * 128, per, c0, 512)
            hi, lo, ub = P.unit(segs, n)
            hi, lo = (x.rearrange("p (k c) -> p k c", k=per) for x in (hi, lo))
            for i in range(2):
                def go(e, i=i, u=u, hi=hi, lo=lo):
                    for k in range(per):
                        kk = u * per + k
                        ins = mm3(e, b[i].ap, [src.ap[:, z, kk, i * 128:(i + 1) * 128] for z in (0, 1)],
                                  [hi[:, k, :], lo[:, k, :]], kk == 0, kk == nk - 1)
                    return ins
                t = pe.put(go, ub.ready, fr[i], src.ready)
                fr[i] = []
                b[i].ready = [t]
            ub.free = [t]
            src.free.append(t)
            yield
        P.res = b

    def t_unit(src, nk, view, n_el, segs, ncols, ring):
        hi, lo, ub = P.unit(segs, n_el)
        banks = []
        for c in range(0, ncols, 2):
            b = ring.take()
            fr = b.refill()

            def go(e, c=c, b=b):
                for cc in range(c, min(c + 2, ncols)):
                    for k in range(nk):
                        ins = mm3(e, b.ap[:, (cc - c) * 256:(cc - c) * 256 + 256], [view(hi, k, cc), view(lo, k, cc)],
                                  [src.ap[:, z, k, :] for z in (0, 1)], k == 0, k == nk - 1)
                return ins
            t = pe.put(go, ub.ready, fr, src.ready)
            b.ready = [t]
            banks.append(b)
        ub.free = [t]
        src.free.append(t)
        return banks

    def proj_T(w, c0, src, nk=8, cols=256, ring=None, srck=0):
        segs, n = wk(w, 0, nk, c0, cols)
        return t_unit(src, nk, lambda a, k, c: a.rearrange("p (k c) -> p k c", k=nk)[:, k, c * 128:(c + 1) * 128],
                      n, segs, cols // 128, ring or LB)

    def pow_m05(dst, src, waits, scale, n):
        a = pool.put(lambda e: e.tensor_scalar(src, src, scale, EPS, ALU.mult, ALU.add), waits)
        return pool.put(lambda e: e.tensor_tensor(dst, src, m["mhalf"][:, 0:n], ALU.pow), a, half_ready)

    half_ready = dve.put(lambda e: e.memset(m["mhalf"][:, :], -0.5))
    zpad = dve.put(lambda e: e.memset(m["zb"][:, :, 0:2], 0.0))

    def load_gb(g, b):
        w = GB.refill()
        P.load(pool, "gb", GB.ap[:, 0, :], g.partition_broadcast(128), w)
        GB.ready = [P.load(pool, "gb", GB.ap[:, 1, :], b.partition_broadcast(128))]

    def layer_norm(acc, scale, tring, final=False):
        nonlocal xw
        new, toks, outs = [], [], []
        fr = XT.refill()
        for i in range(2):
            st, mv, rs = P.small(12), P.small(2), P.small(1)
            sts = []
            for c in range(2):
                xs = X[:, i, c * 512:(c + 1) * 512]
                b = acc[i][c]
                if scale == 1.0:
                    a = dve.put(lambda e, xs=xs, b=b: e.scalar_tensor_tensor(xs, xs, ALPHA, b.ap, ALU.mult, ALU.add),
                                b.ready, xw[i])
                else:
                    a = dve.put(lambda e, xs=xs: e.tensor_scalar(xs, xs, ALPHA, None, ALU.mult), xw[i])
                    a = dve.put(lambda e, xs=xs, b=b: e.scalar_tensor_tensor(xs, b.ap, scale, xs, ALU.mult, ALU.add),
                                b.ready, a)
                b.free = [a]
                sts.append(dve.put(lambda e, xs=xs, c=c, st=st: e.bn_stats(st[:, 6 * c:6 * c + 6], xs), a))
            g = dve.put(lambda e, st=st, mv=mv: e.bn_aggr(mv, st), sts)
            p = pow_m05(rs, mv[:, 1:2], g, 1.0, 1)
            xi = X[:, i, :]
            a = dve.put(lambda e, xi=xi, mv=mv, rs=rs: e.tensor_scalar(xi, xi, mv[:, 0:1], rs, ALU.subtract, ALU.mult), p)
            a = dve.put(lambda e, xi=xi: e.tensor_tensor(xi, xi, GB.ap[:, 0, :], ALU.mult), a, GB.ready)
            a = dve.put(lambda e, xi=xi: e.tensor_tensor(xi, xi, GB.ap[:, 1, :], ALU.add), a)
            GB.free = [a]
            if final:
                o = out_ap[0, i * 128:(i + 1) * 128, :]
                outs.append(P.load(sp, f"out{i}", o, xi, a))
                new.append([a])
            else:
                t, lastpe = to_T(tring, xi, 8, XT.ap, 0, [a, fr], i)
                toks += t
                new.append([a] + lastpe)
        xw = new
        XT.ready = toks
        return outs

    toks = []
    for i in range(2):
        t, lastpe = to_T(AB, X[:, i, :], 8, XT.ap, 0, xw[i], i)
        toks += t
        xw = xw[:i] + [xw[i] + lastpe] + xw[i + 1:]
    XT.ready = toks

    def ffn(gate_up, down, scale):
        acc = [[AB.take(), AB.take()] for _ in range(2)]
        afr = [[b.refill() for b in r] for r in acc]
        o2_free = O2.refill()
        HT = [Buf(m["o2"][:, :, i, :], o2_free) for i in range(4)]

        def up(j):
            segs = gate_up(j)
            b, = t_unit(XT, 8, lambda a, k, c: a.rearrange("p (k g c) -> p k g c", k=8, g=2)[:, k, c, :],
                        UNIT, segs, 2, LB)
            h, th, tm = HT[j % 4], TH.take(), TM.take()
            ga, up_ = b.ap[:, 0:256], b.ap[:, 256:512]
            tha, tma = th.ap[:, 0:256], tm.ap[:, 0:256]
            a = act.put(lambda e: e.activation(tha, ga, ACT.Tanh, scale=0.5), b.ready, th.refill())
            v = dve.put(lambda e: e.scalar_tensor_tensor(tma, tha, 1.0, ga, ALU.add, ALU.mult), a, tm.refill())
            th.free = [v]
            v = dve.put(lambda e: e.scalar_tensor_tensor(tma, tma, 0.5, up_, ALU.mult, ALU.mult), v)
            b.free = [v]
            t = split(h.ap, lambda x: x, tma, [v, h.refill()])
            h.ready = t
            tm.free = t

        def dn(d):
            segs, n = wk(down, d * 256, 2, 0, 1024)
            hi, lo, ub = P.unit(segs, n)
            hi, lo = (x.rearrange("p (k c) -> p k c", k=2) for x in (hi, lo))
            t = None
            for k in range(2):
                h = HT[(2 * d + k) % 4]
                for i in range(2):
                    for c in range(2):
                        def go(e, i=i, c=c, k=k, h=h):
                            return mm3(e, acc[i][c].ap, [h.ap[:, z, i * 128:(i + 1) * 128] for z in (0, 1)],
                                       [hi[:, k, c * 512:(c + 1) * 512], lo[:, k, c * 512:(c + 1) * 512]],
                                       d == 0 and k == 0, d == 10 and k == 1)
                        t = pe.put(go, ub.ready, h.ready, afr[i][c])
                        afr[i][c] = []
                        acc[i][c].ready = [t]
                h.free = [t]
            ub.free = [t]

        up(0)
        up(1)
        up(2)
        for d in range(11):
            dn(d)
            for j in (2 * d + 3, 2 * d + 4):
                if j < 22:
                    up(j)
        O2.free = [h.free for h in HT]
        return acc

    def scores(q, k, js, hh, i, extra, mul=None):
        K = 128 * (i + 1)
        b = AB.take()
        fr = b.refill()

        def go(e):
            for n, j in enumerate(js):
                so = b.ap[:, n * K:(n + 1) * K]
                e.matmul(so, q.ap[64 * hh:64 * hh + 64, j, i * 128:(i + 1) * 128], k(hh, j)[:, 0:K],
                         start=True, stop=False)
                ex = extra(j, hh, i)
                for x, (c, l, r) in enumerate(ex):
                    ins = e.matmul(so[:, c:c + 128], l, r, start=False, stop=x == len(ex) - 1)
            return ins
        t = pe.put(go, fr, q.ready, k(0, 0, True), consts, P.bias)
        q.free.append(t)
        nj = len(js)
        nm = P.small(nj)
        v = dve.put(lambda e: e.tensor_reduce(nm, b.ap[:, 0:nj * K].rearrange("p (n k) -> p n k", n=nj), AX, ALU.max,
                                              negate=True), t)
        er = ER.take()
        w = [v, er.refill()]
        rs = []
        for n, j in enumerate(js):
            def ex_(e, n=n, r=None):
                return e.activation(er.ap[:, n * K:(n + 1) * K], b.ap[:, n * K:(n + 1) * K], ACT.Exp,
                                    bias=nm[:, n:n + 1], accum_out=mul[n])
            a = act.put(ex_, w)
            w = []
        b.free = [a]
        er.ready = [a]
        return er, t

    def weigh(er, heads, i, ob, v_of, odim):
        K = 128 * (i + 1)
        T = i + 1
        blocks = [er.ap[:, n * K + mt * 128:n * K + mt * 128 + 128] for n in range(len(heads)) for mt in range(T)]
        tb = transposes(AB, blocks, er.ready)
        er.free = [*tb.ready]
        et = ET.take()
        w = len(blocks) * 128
        if P.flip:
            a = act.put(lambda e: e.activation(et.ap[:, 0:w], tb.ap[:, 0:w], ACT.Copy), tb.ready, et.refill())
        else:
            a = dve.put(lambda e: e.tensor_copy(et.ap[:, 0:w], tb.ap[:, 0:w]), tb.ready, et.refill())
        P.flip = not P.flip
        tb.free = [a]

        def go(e):
            for n, (o, vs) in enumerate(heads):
                for mt in range(T):
                    x = n * T + mt
                    ins = e.matmul(ob.ap[:, o * odim:(o + 1) * odim], et.ap[:, x * 128:(x + 1) * 128], v_of(mt, vs),
                                   start=mt == 0, stop=mt == T - 1)
            return ins
        t = pe.put(go, a, ob.wait, ob.vready)
        ob.wait = []
        et.free = [t]
        ob.ready = [t]
        return t

    P.flip = True

    def rot(w, c0, nh, dh, dst, scale):
        yield from proj_N(w, c0, XT)
        b = P.res
        cos, sin = ("cosR", "sinR") if dh == 128 else ("cosD", "sinD")
        hd = dh // 2
        fr = dst.refill()
        for i in range(2):
            pv = b[i].ap.rearrange("p (h s d) -> p h s d", h=nh, s=2)
            cv = bc(bc(C(cos).rearrange("p (i d) -> p i d", i=2)[:, i, :], 1, 2), 1, nh)
            sv = C(sin).rearrange("p (i s d) -> p i s d", i=2, s=2)
            t1, t2 = TM.take(), TM.take()
            a1 = t1.ap.rearrange("p (h s d) -> p h s d", h=nh, s=2)
            a2 = t2.ap.rearrange("p (h s d) -> p h s d", h=nh, s=2)
            u1 = dve.put(lambda e, a1=a1, pv=pv, cv=cv: e.tensor_tensor(a1, pv, cv, ALU.mult), b[i].ready, t1.refill(), consts)
            w2 = t2.refill()
            for s in range(2):
                u2 = dve.put(lambda e, s=s, a2=a2, pv=pv, sv=sv, i=i: e.tensor_tensor(
                    a2[:, :, s, :], pv[:, :, 1 - s, :], bc(sv[:, i, s, :], 1, nh), ALU.mult), w2)
                w2 = []
            b[i].free = [u2]
            u = dve.put(lambda e, t1=t1, t2=t2: e.tensor_tensor(t1.ap, t1.ap, t2.ap, ALU.add), u1, u2)
            t2.free = [u]
            tb = transposes(AB, [t1.ap[:, k * 128:(k + 1) * 128] for k in range(4)], u)
            t1.free = [*tb.ready]
            a = act.put(lambda e, tb=tb, i=i: e.activation(dst.ap[:, :, i * 128:(i + 1) * 128],
                                                           tb.ap.rearrange("p (k t) -> p k t", k=4),
                                                           ACT.Copy, scale=scale), tb.ready, fr)
            tb.free = [a]
            dst.ready.append(a)
            yield

    def copy_N(w, c0, dst, sl):
        yield from proj_N(w, c0, XT)
        b = P.res
        for i in range(2):
            a = act.put(lambda e, i=i: e.activation(sl(dst.ap, i), b[i].ap, ACT.Copy), b[i].ready, dst.wait)
            dst.wait = []
            b[i].free = [a]
            dst.ready.append(a)
            yield

    def copy_T(banks, dst, t0, scale, waits=()):
        for k, b in enumerate(banks):
            a = act.put(lambda e, k=k, b=b: e.activation(dst.ap[:, t0 + 2 * k:t0 + 2 * k + 2, :],
                                                         b.ap.rearrange("p (c t) -> p c t", c=2), ACT.Copy, scale=scale),
                        b.ready, waits)
            b.free = [a]
            dst.ready.append(a)

    def staging(rows, n):
        s = Buf(m["stage"])
        w = P.stage_free
        for name_src, r0, r1 in rows:
            t = P.load(pool, "stage", m["stage"][r0:r1, :], name_src, w)
            w = []
        b = AB.take()
        tp = pe.put(lambda e: e.transpose(b.ap[:, 0:n], m["stage"][0:n, :], ident[0:n, 0:n]), t, b.refill(), consts)
        P.stage_free = [tp]
        col = P.small(n)
        a = dve.put(lambda e: e.tensor_copy(col, b.ap[:, 0:n]), tp)
        b.free = [a]
        return col, a

    P.stage_free = []
    P.bias = []
    B = {k: Buf(m[k]) for k in ("q0", "k0", "q1", "k1", "v0", "v1", "sg", "gn", "w2")}

    def first(l):
        P.small_turn()
        w_in = I["w_in"][l]
        lam_init = 0.8 - 0.6 * math.exp(-0.3 * l)
        bm, bm_t = staging([(I["b_merge"][l].rearrange("(r c) -> r c", c=128), 0, 24)], 24)
        bmh = P.small(24)
        bm_t = dve.put(lambda e, bm=bm, bmh=bmh: e.tensor_scalar(bmh, bm, 0.5, None, ALU.mult), bm_t)

        gn = B["gn"]
        w = gn.refill()
        P.load(pool, "gn", gn.ap[:, 0:256], I["ret_norm_g"][l].partition_broadcast(128), w)
        gl = P.load(pool, "gn", gn.ap[:, 256:384], I["da_norm_g"][l].partition_broadcast(128))
        a = dve.put(lambda e, gn=gn: e.tensor_scalar(gn.ap[:, 0:256], gn.ap[:, 0:256], 0.5, None, ALU.mult), gl)
        gn.ready = [a, dve.put(lambda e, gn=gn, li=lam_init: e.tensor_scalar(gn.ap[:, 256:384], gn.ap[:, 256:384],
                                                                           1.0 - li, None, ALU.mult), gl)]
        lv = TM.take()
        w = lv.refill()
        for n, nme in enumerate(("da_lambda_q1", "da_lambda_k1", "da_lambda_q2", "da_lambda_k2")):
            t = P.load(pool, "lv", lv.ap[:, n * 64:(n + 1) * 64], I[nme][l].partition_broadcast(128), w)
            w = []
        lp, le, nlam = P.small(2), P.small(2), P.small(1)
        lvv = lv.ap[:, 0:256].rearrange("p (a b d) -> p a b d", a=2, b=2)
        a = dve.put(lambda e, lvv=lvv: e.tensor_tensor(lvv[:, :, 0, :], lvv[:, :, 0, :], lvv[:, :, 1, :], ALU.mult), t)
        a = dve.put(lambda e, lvv=lvv, lp=lp: e.tensor_reduce(lp, lvv[:, :, 0, :], AX, ALU.add), a)
        lv.free = [a]
        a = act.put(lambda e, lp=lp, le=le: e.activation(le, lp, ACT.Exp), a)
        a = dve.put(lambda e, le=le, nlam=nlam: e.tensor_tensor(nlam, le[:, 1:2], le[:, 0:1], ALU.subtract), a)
        nlam_t = dve.put(lambda e, nlam=nlam, li=lam_init: e.tensor_scalar(nlam, nlam, li, None, ALU.subtract), a)

        rb = I["ca_rel_bias"]
        src = bass.AP(rb.tensor, l * 8 * 513 + 129, [[1, 128], [513, 8], [1, 256]])
        t = P.load(pool, "gb", BTap[:, :, :], src, BT.refill())
        BT.ready = [dve.put(lambda e: e.memset(BTap[0:64, :, 0:64], NEG), t)]

        V0, V1, SG = B["v0"], B["v1"], B["sg"]

        def silu_gate(c0, c):
            yield from proj_N(w_in, c0, XT)
            b = P.res
            for i in range(2):
                th, tm = TH.take(), TM.take()
                a = act.put(lambda e, i=i, th=th: e.activation(th.ap, b[i].ap, ACT.Tanh, scale=0.5), b[i].ready, th.refill())
                v = dve.put(lambda e, i=i, th=th, tm=tm: e.scalar_tensor_tensor(tm.ap, th.ap, 1.0, b[i].ap, ALU.add, ALU.mult),
                            a, tm.refill())
                th.free = [v]
                b[i].free = [v]
                v = dve.put(lambda e, i=i, tm=tm: e.tensor_tensor(
                    SG.ap[:, i, c * 512:(c + 1) * 512].rearrange("p (h d) -> p h d", h=2),
                    tm.ap.rearrange("p (h d) -> p h d", h=2), bc(gn.ap[:, 0:256], 1, 2), ALU.mult), v, gn.ready, SG.wait)
                SG.wait = []
                tm.free = [v]
                SG.ready.append(v)
                gn.free.append(v)
                yield

        def linear_a():
            yield from rot(w_in, 0, 4, 128, B["q0"], 1.0)
            yield from rot(w_in, 512, 4, 128, B["k0"], 1.0)
            V0.wait = V0.refill()
            for c in range(2):
                yield from copy_N(w_in, 1024 + 512 * c, V0, lambda a, i, c=c: a[:, i, c * 512:(c + 1) * 512])
            SG.wait = SG.refill()
            for c in range(2):
                yield from silu_gate(2048 + 512 * c, c)

        def linear_b():
            for dst, c0, sc in ((B["q1"], 3072, 0.125), (B["k1"], 3584, 1.0)):
                fr = dst.refill()
                for u in range(2):
                    copy_T(proj_T(w_in, c0 + 256 * u, XT), dst, 2 * u, sc, fr)
                    yield
            V1.wait = V1.refill()
            yield from copy_N(w_in, 4096, V1, lambda a, i: a[:, i, :])

        def linear_c():
            yield from rot(w_in, 4608, 8, 64, B["q0"], 0.125)
            yield from rot(w_in, 5120, 8, 64, B["k0"], 1.0)
            V0.wait = V0.refill()
            yield from copy_N(w_in, 5632, V0, lambda a, i: a[:, i, 0:512])

        MT = Buf(m["sg"])

        def merge(br, w_br, src, nk):
            per = 1 if nk == 8 else 2
            for u in range(4):
                gb_, = proj_T(w_in, 6144 + br * 1024 + u * 256, XT)
                th = TH.take()
                w = th.refill()
                for c in range(2):
                    col = br * 8 + u * 2 + c
                    a = act.put(lambda e, c=c, col=col, th=th, gb_=gb_: e.activation(
                        th.ap[:, c * 256:(c + 1) * 256], gb_.ap[:, c * 256:(c + 1) * 256], ACT.Tanh,
                        bias=bmh[:, col:col + 1], scale=0.5), gb_.ready, w, bm_t)
                    w = []
                gb_.free = [a]
                yield
                if nk == 8:
                    bb, = proj_T(w_br, u * 256, src)
                elif u % 2 == 0:
                    bb, nxt = proj_T(w_br, u * 256, src, nk=4, cols=512)
                else:
                    bb = nxt
                mt = MT.ap.rearrange("p a b -> p (a b)")[:, u * 512:(u + 1) * 512]
                if br == 0:
                    v = dve.put(lambda e, mt=mt, th=th, bb=bb: e.scalar_tensor_tensor(mt, th.ap, 1.0, bb.ap, ALU.add, ALU.mult),
                                bb.ready, a, MT.wait)
                    MT.ready.append(v)
                else:
                    v = dve.put(lambda e, th=th, bb=bb: e.scalar_tensor_tensor(th.ap, th.ap, 1.0, bb.ap, ALU.add, ALU.mult),
                                bb.ready, a)
                    bb.free = [v]
                    v = dve.put(lambda e, mt=mt, th=th: e.tensor_tensor(mt, mt, th.ap, ALU.add), v, MT.ready)
                    MT.ready[u] = v
                if br == 0:
                    bb.free = [v]
                th.free = [v]
                yield

        def retention():
            q, k = B["q0"], B["k0"]
            fr1 = O1.refill()
            for h in range(4):
                b = AB.take()

                def go(e, h=h, b=b):
                    e.matmul(b.ap[:, 0:256], k.ap[:, h, 0:128], q.ap[:, h, :], start=True, stop=True)
                    return e.matmul(b.ap[:, 256:384], k.ap[:, h, 128:256], q.ap[:, h, 128:256], start=True, stop=True)
                t = pe.put(go, b.refill(), q.ready, k.ready)
                q.free.append(t)
                k.free.append(t)
                er = ER.take()
                dh = C("decay")[:, h * 256:(h + 1) * 256]
                dve.put(lambda e, er=er, b=b, dh=dh: e.tensor_tensor(er.ap[:, 0:256], b.ap[:, 0:256], dh, ALU.mult), t, er.refill(), consts)
                v = dve.put(lambda e, er=er, b=b, dh=dh: e.tensor_tensor(er.ap[:, 256:384], b.ap[:, 256:384], dh[:, 0:128], ALU.mult))
                b.free = [v]
                yield
                ob = AB.take()

                def go2(e, h=h, er=er, ob=ob):
                    vs = [V0.ap[:, i, h * 256:(h + 1) * 256] for i in range(2)]
                    e.matmul(ob.ap[:, 0:256], er.ap[:, 0:128], vs[0], start=True, stop=True)
                    e.matmul(ob.ap[:, 256:512], er.ap[:, 128:256], vs[0], start=True, stop=False)
                    return e.matmul(ob.ap[:, 256:512], er.ap[:, 256:384], vs[1], start=False, stop=True)
                t = pe.put(go2, ob.refill(), v, V0.ready)
                er.free = [t]
                V0.free.append(t)
                ss, rs = P.small(2), P.small(2)
                tm = TM.take()
                w = tm.refill()
                for i in range(2):
                    a = act.put(lambda e, i=i, tm=tm, ob=ob, ss=ss: e.activation(
                        tm.ap[:, 0:256], ob.ap[:, i * 256:(i + 1) * 256], ACT.Square, accum_out=ss[:, i:i + 1]), t, w, a if i else None)
                    w = []
                p = pow_m05(rs, ss, a, 1.0 / 256, 2)
                for i in range(2):
                    v = dve.put(lambda e, i=i, tm=tm, ob=ob, rs=rs, h=h: e.scalar_tensor_tensor(
                        tm.ap[:, i * 256:(i + 1) * 256], ob.ap[:, i * 256:(i + 1) * 256], rs[:, i:i + 1],
                        SG.ap[:, i, h * 256:(h + 1) * 256], ALU.mult, ALU.mult), p, a, SG.ready)
                ob.free = [v]
                SG.free.append(v)
                yield
                tb = transposes(AB, [tm.ap[:, i * 256 + c * 128:i * 256 + (c + 1) * 128] for c in range(2) for i in range(2)], v)
                tm.free = [*tb.ready]
                tt = split(O1.ap, lambda x, h=h: x[:, 2 * h:2 * h + 2, :], tb.ap.rearrange("p (c t) -> p c t", c=2),
                           [tb.ready, fr1])
                tb.free = tt
                O1.ready += tt
                yield

        def ca_attention():
            q, kk, v = B["q1"], B["k1"], V1
            fr = O2.refill()
            P.bias = BT.ready

            def K(hh, j, rdy=False):
                return kk.ready if rdy else kk.ap[64 * hh:64 * hh + 64, j, :]

            def extra(j, hh, i):
                h = 2 * j + hh
                if i == 0:
                    return [(0, BTap[:, h, 0:128], flip)]
                return [(0, BTap[:, h, 128:256], flip), (128, BTap[:, h, 0:128], flip)]
            for i in range(2):
                rs, rc = P.small(8), P.small(8)
                ob = AB.take()
                ob.wait, ob.vready = ob.refill(), v.ready
                pend = None
                for jp in range(2):
                    for hh in range(2):
                        js = (2 * jp, 2 * jp + 1)
                        hs = [2 * j + hh for j in js]
                        er, t = scores(q, K, js, hh, i, extra, [rs[:, h:h + 1] for h in hs])
                        kk.free.append(t)
                        BT.free.append(t)
                        last = er.ready
                        yield
                        if pend:
                            weigh(pend[0], pend[1], i, ob, lambda mt, vs: v.ap[:, mt, vs * 64:(vs + 1) * 64], 64)
                            yield
                        pend = (er, [(h, h) for h in hs])
                t = weigh(pend[0], pend[1], i, ob, lambda mt, vs: v.ap[:, mt, vs * 64:(vs + 1) * 64], 64)
                v.free.append(t)
                u = dve.put(lambda e, rs=rs, rc=rc: e.reciprocal(rc, rs), last)
                tm = TM.take()
                u = dve.put(lambda e, tm=tm, ob=ob, rc=rc: e.tensor_tensor(
                    tm.ap.rearrange("p (h d) -> p h d", h=8), ob.ap.rearrange("p (h d) -> p h d", h=8),
                    bc(rc, 2, 64), ALU.mult), t, u, tm.refill())
                ob.free = [u]
                yield
                tt, lp_ = to_T(AB, tm.ap, 4, O2.ap, 0, [u, fr], i)
                tm.free = lp_
                O2.ready += tt
                yield
            P.bias = []
            load_gb(I["ln1_g"][l], I["ln1_b"][l])

        def da_attention():
            q, kk, v = B["q0"], B["k0"], V0
            fr = O3.refill()

            def K(hh, j, rdy=False):
                return kk.ready if rdy else kk.ap[64 * hh:64 * hh + 64, j, :]

            def extra(j, hh, i):
                return [(128 * i, chunkb, identb)]
            for i in range(2):
                ob = AB.take()
                ob.wait, ob.vready = ob.refill(), v.ready
                KK = 128 * (i + 1)
                pend = None
                for jp in range(2):
                    js = (2 * jp, 2 * jp + 1)
                    rs, rc = P.small(4), P.small(4)
                    e0, t = scores(q, K, js, 0, i, extra, [rs[:, n:n + 1] for n in range(2)])
                    yield
                    e1, t = scores(q, K, js, 1, i, extra, [rs[:, 2 + n:3 + n] for n in range(2)])
                    kk.free.append(t)
                    yield
                    u = dve.put(lambda e, rs=rs, rc=rc: e.reciprocal(rc, rs), e1.ready, e0.ready)
                    u = dve.put(lambda e, rc=rc: e.tensor_scalar(rc[:, 2:4], rc[:, 2:4], nlam, None, ALU.mult), u, nlam_t)
                    for n in range(2):
                        s1 = e1.ap[:, n * KK:(n + 1) * KK]
                        u1 = dve.put(lambda e, s1=s1, n=n, rc=rc: e.tensor_scalar(s1, s1, rc[:, 2 + n:3 + n], None, ALU.mult), u)
                    for n in range(2):
                        s0, s1 = (x.ap[:, n * KK:(n + 1) * KK] for x in (e0, e1))
                        u2 = dve.put(lambda e, s0=s0, s1=s1, n=n, rc=rc: e.scalar_tensor_tensor(
                            s0, s0, rc[:, n:n + 1], s1, ALU.mult, ALU.add), u1)
                    e1.free = [u2]
                    e0.ready = [u2]
                    yield
                    t = weigh(e0, [(j, j) for j in js], i, ob, lambda mt, vs: v.ap[:, mt, vs * 128:(vs + 1) * 128], 128)
                    yield
                v.free.append(t)
                ss, rs = P.small(4), P.small(4)
                tm = TM.take()
                w = tm.refill()
                for j in range(4):
                    a = act.put(lambda e, j=j, tm=tm, ob=ob, ss=ss: e.activation(
                        tm.ap[:, 0:128], ob.ap[:, j * 128:(j + 1) * 128], ACT.Square, accum_out=ss[:, j:j + 1]), t, w, a if j else None)
                    w = []
                p = pow_m05(rs, ss, a, 1.0 / 128, 4)
                tv, ov = (x.rearrange("p (h d) -> p h d", h=4) for x in (tm.ap, ob.ap))
                u = dve.put(lambda e, tv=tv, ov=ov, rs=rs: e.tensor_tensor(tv, ov, bc(rs, 2, 128), ALU.mult), p, a)
                ob.free = [u]
                u = dve.put(lambda e, tv=tv: e.tensor_tensor(tv, tv, bc(gn.ap[:, 256:384], 1, 4), ALU.mult), u, gn.ready)
                gn.free.append(u)
                yield
                tt, lp_ = to_T(AB, tm.ap, 4, O3.ap, 0, [u, fr], i)
                tm.free = lp_
                O3.ready += tt
                yield

        O3 = O1
        for _ in linear_a():
            pass
        mix(linear_b(), retention())
        MT.free = SG.free
        MT.wait = MT.refill()

        def lin2():
            yield from linear_c()
            yield from merge(0, I["w_branch_a"][l], O1, 8)
        mix(lin2(), ca_attention())
        mix(merge(1, I["w_branch_b"][l], O2, 4), da_attention())
        for _ in merge(2, I["w_branch_c"][l], O3, 4):
            pass
        fr = O1.refill()
        for u in range(4):
            mt = MT.ap.rearrange("p a b -> p (a b)")[:, u * 512:(u + 1) * 512]
            t = split(O1.ap, lambda x, u=u: x[:, 2 * u:2 * u + 2, :], mt.rearrange("p (c t) -> p c t", c=2),
                      [MT.ready[u], fr], scale=0.5)
            O1.ready += t
        SG.free = [t]
        acc = [[None, None], [None, None]]
        for c in range(2):
            for _ in proj_N(I["w_out"][l], c * 512, O1):
                pass
            for i in range(2):
                acc[i][c] = P.res[i]
        layer_norm(acc, 1.0, AB)

        load_gb(I["ln2_g"][l], I["ln2_b"][l])
        wf = I["w_ffn_in"][l].rearrange("(k p) (g f) -> p k g f", p=128, g=2)

        def gate_up(j):
            src = wf[:, :, :, j * 128:(j + 1) * 128]
            return [(lambda a, g=g: a.rearrange("p (k g c) -> p k g c", k=8, g=2)[:, :, g, :], src[:, :, g, :])
                    for g in range(2)]
        acc = ffn(gate_up, I["w_ffn_out"][l], 1.0)
        layer_norm(acc, 1.0, LB)

    for l in range(DEPTH):
        first(l)
    B["w1"] = Buf(m["w1"], B["q0"].free + B["k0"].free + B["v0"].free)
    B["wt"] = Buf(m["wt"], B["v1"].free)
    B["vs"] = Buf(m["vs"], B["v1"].free)
    B["ka"] = Buf(m["ka"], B["k1"].free)
    YC = [Buf(m["sg"][:, 1, i * 512:(i + 1) * 512], B["sg"].free) for i in range(2)]

    def swiglu(l, which):
        def gate_up(j):
            return [(lambda a, g=g: a.rearrange("p (k g c) -> p k g c", k=8, g=2)[:, :, g, :],
                     I[f"ffn{which}_{nme}_2"][l][:, j * 128:(j + 1) * 128].rearrange("(k p) f -> p k f", p=128))
                    for g, nme in enumerate(("gate", "up"))]
        return ffn(gate_up, I[f"ffn{which}_down_2"][l], 0.5)

    def second(l):
        P.small_turn()
        load_gb(I["ln1_g_2"][l], I["ln1_b_2"][l])
        cols, cols_t = staging([(I["conv_w_2"][l].rearrange("k (c p) -> (k c) p", p=128), 0, 6),
                                (I["gmlp_b_2"][l], 6, 10),
                                (I["ck_b1_2"][l:l + 1, :], 10, 11),
                                (I["cv_b1_2"][l:l + 1, :], 11, 12)], 12)
        pes = m["stage2"]
        w = P.pe_free
        for n, nme in enumerate(("ck_pe_2", "cv_pe_2")):
            for r in range(2):
                t = P.load(pool, "pes", pes[0:32, n, r * 64:(r + 1) * 64], I[nme][l], w)
                w = []
        b = AB.take()

        def go(e, b=b):
            e.transpose(b.ap[:, 0:32], pes[0:32, 0, :], ident[0:32, 0:32])
            return e.transpose(b.ap[:, 32:64], pes[0:32, 1, :], ident[0:32, 0:32])
        tp = pe.put(go, t, b.refill(), consts)
        P.pe_free = [tp]
        pet = P.small(64)
        pet_t = dve.put(lambda e, b=b, pet=pet: e.tensor_copy(pet, b.ap[:, 0:64]), tp)
        b.free = [pet_t]
        gn = B["gn"]
        w = gn.refill()
        P.load(pool, "gn", gn.ap[:, 0:256], I["gmlp_ln_g_2"][l].partition_broadcast(128), w)
        gn.ready = [P.load(pool, "gn", gn.ap[:, 256:512], I["gmlp_ln_b_2"][l].partition_broadcast(128))]
        w2 = B["w2"]
        w = w2.refill()
        P.load(pool, "w2", w2.ap[:, 0, :], I["ck_w2_2"][l], w)
        w2.ready = [P.load(pool, "w2", w2.ap[:, 1, :], I["cv_w2_2"][l])]
        w1 = B["w1"]
        w = w1.refill()
        for n, nme in enumerate(("ck_w1_2", "cv_w1_2")):
            t = P.load(pool, "w1", w1.ap[:, n, :].rearrange("p (j f) -> p j f", j=16),
                       I[nme][l].rearrange("(j l) d f -> (l d) j f", l=2), w)
            w = []
        w1.ready = [t]
        gw = TM.take()
        t = P.load(pool, "gw", gw.ap[:, :].rearrange("p (h q) -> p h q", h=4),
                   I["gmlp_w_2"][l].rearrange("h p q -> p h q"), gw.refill())
        t = dve.put(lambda e: e.tensor_tensor(gw.ap.rearrange("p (h q) -> p h q", h=4),
                                              gw.ap.rearrange("p (h q) -> p h q", h=4), bc(C("tril"), 1, 4), ALU.mult), t, consts)
        wt = B["wt"]
        tb = transposes(AB, [gw.ap[:, h * 128:(h + 1) * 128] for h in range(4)], t)
        gw.free = [*tb.ready]
        t = act.put(lambda e, tb=tb: e.activation(wt.ap, tb.ap, ACT.Copy), tb.ready, wt.refill())
        tb.free = [t]
        wt.ready = [t]

        acc = swiglu(l, 1)
        layer_norm(acc, 0.5, LB)

        w_in = I["w_in_2"][l]
        frO = O1.refill()

        kcs = P.small(15)
        vcs = m["vcs"]
        ka = B["ka"]
        comp = {}

        def compress(n, bank):
            src = bank.ap[:, 256 * n:256 * n + 256].rearrange("p (t s) -> p s t", s=16)
            w = ka.refill()
            kv = ka.ap.rearrange("p (j g n) -> p j g n", j=16, g=2)
            for g in range(2):
                for par in range(2):
                    for a_ in range(2):
                        u = dve.put(lambda e, g=g, par=par, a_=a_, n=n: e.tensor_tensor(
                            kv[64 * par:64 * par + 64, 8 * a_:8 * a_ + 8, g, :],
                            src[64 * g:64 * g + 64, par::2, a_:a_ + 15],
                            bc(pet[64 * g:64 * g + 64, 32 * n + par + 16 * a_:32 * n + 16 * a_ + 16:2], 2, 15),
                            ALU.add), w, bank.ready, pet_t)
                        w = []
            hb = AB.take()

            def go(e):
                for j in range(16):
                    ins = e.matmul(hb.ap[:, 0:30], w1.ap[:, n, j * 128:(j + 1) * 128], ka.ap[:, j * 30:(j + 1) * 30],
                                   start=j == 0, stop=j == 15)
                return ins
            t = pe.put(go, u, w1.ready, hb.refill())
            ka.free = [t]
            w1.free.append(t)
            x, y, z = P.small(30), P.small(30), P.small(30)
            v = dve.put(lambda e: e.tensor_scalar(x, hb.ap[:, 0:30], cols[:, 10 + n:11 + n], None, ALU.add), t, cols_t)
            hb.free = [v]
            v = dve.put(lambda e: e.tensor_tensor(y, x, x, ALU.mult), v)
            v = dve.put(lambda e: e.tensor_scalar(y, y, GC, 1.0, ALU.mult, ALU.add), v)
            v = dve.put(lambda e: e.tensor_tensor(y, y, x, ALU.mult), v)
            a = act.put(lambda e: e.activation(z, y, ACT.Tanh, scale=GS), v)
            v = dve.put(lambda e: e.scalar_tensor_tensor(y, z, 1.0, x, ALU.add, ALU.mult), a)
            ob = AB.take()
            if n == 0:
                def go2(e):
                    e.matmul(ob.ap[0:64, 0:15], w2.ap[:, 0, :], y[:, 0:15], start=True, stop=True)
                    return e.matmul(ob.ap[64:128, 0:15], w2.ap[:, 0, :], y[:, 15:30], start=True, stop=True)
            else:
                def go2(e):
                    e.matmul(ob.ap[0:15, 0:64], y[:, 0:15], w2.ap[:, 1, :], start=True, stop=True)
                    return e.matmul(ob.ap[0:15, 64:128], y[:, 15:30], w2.ap[:, 1, :], start=True, stop=True)
            t = pe.put(go2, v, w2.ready, ob.refill())
            w2.free.append(t)
            if n == 0:
                a = act.put(lambda e: e.activation(kcs, ob.ap[:, 0:15], ACT.Copy, scale=0.5), t)
            else:
                a = act.put(lambda e: e.activation(vcs[:, :], ob.ap[0:15, 0:128], ACT.Copy, scale=0.5), t, P.vcs_free)
            ob.free = [a]
            comp[n] = a
            return u

        KS, VS, Q = B["k1"], B["vs"], B["q1"]

        def lin_kv():
            b, = proj_T(w_in, 1792, XT)
            yield
            compress(0, b)
            yield
            b.free = [compress(1, b)]
            yield
            fr = Q.refill()
            for u in range(2):
                segs = [(lambda a, g=g, c=c: a.rearrange("p (k c g d) -> p k c g d", k=8, g=2, c=2)[:, :, c, g, :],
                         w_in[:, 1280 + g * 256 + u * 128 + c * 64:1280 + g * 256 + u * 128 + c * 64 + 64]
                         .rearrange("(k p) d -> p k d", p=128))
                        for g in range(2) for c in range(2)]
                bk = t_unit(XT, 8, lambda a, k, c: a.rearrange("p (k c) -> p k c", k=8)[:, k, c * 128:(c + 1) * 128],
                            UNIT, segs, 2, LB)
                copy_T(bk, Q, 2 * u, 0.125, fr)
                yield
            fr = KS.refill()
            segs = [(lambda a, g=g: a.rearrange("p (k g c) -> p k g c", k=8, g=2)[:, :, g, :],
                     w_in[:, 2048 + g * 256:2048 + g * 256 + 128].rearrange("(k p) c -> p k c", p=128)) for g in range(2)]
            bk = t_unit(XT, 8, lambda a, k, c: a.rearrange("p (k g c) -> p k g c", k=8, g=2)[:, k, c, :],
                        UNIT, segs, 2, LB)
            copy_T(bk, KS, 0, 1.0, fr)
            yield
            fr = VS.refill()
            segs = [(lambda a, g=g: a.rearrange("p (k g c) -> p k g c", k=8, g=2)[:, :, g, :],
                     w_in[:, 2176 + g * 256:2176 + g * 256 + 128].rearrange("(k p) c -> p k c", p=128)) for g in range(2)]
            hi, lo, ub = P.unit(segs, UNIT)
            hi, lo = (x.rearrange("p (k c) -> p k c", k=8) for x in (hi, lo))
            bk = LB.take()

            def go(e):
                for i in range(2):
                    for k in range(8):
                        ins = mm3(e, bk.ap[:, i * 256:(i + 1) * 256], [XT.ap[:, z, k, i * 128:(i + 1) * 128] for z in (0, 1)],
                                  [hi[:, k, :], lo[:, k, :]], k == 0, k == 7)
                return ins
            t = pe.put(go, ub.ready, bk.refill(), XT.ready)
            ub.free = [t]
            XT.free.append(t)
            a = act.put(lambda e: e.activation(VS.ap[:, :, 0:256], bk.ap.rearrange("p (i c) -> p i c", i=2), ACT.Copy), t, fr)
            bk.free = [a]
            VS.ready = [a]
            yield
            segs, n = wk(w_in, 0, 8, 2560, 24)
            ghi, glo, gub = P.unit(segs, n)
            ghi, glo = (x.rearrange("p (k c) -> p k c", k=8) for x in (ghi, glo))
            gbk = LB.take()

            def go(e):
                for i in range(2):
                    for k in range(8):
                        ins = mm3(e, gbk.ap[:, i * 24:(i + 1) * 24], [XT.ap[:, z, k, i * 128:(i + 1) * 128] for z in (0, 1)],
                                  [ghi[:, k, :], glo[:, k, :]], k == 0, k == 7)
                return ins
            t = pe.put(go, gub.ready, gbk.refill(), XT.ready)
            gub.free = [t]
            XT.free.append(t)
            a = act.put(lambda e: e.activation(gts, gbk.ap[:, 0:48], ACT.Tanh, scale=0.5), t)
            gbk.free = [a]
            comp["g"] = dve.put(lambda e: e.tensor_scalar(gts, gts, 0.5, 0.5, ALU.mult, ALU.add), a)
            yield

        gts = P.small(48)

        def lin_rest():
            bh, = proj_T(w_in, 0, XT)
            hs = TH.take()
            a = act.put(lambda e: e.activation(hs.ap, bh.ap, ACT.Copy), bh.ready, hs.refill())
            bh.free = [a]
            yield
            bb, = proj_T(w_in, 256, XT)
            yield
            bcg, = proj_T(w_in, 512, XT)
            z = m["zb"]
            v = dve.put(lambda e: e.tensor_tensor(z[:, :, 2:258], hs.ap.rearrange("p (c t) -> p c t", c=2),
                                                  bcg.ap.rearrange("p (c t) -> p c t", c=2), ALU.mult), a, bcg.ready)
            bcg.free = [v]
            hs.free = [v]
            yt = TM.take()
            w = yt.refill()
            for c in range(2):
                ya = yt.ap[:, c * 256:(c + 1) * 256]
                u = dve.put(lambda e, c=c, ya=ya: e.tensor_scalar(ya, z[:, c, 2:258], cols[:, 4 + c:5 + c], None, ALU.mult), v, w, cols_t)
                w = []
                for k in (1, 0):
                    u = dve.put(lambda e, c=c, ya=ya, k=k: e.scalar_tensor_tensor(
                        ya, z[:, c, k:k + 256], cols[:, 2 * k + c:2 * k + c + 1], ya, ALU.mult, ALU.add), u)
            u = dve.put(lambda e: e.tensor_tensor(yt.ap, yt.ap, bb.ap, ALU.mult), u, bb.ready)
            bb.free = [u]
            t = split(O1.ap, lambda x: x[:, 0:2, :], yt.ap.rearrange("p (c t) -> p c t", c=2), [u, frO])
            yt.free = t
            O1.ready += t
            yield
            yield from proj_N(w_in, 768, XT)
            bk = P.res
            SGb = B["sg"]
            w = SGb.refill()
            zz = SGb.ap[:, 0, :].rearrange("p (i c) -> p i c", i=2)
            for i in range(2):
                t1, th = TM.take(), TH.take()
                a = act.put(lambda e, i=i, t1=t1: e.activation(t1.ap, bk[i].ap, ACT.Square), bk[i].ready, t1.refill())
                v = dve.put(lambda e, t1=t1: e.tensor_scalar(t1.ap, t1.ap, GC, 1.0, ALU.mult, ALU.add), a)
                v = dve.put(lambda e, i=i, t1=t1: e.tensor_tensor(t1.ap, t1.ap, bk[i].ap, ALU.mult), v)
                a = act.put(lambda e, t1=t1, th=th: e.activation(th.ap, t1.ap, ACT.Tanh, scale=GS), v, th.refill())
                a = act.put(lambda e, i=i, t1=t1: e.activation(t1.ap, bk[i].ap, ACT.Copy, scale=0.5), a)
                bk[i].free = [a]
                v = dve.put(lambda e, i=i, t1=t1, th=th: e.scalar_tensor_tensor(zz[:, i, :], th.ap, 1.0, t1.ap, ALU.add, ALU.mult), a, w)
                w = []
                t1.free = [v]
                th.free = [v]
                st, mv, rs = P.small(6), P.small(2), P.small(1)
                vi = zz[:, i, 256:512]
                v = dve.put(lambda e, vi=vi, st=st: e.bn_stats(st, vi), v)
                v = dve.put(lambda e, st=st, mv=mv: e.bn_aggr(mv, st), v)
                p = pow_m05(rs, mv[:, 1:2], v, 1.0, 1)
                v = dve.put(lambda e, vi=vi, mv=mv, rs=rs: e.tensor_scalar(vi, vi, mv[:, 0:1], rs, ALU.subtract, ALU.mult), p)
                v = dve.put(lambda e, vi=vi: e.tensor_tensor(vi, vi, gn.ap[:, 0:256], ALU.mult), v, gn.ready)
                v = dve.put(lambda e, vi=vi: e.tensor_tensor(vi, vi, gn.ap[:, 256:512], ALU.add), v)
                gn.free = [v]
                yield
                sb_ = AB.take()

                def go(e, i=i, sb_=sb_):
                    for h in range(4):
                        ins = e.matmul(sb_.ap[:, h * 64:(h + 1) * 64], wt.ap[:, h * 128:(h + 1) * 128],
                                       zz[:, i, 256 + h * 64:256 + (h + 1) * 64], start=True, stop=True)
                    return ins
                t = pe.put(go, v, wt.ready, sb_.refill())
                wt.free.append(t)
                for h in range(4):
                    us = zz[:, i, h * 64:(h + 1) * 64]
                    v = dve.put(lambda e, us=us, h=h, sb_=sb_: e.scalar_tensor_tensor(
                        us, sb_.ap[:, h * 64:(h + 1) * 64], cols[:, 6 + h:7 + h], us, ALU.add, ALU.mult), t, cols_t)
                sb_.free = [v]
                yield
                tt, lp_ = to_T(AB, zz[:, i, 0:256], 2, O1.ap, 2, [v, frO], i)
                SGb.free += lp_ + [t]
                O1.ready += tt
                yield

        def nsa():
            qv = Q

            def extra(j, hh, i):
                return [(128 * i, causalb, identb)]
            for i in range(2):
                yc = YC[i]
                er = ER.take()
                ev = er.ap[:, 0:120].rearrange("p (h n) -> p h n", h=8)
                w = er.refill()
                for hh in range(2):
                    b = AB.take()

                    def go(e, hh=hh, b=b, i=i):
                        for j in range(4):
                            ins = e.matmul(b.ap[:, j * 15:(j + 1) * 15], Q.ap[64 * hh:64 * hh + 64, j, i * 128:(i + 1) * 128],
                                           kcs[64 * hh:64 * hh + 64, :], start=True, stop=True)
                        return ins
                    t = pe.put(go, b.refill(), Q.ready, comp[0])
                    Q.free.append(t)
                    v = dve.put(lambda e, hh=hh, b=b, i=i, ev=ev: e.tensor_tensor(
                        ev[:, 4 * hh:4 * hh + 4, :], b.ap[:, 0:60].rearrange("p (h n) -> p h n", h=4),
                        bc(C("am")[:, 15 * i:15 * i + 15], 1, 4), ALU.add), t, w)
                    w = []
                    b.free = [v]
                mx = P.small(8)
                rs, rc = P.small(24), P.small(24)
                v = dve.put(lambda e, mx=mx, ev=ev: e.tensor_reduce(mx, ev, AX, ALU.max), v)
                v = dve.put(lambda e, mx=mx, ev=ev: e.tensor_tensor(ev, ev, bc(mx, 2, 15), ALU.subtract), v)
                a = act.put(lambda e, er=er: e.activation(er.ap[:, 0:120], er.ap[:, 0:120], ACT.Exp), v)
                v1_ = dve.put(lambda e, rs=rs, ev=ev: e.tensor_reduce(rs[:, 0:8], ev, AX, ALU.add), a)
                v = dve.put(lambda e, ev=ev, i=i: e.tensor_tensor(ev, ev, bc(C("mm")[:, 15 * i:15 * i + 15], 1, 8), ALU.mult), a, v1_)
                yield
                etv = []
                for half in range(2):
                    tb = AB.take()

                    def go(e, half=half, tb=tb, er=er):
                        for h in range(4):
                            x = 4 * half + h
                            ins = e.transpose(tb.ap[0:15, h * 128:(h + 1) * 128], er.ap[:, x * 15:(x + 1) * 15], ident)
                        return ins
                    t = pe.put(go, v, tb.refill(), consts)
                    et = ET.take()
                    a = act.put(lambda e, et=et, tb=tb: e.activation(et.ap[0:15, :], tb.ap[0:15, :], ACT.Copy), t, et.refill())
                    tb.free = [a]
                    etv.append((et, a))
                er.free = [t]
                ob = AB.take()

                def go(e, ob=ob, etv=etv):
                    for h in range(8):
                        g = h // 4
                        ins = e.matmul(ob.ap[:, h * 64:(h + 1) * 64], etv[g][0].ap[0:15, (h % 4) * 128:(h % 4 + 1) * 128],
                                       vcs[:, g * 64:(g + 1) * 64], start=True, stop=True)
                    return ins
                t = pe.put(go, ob.refill(), etv[0][1], etv[1][1], comp[1])
                etv[0][0].free = [t]
                etv[1][0].free = [t]
                P.vcs_free = [t]
                obs = [ob]
                ob.ready = [t]
                gv = gts[:, 24 * i:24 * i + 24].rearrange("p (h b) -> p h b", b=3)

                def collect(bno, ob, waits, first, i=i, rs=rs, rc=rc, gv=gv, yc=yc):
                    r_ = rc[:, 8 * bno:8 * bno + 8]
                    u = dve.put(lambda e: e.reciprocal(r_, rs[:, 8 * bno:8 * bno + 8]), waits)
                    u = dve.put(lambda e: e.tensor_tensor(r_, r_, gv[:, :, bno], ALU.mult), u, comp["g"])
                    ov = ob.ap.rearrange("p (h d) -> p h d", h=8)
                    if first:
                        u = dve.put(lambda e: e.tensor_tensor(yc.ap.rearrange("p (h d) -> p h d", h=8), ov, bc(r_, 2, 64), ALU.mult),
                                    u, ob.ready, yc.refill())
                        ob.free = [u]
                    else:
                        tm = TM.take()
                        u = dve.put(lambda e: e.tensor_tensor(tm.ap.rearrange("p (h d) -> p h d", h=8), ov, bc(r_, 2, 64), ALU.mult),
                                    u, ob.ready, tm.refill())
                        ob.free = [u]
                        u = dve.put(lambda e: e.tensor_tensor(yc.ap, yc.ap, tm.ap, ALU.add), u, yc.ready)
                        tm.free = [u]
                    yc.ready = [u]
                collect(0, ob, [v1_], True)
                yield
                for bno in (1, 2):
                    ob = AB.take()
                    ob.wait, ob.vready = ob.refill(), VS.ready

                    def K(hh, j, rdy=False, bno=bno):
                        return KS.ready if rdy else KS.ap[64 * hh:64 * hh + 64, bno - 1, :]

                    def vof(mt, vs, bno=bno):
                        return VS.ap[:, mt, (bno - 1) * 128 + vs * 64:(bno - 1) * 128 + (vs + 1) * 64]
                    pend = None
                    for jp in range(2):
                        for hh in range(2):
                            js = (2 * jp, 2 * jp + 1)
                            hs = [hh * 4 + j for j in js]
                            er, t = scores(Q, K, js, hh, i, extra, [rs[:, 8 * bno + h:8 * bno + h + 1] for h in hs])
                            KS.free.append(t)
                            last = er.ready
                            yield
                            if pend:
                                weigh(pend[0], pend[1], i, ob, vof, 64)
                                yield
                            pend = (er, [(h, hh) for h in hs])
                    t = weigh(pend[0], pend[1], i, ob, vof, 64)
                    VS.free.append(t)
                    collect(bno, ob, last, False)
                    yield
                tt, lp_ = to_T(AB, yc.ap, 4, O1.ap, 4, [yc.ready, frO], i)
                yc.free = lp_
                O1.ready += tt
                yield

        for _ in lin_kv():
            pass
        mix(lin_rest(), nsa())
        acc = [[None, None], [None, None]]
        for c in range(2):
            for _ in proj_N(I["w_out_2"][l], c * 512, O1):
                pass
            for i in range(2):
                acc[i][c] = P.res[i]
        load_gb(I["ln2_g_2"][l], I["ln2_b_2"][l])
        layer_norm(acc, 1.0, AB)
        load_gb(I["ln3_g_2"][l], I["ln3_b_2"][l])
        acc = swiglu(l, 2)
        return layer_norm(acc, 0.5, LB, final=l == DEPTH - 1)

    for l in range(DEPTH):
        outs = second(l)
    sp.items.append((lambda e: None, outs, Tok(), None))


def build(nc, I, out_ap):
    with ExitStack() as ctx:
        def sb(name, shape, dt=F):
            return ctx.enter_context(nc.sbuf_tensor(name, shape, dt))

        m = {
            "raw": sb("raw", [128, NRAW, UNIT]), "hl": sb("hl", [128, NHL, 2, UNIT], R),
            "const": sb("cst", [128, NCONST]), "maskb": sb("maskb", [128, 3, 128], BF),
            "x": sb("xs", [128, 2, D]), "xt": sb("xt", [128, 2, 8, S], R),
            "o1": sb("o1", [128, 2, 8, S], R), "o2": sb("o2", [128, 2, 4, S], R), "gb": sb("gb", [128, 2, D]),
            "th": sb("th", [128, 2, 512]), "tm": sb("tm", [128, 3, 512]), "er": sb("er", [128, 4, 512]),
            "et": sb("et", [128, 2, 512]), "mhalf": sb("mhalf", [128, 8]), "small": sb("small", [128, 1180]),
            "stage": sb("stage", [24, 128]), "stage2": sb("stage2", [32, 2, 128]), "gn": sb("gn", [128, 512]),
            "vcs": sb("vcs", [15, 128]), "zb": sb("zb", [128, 2, 258]),
            "q1": sb("q1", [128, 4, S]), "k1": sb("k1", [128, 4, S]), "sg": sb("sg", [128, 2, 1024]),
            "w2": sb("w2", [128, 2, 64]),
            "psum": ctx.enter_context(nc.psum_tensor("ps", [128, 8, 512], F)),
        }
        m = {k: v[:] for k, v in m.items()}
        qkv, v1 = sb("qkv", [128, 4096])[:], sb("v1", [128, 1024])[:]
        m["q0"] = qkv[:, 0:1024].rearrange("p (j t) -> p j t", j=4)
        m["k0"] = qkv[:, 1024:2048].rearrange("p (j t) -> p j t", j=4)
        m["v0"] = qkv[:, 2048:4096].rearrange("p (i c) -> p i c", i=2)
        m["w1"] = qkv.rearrange("p (n c) -> p n c", n=2)
        m["v1"] = v1.rearrange("p (i c) -> p i c", i=2)
        m["vs"] = v1[:, 0:512].rearrange("p (i c) -> p i c", i=2)
        m["wt"] = v1[:, 512:1024]
        m["ka"] = m["k1"].rearrange("p j t -> p (j t)")[:, 512:992]
        sems = {k: ctx.enter_context(nc.semaphore("s_" + k)) for k in
                ["pe", "act", "dve", "pool", "sp", "const", "x", "gb", "stage", "gn", "lv", "pes", "w2", "w1", "gw",
                 "out0", "out1"] + [f"raw{i}" for i in range(NRAW)]}
        units = None
        for _ in range(2):
            P = Program(m, sems, units)
            P.pe_free, P.vcs_free = [], []
            script(P, I, out_ap)
            units = P.units
        for q in (P.pe, P.act, P.dve, P.pool, P.sp):
            q.number()
        block = ctx.enter_context(nc.Block())
        block.sync(P.sp.emit)
        block.tensor(P.pe.emit)
        block.vector(P.dve.emit)
        block.scalar(P.act.emit)
        block.gpsimd(P.pool.emit)


_INS = ["x", "w_in", "ret_norm_g", "ca_rel_bias", "da_lambda_q1", "da_lambda_k1", "da_lambda_q2", "da_lambda_k2",
        "da_norm_g", "w_branch_a", "w_branch_b", "w_branch_c", "b_merge", "w_out", "ln1_g", "ln1_b", "w_ffn_in",
        "w_ffn_out", "ln2_g", "ln2_b", "ffn1_gate_2", "ffn1_up_2", "ffn1_down_2", "ln1_g_2", "ln1_b_2", "w_in_2",
        "conv_w_2", "gmlp_ln_g_2", "gmlp_ln_b_2", "gmlp_w_2", "gmlp_b_2", "ck_pe_2", "ck_w1_2", "ck_b1_2", "ck_w2_2",
        "cv_pe_2", "cv_w1_2", "cv_b1_2", "cv_w2_2", "w_out_2", "ln2_g_2", "ln2_b_2", "ffn2_gate_2", "ffn2_up_2",
        "ffn2_down_2", "ln3_g_2", "ln3_b_2"]


def kernel(**inputs):
    import concourse.bacc as bacc
    from concourse.bass_utils import run_bass_kernel_spmd

    nc = bacc.Bacc("TRN2", target_bir_lowering=False, num_devices=1)
    arrays, aps = {}, {}
    for name in _INS:
        a = np.ascontiguousarray(inputs[name])
        arrays["in_" + name] = a
        aps[name] = nc.dram_tensor("in_" + name, a.shape, mybir.dt.from_np(a.dtype), kind="ExternalInput").ap()
    arrays["in_const"] = constants()
    aps["const"] = nc.dram_tensor("in_const", (128, NCONST), F, kind="ExternalInput").ap()
    out = nc.dram_tensor("out", (1, S, D), F, kind="ExternalOutput").ap()
    build(nc, aps, out)
    r = run_bass_kernel_spmd(nc, [arrays], core_ids=[0])
    return r.results[0]["out"]
```

```python
from contextlib import ExitStack
import math

import numpy as np
import concourse.bass as bass
from concourse import mybir
from concourse.alu_op_type import AluOpType as ALU

F = mybir.dt.float32
R = mybir.dt.float32r
BF = mybir.dt.bfloat16
ACT = mybir.ActivationFunctionType
AX = mybir.AxisListType.X

DEPTH = 2
D = 1024
S = 256
FF = 2816
ALPHA = (2.0 * DEPTH) ** 0.25
EPS = 1e-5
NEG = -1e30
GC = 0.044715
GS = math.sqrt(2.0 / math.pi)

UNIT = 2048
NRAW = 3
NHL = 3

CO = {}
_at = 0
for _n, _w in (("ident", 128), ("flip", 128), ("cosR", 128), ("sinR", 256), ("cosD", 64), ("sinD", 128), ("decay", 1024),
               ("chunk", 128), ("causal", 128), ("tril", 128), ("aident", 128), ("am", 30), ("mm", 30)):
    CO[_n] = (_at, _at + _w)
    _at += _w
NCONST = _at


def constants():
    c = np.zeros((128, NCONST), np.float32)
    p = np.arange(128)

    def put(name, a):
        c[:, CO[name][0]:CO[name][1]] = a.reshape(128, -1)

    put("ident", np.eye(128))
    put("aident", np.eye(128) * ALPHA)
    put("flip", np.eye(128)[:, ::-1])
    for name, d in (("R", 128), ("D", 64)):
        inv = (np.float32(10000.0) ** (-np.arange(0, d, 2, dtype=np.float32) / np.float32(d))).astype(np.float32)
        ang = (np.arange(S, dtype=np.float32)[:, None] * inv[None, :]).astype(np.float32)
        cos = np.cos(ang).astype(np.float32).reshape(2, 128, d // 2).transpose(1, 0, 2)
        sin = np.sin(ang).astype(np.float32).reshape(2, 128, d // 2).transpose(1, 0, 2)
        put("cos" + name, cos)
        put("sin" + name, np.stack([-sin, sin], axis=2))
    lg = np.log1p(-np.exp2(-5.0 - np.arange(4)))
    n = np.arange(S)
    cn, cm = n[None, :] // 64, p[:, None] // 64
    diff = n[None, :] - p[:, None]
    dec = np.zeros((128, 4, S))
    for h in range(4):
        dec[:, h] = np.where(cn >= cm, np.exp(lg[h] * np.where(cn == cm, np.abs(diff), diff)), 0.0)
    put("decay", dec * 128 ** -0.5)
    put("chunk", np.where((p[:, None] >= 64) & (p[None, :] < 64), NEG, 0.0))
    put("causal", np.where(p[:, None] > p[None, :], NEG, 0.0))
    put("tril", np.where(p[None, :] <= p[:, None], 1.0, 0.0))
    t = p[:, None, None] + 128 * np.arange(2)[None, :, None]
    ok = 16 * np.arange(15)[None, None, :] + 31 <= t
    put("am", np.where(ok, 0.0, NEG))
    put("mm", np.where(ok, 1.0, 0.0))
    return c


class Tok:

    def __init__(self, sem=None, value=0):
        self.sem, self.value, self.need = sem, value, False


def flat(ws):
    for w in ws:
        if w is None:
            continue
        if isinstance(w, Tok):
            yield w
        else:
            yield from flat(w)


class Queue:

    def __init__(self, sem):
        self.sem, self.items = sem, []

    def put(self, fn, *waits):
        tok = Tok(self.sem)
        ws = list(flat(waits))
        for w in ws:
            w.need = True
        self.items.append((fn, ws, tok, None))
        return tok

    def dma(self, fn, sem, value, *waits):
        tok = Tok(sem, value)
        ws = list(flat(waits))
        for w in ws:
            w.need = True
        self.items.append((fn, ws, tok, sem))
        return tok

    def number(self):
        n = 0
        for _, _, tok, dsem in self.items:
            if dsem is None and tok.need:
                n += 1
                tok.value = n

    def emit(self, e):
        seen = {}
        for fn, ws, tok, dsem in self.items:
            need = {}
            for w in ws:
                need[w.sem] = max(need.get(w.sem, 0), w.value)
            for s, v in need.items():
                if seen.get(s, 0) < v:
                    e.wait_ge(s, v)
                    seen[s] = v
            ins = fn(e)
            if dsem is not None:
                ins.then_inc(dsem, 16)
            elif tok.need:
                ins.then_inc(self.sem, 1)


class Buf:

    def __init__(self, ap, free=()):
        self.ap, self.ready, self._free, self.held = ap, [], list(free), False
        self.wait, self.vready = [], []

    @property
    def free(self):
        return self._free

    @free.setter
    def free(self, toks):
        self._free, self.held = toks, False

    def refill(self):
        f, self._free, self.ready = self._free, [], []
        return f


class Ring:

    def __init__(self, bufs):
        self.bufs = list(bufs)

    def take(self):
        b = next(b for b in self.bufs if not b.held)
        self.bufs.remove(b)
        self.bufs.append(b)
        b.held = True
        return b


class Program:
    def __init__(self, mem, sems, units):
        self.m = mem
        self.pe, self.act, self.dve, self.pool, self.sp = (Queue(sems[k]) for k in ("pe", "act", "dve", "pool", "sp"))
        self.sems = sems
        self.planned, self.units, self.prepped = units, [], []
        self.got = 0
        self.raw = [Buf(mem["raw"][:, i, :]) for i in range(NRAW)]
        self.rawn = [0] * NRAW
        self.hl = [Buf(mem["hl"][:, i, :, :]) for i in range(NHL)]
        self.small_at = self.small_end = 0
        self.nstage = 0
        self.dman = {}
        self.pending = []

    def small_turn(self):
        half = self.m["small"].shape[1] // 2
        self.small_end = half if self.small_end != half else 2 * half
        self.small_at = self.small_end - half

    def small(self, n):
        a = self.small_at
        self.small_at += n
        assert self.small_at <= self.small_end, self.small_at
        return self.m["small"][:, a:a + n]

    def load(self, q, name, out, src, *waits):
        n = self.dman[name] = self.dman.get(name, 0) + 1
        return q.dma(lambda e: e.dma_start(out, src), self.sems[name], 16 * n, *waits)

    def prep(self, k):
        segs, n = self.planned[k]
        r = k % NRAW
        raw, hl = self.raw[r], self.hl[k % NHL]
        waits = raw.refill()
        for view, src in segs:
            self.rawn[r] += 1
            out = view(raw.ap)
            dma = self.sp.dma(lambda e, o=out, s=src: e.dma_start(o, s), self.sems[f"raw{r}"], 16 * self.rawn[r], waits)
            waits = []
        src, hi, lo = raw.ap[:, 0:n], hl.ap[:, 0, 0:n], hl.ap[:, 1, 0:n]
        a = self.act.put(lambda e: e.activation(hi, src, ACT.Copy), dma, hl.refill())
        v = self.dve.put(lambda e: e.tensor_tensor(lo, src, hi.bitcast(F), ALU.subtract), a)
        raw.free = [v]
        hl.ready = [a, v]
        self.prepped.append(hl)

    def later(self, units, fn):
        self.pending.append([units, fn])

    def tick(self):
        for p in list(self.pending):
            p[0] -= 1
            if p[0] <= 0:
                self.pending.remove(p)
                p[1]()

    def flush(self):
        while self.pending:
            self.pending.pop(0)[1]()

    def unit(self, segs, n):
        self.units.append((segs, n))
        if self.planned is None:
            b = Buf(self.m["hl"][:, 0, :, :])
        else:
            while len(self.prepped) < min(len(self.planned), self.got + NHL):
                self.prep(len(self.prepped))
            b = self.prepped[self.got]
        self.got += 1
        return b.ap[:, 0, 0:n], b.ap[:, 1, 0:n], b


def bc(ap, axis, n):
    a = ap.unsqueeze(axis)
    shape = list(a.shape)
    shape[axis] = n
    return a.to_broadcast(shape)


def mm3(e, out, l, r, start, stop):
    e.matmul(out, l[0], r[0], start=start, stop=False)
    e.matmul(out, l[0], r[1], start=False, stop=False)
    return e.matmul(out, l[1], r[0], start=False, stop=stop)


def mix(a, b, ratio=1.0):
    b = iter(b)
    due = 0.0
    for _ in a:
        due += ratio
        while due >= 1.0:
            due -= 1.0
            next(b, None)
    for _ in b:
        pass


def weave(tasks, width):
    tasks = iter(tasks)
    live = []
    while True:
        while len(live) < width:
            t = next(tasks, None)
            if t is None:
                break
            live.append(t)
        if not live:
            return
        for t in list(live):
            try:
                next(t)
            except StopIteration:
                live.remove(t)
                continue
            yield


def chain(*gens):
    for g in gens:
        yield from g


def script(P, I, out_ap):
    m = P.m
    pe, act, dve, pool, sp = P.pe, P.act, P.dve, P.pool, P.sp
    cst = m["const"]

    def C(name, *dims):
        a = cst[:, CO[name][0]:CO[name][1]]
        return a

    cload = P.load(sp, "const", cst[:, :], I["const"])
    identb, chunkb, causalb = m["maskb"][:, 0, :], m["maskb"][:, 1, :], m["maskb"][:, 2, :]
    ident, flip = C("ident"), C("flip")
    dve.put(lambda e: e.tensor_copy(identb, ident), cload)
    dve.put(lambda e: e.tensor_copy(chunkb, C("chunk")))
    mask_ready = dve.put(lambda e: e.tensor_copy(causalb, C("causal")))
    ai = [m["ai"][:, z, :] for z in (0, 1)]
    a = act.put(lambda e: e.activation(ai[0], C("aident"), ACT.Copy), cload)
    ai_ready = dve.put(lambda e: e.tensor_tensor(ai[1], C("aident"), ai[0].bitcast(F), ALU.subtract), a)
    consts = [cload, mask_ready]

    LB = Ring([Buf(m["psum"][:, i, :]) for i in range(4)])
    AB = Ring([Buf(m["psum"][:, 4 + i, :]) for i in range(4)])
    TH = Ring([Buf(m["th"][:, i, :]) for i in range(2)])
    TM = Ring([Buf(m["tm"][:, i, :]) for i in range(5)])
    RT = Ring([Buf(m["rt"][:, i, :]) for i in range(2)])
    ER = Ring([Buf(m["er"][:, i, :]) for i in range(5)])
    ET = Ring([Buf(m["et"][:, i, :]) for i in range(3)])
    X = m["x"]
    XT = Buf(m["xt"])
    O1 = Buf(m["o1"])
    O2 = Buf(m["o2"])
    GB = Buf(m["gb"])
    BT = GB
    BTap = m["gb"].rearrange("p a (b c) -> p (a b) c", c=S)
    xload = P.load(sp, "x", X[:, :, :], I["x"][0].rearrange("(i p) d -> p i d", p=128))

    def split(dst, sl, src, waits, scale=1.0):
        hi, lo = sl(dst[:, 0]), sl(dst[:, 1])
        a = act.put(lambda e: e.activation(hi, src, ACT.Copy, scale=scale), waits)
        if scale == 1.0:
            v = dve.put(lambda e: e.tensor_tensor(lo, src, hi.bitcast(F), ALU.subtract), a)
        else:
            v = dve.put(lambda e: e.scalar_tensor_tensor(lo, src, scale, hi.bitcast(F), ALU.mult, ALU.subtract), a)
        return [a, v]

    def transposes(ring, blocks, waits):
        b = ring.take()

        def go(e):
            for k, x in enumerate(blocks):
                i = e.transpose(b.ap[:, k * 128:(k + 1) * 128], x, ident)
            return i
        b.ready = [pe.put(go, b.refill(), waits, consts)]
        return b

    def to_T(ring, src, nk, dst, k0, waits, i):
        toks = []
        for g in range(0, nk, 4):
            n = min(4, nk - g)
            b = transposes(ring, [src[:, (g + k) * 128:(g + k + 1) * 128] for k in range(n)], waits)
            t = split(dst, lambda x, g=g, n=n: x[:, k0 + g:k0 + g + n, i * 128:(i + 1) * 128],
                      b.ap[:, 0:n * 128].rearrange("p (k t) -> p k t", k=n), b.ready)
            b.free = t
            toks += t
            last = b.ready
        return toks, last

    def wk(w, r0, kt, c0, nc):
        src = w[r0:r0 + kt * 128, c0:c0 + nc].rearrange("(k p) c -> p k c", p=128)
        return [(lambda a: a[:, 0:kt * nc].rearrange("p (k c) -> p k c", k=kt), src)], kt * nc

    def n_unit(w, r, c0, src, b, fr, first, last, per=4):
        segs, n = wk(w, r * 128, per, c0, 512)
        hi, lo, ub = P.unit(segs, n)
        hi, lo = (x.rearrange("p (k c) -> p k c", k=per) for x in (hi, lo))
        for i in range(2):
            for ks in ([[k] for k in range(per)] if src.fresh and i == 0 else [range(per)]):
                def go(e, i=i, ks=ks):
                    for k in ks:
                        ins = mm3(e, b[i].ap, [src.ap[:, z, r + k, i * 128:(i + 1) * 128] for z in (0, 1)],
                                  [hi[:, k, :], lo[:, k, :]], first and k == 0, last and k == per - 1)
                    return ins
                rdy = [src.kt[r + k] for k in ks] if src.fresh else src.ready
                t = pe.put(go, ub.ready, fr[i], rdy)
                fr[i] = []
            b[i].ready = [t]
        ub.free = [t]
        src.free.append(t)
        if r + per >= 8:
            src.fresh = False
        P.tick()

    def proj_N(w, c0, src, nk=8):
        b = [LB.take(), LB.take()]
        fr = [x.refill() for x in b]
        for r in range(0, nk, 4):
            n_unit(w, r, c0, src, b, fr, r == 0, r + 4 == nk)
            yield
        P.res = b

    def t_unit(src, nk, view, n_el, segs, ncols, ring):
        hi, lo, ub = P.unit(segs, n_el)
        banks = []
        for c in range(0, ncols, 2):
            b = ring.take()
            fr = b.refill()
            for cc in range(c, min(c + 2, ncols)):
                for ks in ([[k] for k in range(nk)] if src.fresh and cc == 0 else [range(nk)]):
                    def go(e, cc=cc, b=b, ks=ks, c=c):
                        for k in ks:
                            ins = mm3(e, b.ap[:, (cc - c) * 256:(cc - c) * 256 + 256], [view(hi, k, cc), view(lo, k, cc)],
                                      [src.ap[:, z, k, :] for z in (0, 1)], k == 0, k == nk - 1)
                        return ins
                    rdy = [src.kt[k] for k in ks] if src.fresh else src.ready
                    t = pe.put(go, ub.ready, fr, rdy)
                    fr = []
            b.ready = [t]
            banks.append(b)
        ub.free = [t]
        src.free.append(t)
        src.fresh = False
        P.tick()
        return banks

    def proj_T(w, c0, src, nk=8, cols=256, ring=None, srck=0):
        segs, n = wk(w, 0, nk, c0, cols)
        return t_unit(src, nk, lambda a, k, c: a.rearrange("p (k c) -> p k c", k=nk)[:, k, c * 128:(c + 1) * 128],
                      n, segs, cols // 128, ring or LB)

    def pow_m05(dst, src, waits, scale, n):
        a = pool.put(lambda e: e.tensor_scalar(src, src, scale, EPS, ALU.mult, ALU.add), waits)
        return pool.put(lambda e: e.tensor_tensor(dst, src, m["mhalf"][:, 0:n], ALU.pow), a, half_ready)

    half_ready = dve.put(lambda e: e.memset(m["mhalf"][:, :], -0.5))
    zpad = dve.put(lambda e: e.memset(m["zb"][:, :, 0:2], 0.0))

    def load_gb(g, b):
        w = GB.refill()
        P.load(sp, "gb", GB.ap[:, 0, :], g.partition_broadcast(128), w)
        GB.ready = [P.load(sp, "gb", GB.ap[:, 1, :], b.partition_broadcast(128))]

    def residual(b, i, c, waits):
        def go(e):
            for k in range(4):
                ins = mm3(e, b.ap[:, k * 128:(k + 1) * 128], [XT.ap[:, z, 4 * c + k, i * 128:(i + 1) * 128] for z in (0, 1)],
                          ai, k == 0, False)
            return ins
        t = pe.put(go, waits, XT.ready, ai_ready)
        XT.free.append(t)

    def layer_norm(acc, gb, gb_t, tring, final=False):
        xn = []
        for i in range(2):
            st, mv, rs, nb = P.small(12), P.small(2), P.small(1), P.small(1)
            for c in range(2):
                b = acc[i][c]
                v = dve.put(lambda e, b=b, c=c, st=st: e.bn_stats(st[:, 6 * c:6 * c + 6], b.ap), b.ready)
            g = dve.put(lambda e, st=st, mv=mv: e.bn_aggr(mv, st), v)
            p = pow_m05(rs, mv[:, 1:2], g, 1.0, 1)
            xn.append((mv, rs, nb, p))
        waits = X_free.refill()
        done = []
        for i in range(2):
            mv, rs, nb, p = xn[i]
            v = dve.put(lambda e, mv=mv, rs=rs, nb=nb: e.scalar_tensor_tensor(nb, mv[:, 0:1], -1.0, rs, ALU.mult, ALU.mult), p)
            for c in range(2):
                b = acc[i][c]
                xs = X[:, i, c * 512:(c + 1) * 512]
                a = act.put(lambda e, b=b, xs=xs, rs=rs, nb=nb: e.activation(xs, b.ap, ACT.Identity, bias=nb, scale=rs),
                            v, waits)
                b.free = [a]
                done.append(a)
        if final:
            outs = []
            for i in range(2):
                xi = X[:, i, :]
                a = dve.put(lambda e, xi=xi: e.tensor_tensor(xi, xi, GB.ap[:, 0, :], ALU.mult), done[2 * i + 1], GB.ready)
                a = dve.put(lambda e, xi=xi: e.tensor_tensor(xi, xi, GB.ap[:, 1, :], ALU.add), a)
                outs.append(P.load(sp, f"out{i}", out_ap[0, i * 128:(i + 1) * 128, :], xi, a))
            return outs
        banks = [tring.take() for _ in range(4)]
        frs = [b.refill() for b in banks]
        fr = XT.refill()
        for i in range(2):
            for q in range(4):
                b = banks[q]

                def go(e, i=i, q=q, b=b):
                    for k in range(2):
                        ins = e.transpose(b.ap[:, k * 256 + i * 128:k * 256 + (i + 1) * 128],
                                          X[:, i, (2 * q + k) * 128:(2 * q + k + 1) * 128], ident)
                    return ins
                t = pe.put(go, frs[q], done[2 * i + q // 2], consts)
                frs[q] = []
                b.ready = [t]
        X_free.free = [t]
        XT.kt = []
        fulls = []

        def full(q):
            tm = TM.take()
            w = tm.refill()
            b = banks[q]
            for k in range(2):
                kk = 2 * q + k
                v = dve.put(lambda e, k=k, kk=kk: e.tensor_scalar(tm.ap[:, k * 256:(k + 1) * 256], b.ap[:, k * 256:(k + 1) * 256],
                                                                  gb[:, kk:kk + 1], gb[:, 8 + kk:9 + kk], ALU.mult, ALU.add),
                            b.ready, w, gb_t)
            b.free = [v]
            hi = XT.ap[:, 0, 2 * q:2 * q + 2, :]
            a = act.put(lambda e: e.activation(hi, tm.ap.rearrange("p (k t) -> p k t", k=2), ACT.Copy), v, fr)
            fulls.append((tm, a, hi))

        def low(q):
            tm, a, hi = fulls[q]
            v = dve.put(lambda e: e.tensor_tensor(XT.ap[:, 1, 2 * q:2 * q + 2, :], tm.ap.rearrange("p (k t) -> p k t", k=2),
                                                  hi.bitcast(F), ALU.subtract), a)
            tm.free = [v]
            XT.kt += [[v], [v]]
        full(0)
        for q in range(1, 4):
            full(q)
            low(q - 1)
        low(3)
        XT.ready = list(XT.kt)
        XT.fresh = True

    X_free = Buf(None)
    XT.fresh = O1.fresh = O2.fresh = False
    toks = []
    for i in range(2):
        t, lastpe = to_T(AB, X[:, i, :], 8, XT.ap, 0, xload, i)
        toks += t
        X_free.free += lastpe
    XT.ready = toks

    def out_begin():
        acc = [[LB.take(), LB.take()] for _ in range(2)]
        for i in range(2):
            for c in range(2):
                residual(acc[i][c], i, c, acc[i][c].refill())
        return acc

    def out_part(w, acc, r):
        for c in range(2):
            n_unit(w, r, c * 512, O1, [acc[0][c], acc[1][c]], [[], []], False, r == 4)

    def ffn(gate_up, down, scale):
        acc = [[AB.take(), AB.take()] for _ in range(2)]
        afr = [[b.refill() for b in r] for r in acc]
        o2_free = O2.refill()
        HT = [Buf(m["o2"][:, :, i, :], o2_free) for i in range(4)]

        def up(j):
            segs = gate_up(j)
            b, = t_unit(XT, 8, lambda a, k, c: a.rearrange("p (k g c) -> p k g c", k=8, g=2)[:, k, c, :],
                        UNIT, segs, 2, LB)
            h, th, tm = HT[j % 4], TH.take(), TM.take()
            ga, up_ = b.ap[:, 0:256], b.ap[:, 256:512]
            tha, tma = th.ap[:, 0:256], tm.ap[:, 0:256]
            a = act.put(lambda e: e.activation(tha, ga, ACT.Tanh, scale=0.5), b.ready, th.refill())
            v = dve.put(lambda e: e.scalar_tensor_tensor(tma, tha, 1.0, ga, ALU.add, ALU.mult), a, tm.refill())
            th.free = [v]
            v = dve.put(lambda e: e.scalar_tensor_tensor(tma, tma, 0.5 * scale, up_, ALU.mult, ALU.mult), v)
            b.free = [v]
            t = split(h.ap, lambda x: x, tma, [v, h.refill()])
            h.ready = t
            tm.free = t

        def dn(d):
            segs, n = wk(down, d * 256, 2, 0, 1024)
            hi, lo, ub = P.unit(segs, n)
            hi, lo = (x.rearrange("p (k c) -> p k c", k=2) for x in (hi, lo))
            hs = [HT[(2 * d + k) % 4] for k in range(2)]
            for i in range(2):
                for c in range(2):
                    def go(e, i=i, c=c):
                        for k in range(2):
                            ins = mm3(e, acc[i][c].ap, [hs[k].ap[:, z, i * 128:(i + 1) * 128] for z in (0, 1)],
                                      [hi[:, k, c * 512:(c + 1) * 512], lo[:, k, c * 512:(c + 1) * 512]],
                                      False, d == 10 and k == 1)
                        return ins
                    t = pe.put(go, ub.ready, hs[0].ready, hs[1].ready)
                    acc[i][c].ready = [t]
            for h in hs:
                h.free = [t]
            ub.free = [t]
            P.tick()

        up(0)
        for i in range(2):
            for c in range(2):
                residual(acc[i][c], i, c, afr[i][c])
        up(1)
        up(2)
        for d in range(11):
            dn(d)
            for j in (2 * d + 3, 2 * d + 4):
                if j < 22:
                    up(j)
        O2.free = [h.free for h in HT]
        return acc

    def scores(q, k, js, hh, i, extra, mul=None):
        K = 128 * (i + 1)
        b = AB.take()
        fr = b.refill()

        def go(e):
            for n, j in enumerate(js):
                so = b.ap[:, n * K:(n + 1) * K]
                e.matmul(so, q.ap[64 * hh:64 * hh + 64, j, i * 128:(i + 1) * 128], k(hh, j)[:, 0:K],
                         start=True, stop=False)
                ex = extra(j, hh, i)
                for x, (c, l, r) in enumerate(ex):
                    ins = e.matmul(so[:, c:c + 128], l, r, start=False, stop=x == len(ex) - 1)
            return ins
        t = pe.put(go, fr, q.ready, k(0, 0, True), consts, P.bias)
        q.free.append(t)
        nj = len(js)
        nm = P.small(nj)
        v = dve.put(lambda e: e.tensor_reduce(nm, b.ap[:, 0:nj * K].rearrange("p (n k) -> p n k", n=nj), AX, ALU.max,
                                              negate=True), t)
        er = ER.take()
        w = [v, er.refill()]
        rs = []
        for n, j in enumerate(js):
            def ex_(e, n=n, r=None):
                return e.activation(er.ap[:, n * K:(n + 1) * K], b.ap[:, n * K:(n + 1) * K], ACT.Exp,
                                    bias=nm[:, n:n + 1], accum_out=mul[n])
            a = act.put(ex_, w)
            w = []
        b.free = [a]
        er.ready = [a]
        return er, t

    def weigh(er, heads, i, ob, v_of, odim):
        K = 128 * (i + 1)
        T = i + 1
        blocks = [er.ap[:, n * K + mt * 128:n * K + mt * 128 + 128] for n in range(len(heads)) for mt in range(T)]
        tb = transposes(AB, blocks, er.ready)
        er.free = [*tb.ready]
        et = ET.take()
        w = len(blocks) * 128
        if P.flip:
            a = act.put(lambda e: e.activation(et.ap[:, 0:w], tb.ap[:, 0:w], ACT.Copy), tb.ready, et.refill())
        else:
            a = dve.put(lambda e: e.tensor_copy(et.ap[:, 0:w], tb.ap[:, 0:w]), tb.ready, et.refill())
        P.flip = not P.flip
        tb.free = [a]

        def go(e):
            for n, (o, vs) in enumerate(heads):
                for mt in range(T):
                    x = n * T + mt
                    ins = e.matmul(ob.ap[:, o * odim:(o + 1) * odim], et.ap[:, x * 128:(x + 1) * 128], v_of(mt, vs),
                                   start=mt == 0, stop=mt == T - 1)
            return ins
        t = pe.put(go, a, ob.wait, ob.vready)
        ob.wait = []
        et.free = [t]
        ob.ready = [t]
        return t

    P.flip = True

    def rot(w, c0, nh, dh, dst, scale):
        yield from proj_N(w, c0, XT)
        b = P.res
        cos, sin = ("cosR", "sinR") if dh == 128 else ("cosD", "sinD")
        hd = dh // 2
        fr = dst.refill()
        for i in range(2):
            pv = b[i].ap.rearrange("p (h s d) -> p h s d", h=nh, s=2)
            cv = bc(bc(C(cos).rearrange("p (i d) -> p i d", i=2)[:, i, :], 1, 2), 1, nh)
            sv = C(sin).rearrange("p (i s d) -> p i s d", i=2, s=2)
            t1, t2 = RT.take(), TM.take()
            a1 = t1.ap.rearrange("p (h s d) -> p h s d", h=nh, s=2)
            a2 = t2.ap.rearrange("p (h s d) -> p h s d", h=nh, s=2)
            u1 = dve.put(lambda e, a1=a1, pv=pv, cv=cv: e.tensor_tensor(a1, pv, cv, ALU.mult), b[i].ready, t1.refill(), consts)
            w2 = t2.refill()
            for s in range(2):
                u2 = dve.put(lambda e, s=s, a2=a2, pv=pv, sv=sv, i=i: e.tensor_tensor(
                    a2[:, :, s, :], pv[:, :, 1 - s, :], bc(sv[:, i, s, :], 1, nh), ALU.mult), w2)
                w2 = []
            b[i].free = [u2]
            u = dve.put(lambda e, t1=t1, t2=t2: e.tensor_tensor(t1.ap, t1.ap, t2.ap, ALU.add), u1, u2)
            t2.free = [u]

            def turn(i=i, t1=t1, u=u):
                tb = transposes(AB, [t1.ap[:, k * 128:(k + 1) * 128] for k in range(4)], u)
                t1.free = [*tb.ready]
                a = act.put(lambda e: e.activation(dst.ap[:, :, i * 128:(i + 1) * 128],
                                                   tb.ap.rearrange("p (k t) -> p k t", k=4), ACT.Copy, scale=scale),
                            tb.ready, fr)
                tb.free = [a]
                dst.ready.append(a)
            P.later(1 + i, turn)

    def copy_N(w, c0, dst, sl):
        yield from proj_N(w, c0, XT)
        b = P.res
        for i in range(2):
            a = act.put(lambda e, i=i: e.activation(sl(dst.ap, i), b[i].ap, ACT.Copy), b[i].ready, dst.wait)
            dst.wait = []
            b[i].free = [a]
            dst.ready.append(a)
            yield

    def copy_T(banks, dst, t0, scale, waits=()):
        for k, b in enumerate(banks):
            a = act.put(lambda e, k=k, b=b: e.activation(dst.ap[:, t0 + 2 * k:t0 + 2 * k + 2, :],
                                                         b.ap.rearrange("p (c t) -> p c t", c=2), ACT.Copy, scale=scale),
                        b.ready, waits)
            b.free = [a]
            dst.ready.append(a)

    def staging(rows, n):
        s = Buf(m["stage"])
        w = P.stage_free
        for name_src, r0, r1 in rows:
            t = P.load(sp, "stage", m["stage"][r0:r1, :], name_src, w)
            w = []
        b = AB.take()
        tp = pe.put(lambda e: e.transpose(b.ap[:, 0:n], m["stage"][0:n, :], ident[0:n, 0:n]), t, b.refill(), consts)
        P.stage_free = [tp]
        col = P.small(n)
        a = dve.put(lambda e: e.tensor_copy(col, b.ap[:, 0:n]), tp)
        b.free = [a]
        return col, a

    P.stage_free = []
    P.bias = []
    B = {k: Buf(m[k]) for k in ("q0", "k0", "q1", "k1", "v0", "v1", "sg", "gn", "w2")}

    def first(l):
        P.small_turn()
        w_in = I["w_in"][l]
        lam_init = 0.8 - 0.6 * math.exp(-0.3 * l)
        def rows(name):
            return I[name][l].rearrange("(r c) -> r c", c=128)
        bm, bm_t = staging([(rows("b_merge"), 0, 24)] +
                           [(rows(nme), 24 + 8 * n, 32 + 8 * n) for n, nme in enumerate(("ln1_g", "ln1_b", "ln2_g", "ln2_b"))], 56)
        cols_t = bm_t
        bmh = P.small(24)
        bm_t = dve.put(lambda e, bm=bm, bmh=bmh: e.tensor_scalar(bmh, bm[:, 0:24], 0.5, None, ALU.mult), bm_t)

        gn = B["gn"]
        w = gn.refill()
        P.load(sp, "gn", gn.ap[:, 0:256], I["ret_norm_g"][l].partition_broadcast(128), w)
        gl = P.load(sp, "gn", gn.ap[:, 256:384], I["da_norm_g"][l].partition_broadcast(128))
        a = dve.put(lambda e, gn=gn: e.tensor_scalar(gn.ap[:, 0:256], gn.ap[:, 0:256], 0.5, None, ALU.mult), gl)
        gn.ready = [a, dve.put(lambda e, gn=gn, li=lam_init: e.tensor_scalar(gn.ap[:, 256:384], gn.ap[:, 256:384],
                                                                           1.0 - li, None, ALU.mult), gl)]
        lv = TM.take()
        w = lv.refill()
        for n, nme in enumerate(("da_lambda_q1", "da_lambda_k1", "da_lambda_q2", "da_lambda_k2")):
            t = P.load(sp, "lv", lv.ap[:, n * 64:(n + 1) * 64], I[nme][l].partition_broadcast(128), w)
            w = []
        lp, le, nlam = P.small(2), P.small(2), P.small(1)
        lvv = lv.ap[:, 0:256].rearrange("p (a b d) -> p a b d", a=2, b=2)
        a = dve.put(lambda e, lvv=lvv: e.tensor_tensor(lvv[:, :, 0, :], lvv[:, :, 0, :], lvv[:, :, 1, :], ALU.mult), t)
        a = dve.put(lambda e, lvv=lvv, lp=lp: e.tensor_reduce(lp, lvv[:, :, 0, :], AX, ALU.add), a)
        lv.free = [a]
        a = act.put(lambda e, lp=lp, le=le: e.activation(le, lp, ACT.Exp), a)
        a = dve.put(lambda e, le=le, nlam=nlam: e.tensor_tensor(nlam, le[:, 1:2], le[:, 0:1], ALU.subtract), a)
        nlam_t = dve.put(lambda e, nlam=nlam, li=lam_init: e.tensor_scalar(nlam, nlam, li, None, ALU.subtract), a)

        rb = I["ca_rel_bias"]
        src = bass.AP(rb.tensor, l * 8 * 513 + 129, [[1, 128], [513, 8], [1, 256]])
        t = P.load(sp, "gb", BTap[:, :, :], src, BT.refill())
        BT.ready = [dve.put(lambda e: e.memset(BTap[0:64, :, 0:64], NEG), t)]

        V0, V1, SG = B["v0"], B["v1"], B["sg"]

        def silu_gate(c0, c):
            yield from proj_N(w_in, c0, XT)
            b = P.res
            for i in range(2):
                th, tm = TH.take(), TM.take()
                a = act.put(lambda e, i=i, th=th: e.activation(th.ap, b[i].ap, ACT.Tanh, scale=0.5), b[i].ready, th.refill())
                v = dve.put(lambda e, i=i, th=th, tm=tm: e.scalar_tensor_tensor(tm.ap, th.ap, 1.0, b[i].ap, ALU.add, ALU.mult),
                            a, tm.refill())
                th.free = [v]
                b[i].free = [v]
                v = dve.put(lambda e, i=i, tm=tm: e.tensor_tensor(
                    SG.ap[:, i, c * 512:(c + 1) * 512].rearrange("p (h d) -> p h d", h=2),
                    tm.ap.rearrange("p (h d) -> p h d", h=2), bc(gn.ap[:, 0:256], 1, 2), ALU.mult), v, gn.ready, SG.wait)
                SG.wait = []
                tm.free = [v]
                SG.ready.append(v)
                gn.free.append(v)
                yield

        def linear_a():
            yield from rot(w_in, 0, 4, 128, B["q0"], 1.0)
            yield from rot(w_in, 512, 4, 128, B["k0"], 1.0)
            V0.wait = V0.refill()
            for c in range(2):
                yield from copy_N(w_in, 1024 + 512 * c, V0, lambda a, i, c=c: a[:, i, c * 512:(c + 1) * 512])
            SG.wait = SG.refill()
            for c in range(2):
                yield from silu_gate(2048 + 512 * c, c)

        def linear_b():
            for dst, c0, sc in ((B["q1"], 3072, 0.125), (B["k1"], 3584, 1.0)):
                fr = dst.refill()
                for u in range(2):
                    copy_T(proj_T(w_in, c0 + 256 * u, XT), dst, 2 * u, sc, fr)
                    yield
            V1.wait = V1.refill()
            yield from copy_N(w_in, 4096, V1, lambda a, i: a[:, i, :])

        def linear_c():
            yield from rot(w_in, 4608, 8, 64, B["q0"], 0.125)
            yield from rot(w_in, 5120, 8, 64, B["k0"], 1.0)
            V0.wait = V0.refill()
            yield from copy_N(w_in, 5632, V0, lambda a, i: a[:, i, 0:512])

        MT = Buf(m["sg"])

        def merge(br, w_br, src, nk):
            per = 1 if nk == 8 else 2
            for u in range(4):
                gb_, = proj_T(w_in, 6144 + br * 1024 + u * 256, XT)
                th = TH.take()
                w = th.refill()
                for c in range(2):
                    col = br * 8 + u * 2 + c
                    a = act.put(lambda e, c=c, col=col, th=th, gb_=gb_: e.activation(
                        th.ap[:, c * 256:(c + 1) * 256], gb_.ap[:, c * 256:(c + 1) * 256], ACT.Tanh,
                        bias=bmh[:, col:col + 1], scale=0.5), gb_.ready, w, bm_t)
                    w = []
                gb_.free = [a]
                yield
                if nk == 8:
                    bb, = proj_T(w_br, u * 256, src)
                elif u % 2 == 0:
                    bb, nxt = proj_T(w_br, u * 256, src, nk=4, cols=512)
                else:
                    bb = nxt
                mt = MT.ap.rearrange("p a b -> p (a b)")[:, u * 512:(u + 1) * 512]
                if br == 0:
                    v = dve.put(lambda e, mt=mt, th=th, bb=bb: e.scalar_tensor_tensor(mt, th.ap, 1.0, bb.ap, ALU.add, ALU.mult),
                                bb.ready, a, MT.wait)
                    MT.ready.append(v)
                else:
                    v = dve.put(lambda e, th=th, bb=bb: e.scalar_tensor_tensor(th.ap, th.ap, 1.0, bb.ap, ALU.add, ALU.mult),
                                bb.ready, a)
                    bb.free = [v]
                    v = dve.put(lambda e, mt=mt, th=th: e.tensor_tensor(mt, mt, th.ap, ALU.add), v, MT.ready)
                    MT.ready[u] = v
                if br == 0:
                    bb.free = [v]
                th.free = [v]
                yield

        def retention():
            q, k = B["q0"], B["k0"]
            fr1 = O1.refill()

            def head(h):
                b = AB.take()

                def go(e, h=h, b=b):
                    e.matmul(b.ap[:, 0:256], k.ap[:, h, 0:128], q.ap[:, h, :], start=True, stop=True)
                    return e.matmul(b.ap[:, 256:384], k.ap[:, h, 128:256], q.ap[:, h, 128:256], start=True, stop=True)
                t = pe.put(go, b.refill(), q.ready, k.ready)
                q.free.append(t)
                k.free.append(t)
                er = ER.take()
                dh = C("decay")[:, h * 256:(h + 1) * 256]
                dve.put(lambda e, er=er, b=b, dh=dh: e.tensor_tensor(er.ap[:, 0:256], b.ap[:, 0:256], dh, ALU.mult), t, er.refill(), consts)
                v = dve.put(lambda e, er=er, b=b, dh=dh: e.tensor_tensor(er.ap[:, 256:384], b.ap[:, 256:384], dh[:, 0:128], ALU.mult))
                b.free = [v]
                yield
                ob = AB.take()

                def go2(e, h=h, er=er, ob=ob):
                    vs = [V0.ap[:, i, h * 256:(h + 1) * 256] for i in range(2)]
                    e.matmul(ob.ap[:, 0:256], er.ap[:, 0:128], vs[0], start=True, stop=True)
                    e.matmul(ob.ap[:, 256:512], er.ap[:, 128:256], vs[0], start=True, stop=False)
                    return e.matmul(ob.ap[:, 256:512], er.ap[:, 256:384], vs[1], start=False, stop=True)
                t = pe.put(go2, ob.refill(), v, V0.ready)
                er.free = [t]
                V0.free.append(t)
                ss, rs = P.small(2), P.small(2)
                tm = TM.take()
                w = tm.refill()
                for i in range(2):
                    a = act.put(lambda e, i=i, tm=tm, ob=ob, ss=ss: e.activation(
                        tm.ap[:, 0:256], ob.ap[:, i * 256:(i + 1) * 256], ACT.Square, accum_out=ss[:, i:i + 1]), t, w, a if i else None)
                    w = []
                p = pow_m05(rs, ss, a, 1.0 / 256, 2)
                for i in range(2):
                    v = dve.put(lambda e, i=i, tm=tm, ob=ob, rs=rs, h=h: e.scalar_tensor_tensor(
                        tm.ap[:, i * 256:(i + 1) * 256], ob.ap[:, i * 256:(i + 1) * 256], rs[:, i:i + 1],
                        SG.ap[:, i, h * 256:(h + 1) * 256], ALU.mult, ALU.mult), p, a, SG.ready)
                ob.free = [v]
                SG.free.append(v)
                yield
                tb = transposes(AB, [tm.ap[:, i * 256 + c * 128:i * 256 + (c + 1) * 128] for c in range(2) for i in range(2)], v)
                tm.free = [*tb.ready]
                tt = split(O1.ap, lambda x, h=h: x[:, 2 * h:2 * h + 2, :], tb.ap.rearrange("p (c t) -> p c t", c=2),
                           [tb.ready, fr1])
                tb.free = tt
                O1.ready += tt
                yield
            return weave([head(h) for h in range(4)], 2)

        def ca_attention():
            q, kk, v = B["q1"], B["k1"], V1
            fr = O2.refill()

            def K(hh, j, rdy=False):
                return kk.ready if rdy else kk.ap[64 * hh:64 * hh + 64, j, :]

            def extra(j, hh, i):
                h = 2 * j + hh
                if i == 0:
                    return [(0, BTap[:, h, 0:128], flip)]
                return [(0, BTap[:, h, 128:256], flip), (128, BTap[:, h, 0:128], flip)]
            vof = lambda mt, vs: v.ap[:, mt, vs * 64:(vs + 1) * 64]

            def tile(i):
                rs, rc = P.small(8), P.small(8)
                ob = AB.take()
                ob.wait, ob.vready = ob.refill(), v.ready
                ends = []

                def heads(jp, hh):
                    js = (2 * jp, 2 * jp + 1)
                    hs = [2 * j + hh for j in js]
                    er, t = scores(q, K, js, hh, i, extra, [rs[:, h:h + 1] for h in hs])
                    kk.free.append(t)
                    BT.free.append(t)
                    ends.append(er.ready)
                    yield
                    yield
                    v.free.append(weigh(er, [(h, h) for h in hs], i, ob, vof, 64))
                    yield
                yield from weave([heads(jp, hh) for jp in range(2) for hh in range(2)], 2)
                u = dve.put(lambda e: e.reciprocal(rc, rs), ends)
                tm = TM.take()
                u = dve.put(lambda e: e.tensor_tensor(
                    tm.ap.rearrange("p (h d) -> p h d", h=8), ob.ap.rearrange("p (h d) -> p h d", h=8),
                    bc(rc, 2, 64), ALU.mult), ob.ready, u, tm.refill())
                ob.free = [u]
                yield
                tt, lp_ = to_T(AB, tm.ap, 4, O2.ap, 0, [u, fr], i)
                tm.free = lp_
                O2.ready += tt
                yield
            return chain(tile(0), tile(1))

        def da_attention():
            q, kk, v = B["q0"], B["k0"], V0
            fr = O3.refill()

            def K(hh, j, rdy=False):
                return kk.ready if rdy else kk.ap[64 * hh:64 * hh + 64, j, :]

            def extra(j, hh, i):
                return [(128 * i, chunkb, identb)]
            vof = lambda mt, vs: v.ap[:, mt, vs * 128:(vs + 1) * 128]

            def tile(i):
                ob = AB.take()
                ob.wait, ob.vready = ob.refill(), v.ready
                KK = 128 * (i + 1)

                def heads(jp):
                    js = (2 * jp, 2 * jp + 1)
                    rs, rc = P.small(4), P.small(4)
                    e0, t = scores(q, K, js, 0, i, extra, [rs[:, n:n + 1] for n in range(2)])
                    yield
                    e1, t = scores(q, K, js, 1, i, extra, [rs[:, 2 + n:3 + n] for n in range(2)])
                    kk.free.append(t)
                    yield
                    u = dve.put(lambda e: e.reciprocal(rc, rs), e1.ready, e0.ready)
                    u = dve.put(lambda e: e.tensor_scalar(rc[:, 2:4], rc[:, 2:4], nlam, None, ALU.mult), u, nlam_t)
                    for n in range(2):
                        s1 = e1.ap[:, n * KK:(n + 1) * KK]
                        u1 = dve.put(lambda e, s1=s1, n=n: e.tensor_scalar(s1, s1, rc[:, 2 + n:3 + n], None, ALU.mult), u)
                    for n in range(2):
                        s0, s1 = (x.ap[:, n * KK:(n + 1) * KK] for x in (e0, e1))
                        u2 = dve.put(lambda e, s0=s0, s1=s1, n=n: e.scalar_tensor_tensor(
                            s0, s0, rc[:, n:n + 1], s1, ALU.mult, ALU.add), u1)
                    e1.free = [u2]
                    e0.ready = [u2]
                    yield
                    v.free.append(weigh(e0, [(j, j) for j in js], i, ob, vof, 128))
                    yield
                yield from weave([heads(0), heads(1)], 2)
                ss, rs = P.small(4), P.small(4)
                tm = TM.take()
                w = tm.refill()
                for j in range(4):
                    a = act.put(lambda e, j=j: e.activation(
                        tm.ap[:, 0:128], ob.ap[:, j * 128:(j + 1) * 128], ACT.Square, accum_out=ss[:, j:j + 1]), ob.ready, w,
                        a if j else None)
                    w = []
                p = pow_m05(rs, ss, a, 1.0 / 128, 4)
                tv, ov = (x.rearrange("p (h d) -> p h d", h=4) for x in (tm.ap, ob.ap))
                u = dve.put(lambda e: e.tensor_tensor(tv, ov, bc(rs, 2, 128), ALU.mult), p, a)
                ob.free = [u]
                u = dve.put(lambda e: e.tensor_tensor(tv, tv, bc(gn.ap[:, 256:384], 1, 4), ALU.mult), u, gn.ready)
                gn.free.append(u)
                yield
                tt, lp_ = to_T(AB, tm.ap, 4, O3.ap, 0, [u, fr], i)
                tm.free = lp_
                O3.ready += tt
                yield
            return chain(tile(0), tile(1))

        O3 = O1
        for _ in linear_a():
            pass
        P.flush()
        mix(linear_b(), retention(), 2)
        MT.free = SG.free
        MT.wait = MT.refill()
        P.bias = BT.ready
        mix(chain(linear_c(), merge(0, I["w_branch_a"][l], O1, 8)), ca_attention(), 1.2)
        P.bias = []
        P.flush()
        mix(merge(1, I["w_branch_b"][l], O2, 4), da_attention(), 2)
        for _ in merge(2, I["w_branch_c"][l], O3, 4):
            pass
        fr = O1.refill()
        for u in range(4):
            mt = MT.ap.rearrange("p a b -> p (a b)")[:, u * 512:(u + 1) * 512]
            t = split(O1.ap, lambda x, u=u: x[:, 2 * u:2 * u + 2, :], mt.rearrange("p (c t) -> p c t", c=2),
                      [MT.ready[u], fr], scale=0.5)
            O1.ready += t
        SG.free = [t]
        acc = out_begin()
        out_part(I["w_out"][l], acc, 0)
        out_part(I["w_out"][l], acc, 4)
        layer_norm(acc, bm[:, 24:40], cols_t, AB)

        wf = I["w_ffn_in"][l].rearrange("(k p) (g f) -> p k g f", p=128, g=2)

        def gate_up(j):
            src = wf[:, :, :, j * 128:(j + 1) * 128]
            return [(lambda a, g=g: a.rearrange("p (k g c) -> p k g c", k=8, g=2)[:, :, g, :], src[:, :, g, :])
                    for g in range(2)]
        acc = ffn(gate_up, I["w_ffn_out"][l], 1.0)
        layer_norm(acc, bm[:, 40:56], cols_t, LB)

    for l in range(DEPTH):
        first(l)
    B["w1"] = Buf(m["w1"], B["q0"].free + B["k0"].free + B["v0"].free)
    B["wt"] = Buf(m["wt"], B["v1"].free)
    B["vs"] = Buf(m["vs"], B["v1"].free)
    B["ka"] = Buf(m["ka"], B["k1"].free)
    YC = [Buf(m["sg"][:, 1, i * 512:(i + 1) * 512], B["sg"].free) for i in range(2)]

    def swiglu(l, which):
        def gate_up(j):
            return [(lambda a, g=g: a.rearrange("p (k g c) -> p k g c", k=8, g=2)[:, :, g, :],
                     I[f"ffn{which}_{nme}_2"][l][:, j * 128:(j + 1) * 128].rearrange("(k p) f -> p k f", p=128))
                    for g, nme in enumerate(("gate", "up"))]
        return ffn(gate_up, I[f"ffn{which}_down_2"][l], 0.5)

    def second(l):
        P.small_turn()
        def rows(name):
            return I[name][l].rearrange("(r c) -> r c", c=128)
        lns = ("ln1_g_2", "ln1_b_2", "ln2_g_2", "ln2_b_2", "ln3_g_2", "ln3_b_2")
        cols, cols_t = staging([(rows(nme), 12 + 8 * n, 20 + 8 * n) for n, nme in enumerate(lns)] + [(I["conv_w_2"][l].rearrange("k (c p) -> (k c) p", p=128), 0, 6),
                                (I["gmlp_b_2"][l], 6, 10),
                                (I["ck_b1_2"][l:l + 1, :], 10, 11),
                                (I["cv_b1_2"][l:l + 1, :], 11, 12)], 60)
        pes = m["stage2"]
        w = P.pe_free
        for n, nme in enumerate(("ck_pe_2", "cv_pe_2")):
            for r in range(2):
                t = P.load(sp, "pes", pes[0:32, n, r * 64:(r + 1) * 64], I[nme][l], w)
                w = []
        b = AB.take()

        def go(e, b=b):
            e.transpose(b.ap[:, 0:32], pes[0:32, 0, :], ident[0:32, 0:32])
            return e.transpose(b.ap[:, 32:64], pes[0:32, 1, :], ident[0:32, 0:32])
        tp = pe.put(go, t, b.refill(), consts)
        P.pe_free = [tp]
        pet = P.small(64)
        pet_t = dve.put(lambda e, b=b, pet=pet: e.tensor_copy(pet, b.ap[:, 0:64]), tp)
        b.free = [pet_t]
        gn = B["gn"]
        w = gn.refill()
        P.load(sp, "gn", gn.ap[:, 0:256], I["gmlp_ln_g_2"][l].partition_broadcast(128), w)
        gn.ready = [P.load(sp, "gn", gn.ap[:, 256:512], I["gmlp_ln_b_2"][l].partition_broadcast(128))]
        w2 = B["w2"]
        w = w2.refill()
        P.load(sp, "w2", w2.ap[:, 0, :], I["ck_w2_2"][l], w)
        w2.ready = [P.load(sp, "w2", w2.ap[:, 1, :], I["cv_w2_2"][l])]
        w1 = B["w1"]
        w = w1.refill()
        for n, nme in enumerate(("ck_w1_2", "cv_w1_2")):
            t = P.load(sp, "w1", w1.ap[:, n, :].rearrange("p (j f) -> p j f", j=16),
                       I[nme][l].rearrange("(j l) d f -> (l d) j f", l=2), w)
            w = []
        w1.ready = [t]
        gw = TM.take()
        t = P.load(sp, "gw", gw.ap[:, :].rearrange("p (h q) -> p h q", h=4),
                   I["gmlp_w_2"][l].rearrange("h p q -> p h q"), gw.refill())
        t = dve.put(lambda e: e.tensor_tensor(gw.ap.rearrange("p (h q) -> p h q", h=4),
                                              gw.ap.rearrange("p (h q) -> p h q", h=4), bc(C("tril"), 1, 4), ALU.mult), t, consts)
        wt = B["wt"]
        tb = transposes(AB, [gw.ap[:, h * 128:(h + 1) * 128] for h in range(4)], t)
        gw.free = [*tb.ready]
        t = act.put(lambda e, tb=tb: e.activation(wt.ap, tb.ap, ACT.Copy), tb.ready, wt.refill())
        tb.free = [t]
        wt.ready = [t]

        acc = swiglu(l, 1)
        layer_norm(acc, cols[:, 12:28], cols_t, LB)

        w_in = I["w_in_2"][l]
        frO = O1.refill()

        kcs = P.small(15)
        vcs = m["vcs"]
        ka = B["ka"]
        comp = {}

        def compress(n, bank):
            src = bank.ap[:, 256 * n:256 * n + 256].rearrange("p (t s) -> p s t", s=16)
            w = ka.refill()
            kv = ka.ap.rearrange("p (j g n) -> p j g n", j=16, g=2)
            for g in range(2):
                for par in range(2):
                    for a_ in range(2):
                        u = dve.put(lambda e, g=g, par=par, a_=a_, n=n: e.tensor_tensor(
                            kv[64 * par:64 * par + 64, 8 * a_:8 * a_ + 8, g, :],
                            src[64 * g:64 * g + 64, par::2, a_:a_ + 15],
                            bc(pet[64 * g:64 * g + 64, 32 * n + par + 16 * a_:32 * n + 16 * a_ + 16:2], 2, 15),
                            ALU.add), w, bank.ready, pet_t)
                        w = []
            hb = AB.take()

            def go(e):
                for j in range(16):
                    ins = e.matmul(hb.ap[:, 0:30], w1.ap[:, n, j * 128:(j + 1) * 128], ka.ap[:, j * 30:(j + 1) * 30],
                                   start=j == 0, stop=j == 15)
                return ins
            t = pe.put(go, u, w1.ready, hb.refill())
            ka.free = [t]
            w1.free.append(t)
            x, y, z = P.small(30), P.small(30), P.small(30)
            v = dve.put(lambda e: e.tensor_scalar(x, hb.ap[:, 0:30], cols[:, 10 + n:11 + n], None, ALU.add), t, cols_t)
            hb.free = [v]
            v = dve.put(lambda e: e.tensor_tensor(y, x, x, ALU.mult), v)
            v = dve.put(lambda e: e.tensor_scalar(y, y, GC, 1.0, ALU.mult, ALU.add), v)
            v = dve.put(lambda e: e.tensor_tensor(y, y, x, ALU.mult), v)
            a = act.put(lambda e: e.activation(z, y, ACT.Tanh, scale=GS), v)
            v = dve.put(lambda e: e.scalar_tensor_tensor(y, z, 1.0, x, ALU.add, ALU.mult), a)
            ob = AB.take()
            if n == 0:
                def go2(e):
                    e.matmul(ob.ap[0:64, 0:15], w2.ap[:, 0, :], y[:, 0:15], start=True, stop=True)
                    return e.matmul(ob.ap[64:128, 0:15], w2.ap[:, 0, :], y[:, 15:30], start=True, stop=True)
            else:
                def go2(e):
                    e.matmul(ob.ap[0:15, 0:64], y[:, 0:15], w2.ap[:, 1, :], start=True, stop=True)
                    return e.matmul(ob.ap[0:15, 64:128], y[:, 15:30], w2.ap[:, 1, :], start=True, stop=True)
            t = pe.put(go2, v, w2.ready, ob.refill())
            w2.free.append(t)
            if n == 0:
                a = act.put(lambda e: e.activation(kcs, ob.ap[:, 0:15], ACT.Copy, scale=0.5), t)
            else:
                a = act.put(lambda e: e.activation(vcs[:, :], ob.ap[0:15, 0:128], ACT.Copy, scale=0.5), t, P.vcs_free)
            ob.free = [a]
            comp[n] = a
            return u

        KS, VS, Q = B["k1"], B["vs"], B["q1"]

        def lin_cmp():
            b, = proj_T(w_in, 1792, XT)
            yield
            compress(0, b)
            b.free = [compress(1, b)]
            yield
            segs, n = wk(w_in, 0, 8, 2560, 24)
            ghi, glo, gub = P.unit(segs, n)
            ghi, glo = (x.rearrange("p (k c) -> p k c", k=8) for x in (ghi, glo))
            gbk = LB.take()

            def go(e):
                for i in range(2):
                    for k in range(8):
                        ins = mm3(e, gbk.ap[:, i * 24:(i + 1) * 24], [XT.ap[:, z, k, i * 128:(i + 1) * 128] for z in (0, 1)],
                                  [ghi[:, k, :], glo[:, k, :]], k == 0, k == 7)
                return ins
            t = pe.put(go, gub.ready, gbk.refill(), XT.ready)
            gub.free = [t]
            XT.free.append(t)
            a = act.put(lambda e: e.activation(gts, gbk.ap[:, 0:48], ACT.Tanh, scale=0.5), t)
            gbk.free = [a]
            comp["g"] = dve.put(lambda e: e.tensor_scalar(gts, gts, 0.5, 0.5, ALU.mult, ALU.add), a)
            yield

        def lin_kv():
            fr = Q.refill()
            for u in range(2):
                segs = [(lambda a, g=g, c=c: a.rearrange("p (k c g d) -> p k c g d", k=8, g=2, c=2)[:, :, c, g, :],
                         w_in[:, 1280 + g * 256 + u * 128 + c * 64:1280 + g * 256 + u * 128 + c * 64 + 64]
                         .rearrange("(k p) d -> p k d", p=128))
                        for g in range(2) for c in range(2)]
                bk = t_unit(XT, 8, lambda a, k, c: a.rearrange("p (k c) -> p k c", k=8)[:, k, c * 128:(c + 1) * 128],
                            UNIT, segs, 2, LB)
                copy_T(bk, Q, 2 * u, 0.125, fr)
                yield
            fr = KS.refill()
            segs = [(lambda a, g=g: a.rearrange("p (k g c) -> p k g c", k=8, g=2)[:, :, g, :],
                     w_in[:, 2048 + g * 256:2048 + g * 256 + 128].rearrange("(k p) c -> p k c", p=128)) for g in range(2)]
            bk = t_unit(XT, 8, lambda a, k, c: a.rearrange("p (k g c) -> p k g c", k=8, g=2)[:, k, c, :],
                        UNIT, segs, 2, LB)
            copy_T(bk, KS, 0, 1.0, fr)
            yield
            fr = VS.refill()
            segs = [(lambda a, g=g: a.rearrange("p (k g c) -> p k g c", k=8, g=2)[:, :, g, :],
                     w_in[:, 2176 + g * 256:2176 + g * 256 + 128].rearrange("(k p) c -> p k c", p=128)) for g in range(2)]
            hi, lo, ub = P.unit(segs, UNIT)
            hi, lo = (x.rearrange("p (k c) -> p k c", k=8) for x in (hi, lo))
            bk = LB.take()

            def go(e):
                for i in range(2):
                    for k in range(8):
                        ins = mm3(e, bk.ap[:, i * 256:(i + 1) * 256], [XT.ap[:, z, k, i * 128:(i + 1) * 128] for z in (0, 1)],
                                  [hi[:, k, :], lo[:, k, :]], k == 0, k == 7)
                return ins
            t = pe.put(go, ub.ready, bk.refill(), XT.ready)
            ub.free = [t]
            XT.free.append(t)
            a = act.put(lambda e: e.activation(VS.ap[:, :, 0:256], bk.ap.rearrange("p (i c) -> p i c", i=2), ACT.Copy), t, fr)
            bk.free = [a]
            VS.ready = [a]
            yield
        gts = P.small(48)

        def lin_rest():
            bh, = proj_T(w_in, 0, XT)
            hs = TH.take()
            a = act.put(lambda e: e.activation(hs.ap, bh.ap, ACT.Copy), bh.ready, hs.refill())
            bh.free = [a]
            yield
            bb, = proj_T(w_in, 256, XT)
            yield
            bcg, = proj_T(w_in, 512, XT)
            z = m["zb"]
            v = dve.put(lambda e: e.tensor_tensor(z[:, :, 2:258], hs.ap.rearrange("p (c t) -> p c t", c=2),
                                                  bcg.ap.rearrange("p (c t) -> p c t", c=2), ALU.mult), a, bcg.ready)
            bcg.free = [v]
            hs.free = [v]
            yt = TM.take()
            w = yt.refill()
            for c in range(2):
                ya = yt.ap[:, c * 256:(c + 1) * 256]
                u = dve.put(lambda e, c=c, ya=ya: e.tensor_scalar(ya, z[:, c, 2:258], cols[:, 4 + c:5 + c], None, ALU.mult), v, w, cols_t)
                w = []
                for k in (1, 0):
                    u = dve.put(lambda e, c=c, ya=ya, k=k: e.scalar_tensor_tensor(
                        ya, z[:, c, k:k + 256], cols[:, 2 * k + c:2 * k + c + 1], ya, ALU.mult, ALU.add), u)
            u = dve.put(lambda e: e.tensor_tensor(yt.ap, yt.ap, bb.ap, ALU.mult), u, bb.ready)
            bb.free = [u]
            t = split(O1.ap, lambda x: x[:, 0:2, :], yt.ap.rearrange("p (c t) -> p c t", c=2), [u, frO])
            yt.free = t
            O1.ready += t
            yield
            yield from proj_N(w_in, 768, XT)
            bk = P.res
            SGb = B["sg"]
            w = SGb.refill()
            zz = SGb.ap[:, 0, :].rearrange("p (i c) -> p i c", i=2)
            for i in range(2):
                t1, th = TM.take(), TH.take()
                a = act.put(lambda e, i=i, t1=t1: e.activation(t1.ap, bk[i].ap, ACT.Square), bk[i].ready, t1.refill())
                v = dve.put(lambda e, t1=t1: e.tensor_scalar(t1.ap, t1.ap, GC, 1.0, ALU.mult, ALU.add), a)
                v = dve.put(lambda e, i=i, t1=t1: e.tensor_tensor(t1.ap, t1.ap, bk[i].ap, ALU.mult), v)
                a = act.put(lambda e, t1=t1, th=th: e.activation(th.ap, t1.ap, ACT.Tanh, scale=GS), v, th.refill())
                a = act.put(lambda e, i=i, t1=t1: e.activation(t1.ap, bk[i].ap, ACT.Copy, scale=0.5), a)
                bk[i].free = [a]
                v = dve.put(lambda e, i=i, t1=t1, th=th: e.scalar_tensor_tensor(zz[:, i, :], th.ap, 1.0, t1.ap, ALU.add, ALU.mult), a, w)
                w = []
                t1.free = [v]
                th.free = [v]
                st, mv, rs = P.small(6), P.small(2), P.small(1)
                vi = zz[:, i, 256:512]
                v = dve.put(lambda e, vi=vi, st=st: e.bn_stats(st, vi), v)
                v = dve.put(lambda e, st=st, mv=mv: e.bn_aggr(mv, st), v)
                p = pow_m05(rs, mv[:, 1:2], v, 1.0, 1)
                v = dve.put(lambda e, vi=vi, mv=mv, rs=rs: e.tensor_scalar(vi, vi, mv[:, 0:1], rs, ALU.subtract, ALU.mult), p)
                v = dve.put(lambda e, vi=vi: e.tensor_tensor(vi, vi, gn.ap[:, 0:256], ALU.mult), v, gn.ready)
                v = dve.put(lambda e, vi=vi: e.tensor_tensor(vi, vi, gn.ap[:, 256:512], ALU.add), v)
                gn.free = [v]
                yield
                sb_ = AB.take()

                def go(e, i=i, sb_=sb_):
                    for h in range(4):
                        ins = e.matmul(sb_.ap[:, h * 64:(h + 1) * 64], wt.ap[:, h * 128:(h + 1) * 128],
                                       zz[:, i, 256 + h * 64:256 + (h + 1) * 64], start=True, stop=True)
                    return ins
                t = pe.put(go, v, wt.ready, sb_.refill())
                wt.free.append(t)
                for h in range(4):
                    us = zz[:, i, h * 64:(h + 1) * 64]
                    v = dve.put(lambda e, us=us, h=h, sb_=sb_: e.scalar_tensor_tensor(
                        us, sb_.ap[:, h * 64:(h + 1) * 64], cols[:, 6 + h:7 + h], us, ALU.add, ALU.mult), t, cols_t)
                sb_.free = [v]
                yield
                tt, lp_ = to_T(AB, zz[:, i, 0:256], 2, O1.ap, 2, [v, frO], i)
                SGb.free += lp_ + [t]
                O1.ready += tt
                yield

        def nsa():
            def extra(j, hh, i):
                return [(128 * i, causalb, identb)]
            rss = [(P.small(24), P.small(24)) for _ in range(2)]

            def collect(i, bno, ob, waits, first):
                yc, (rs, rc) = YC[i], rss[i]
                gv = gts[:, 24 * i:24 * i + 24].rearrange("p (h b) -> p h b", b=3)
                r_ = rc[:, 8 * bno:8 * bno + 8]
                u = dve.put(lambda e: e.reciprocal(r_, rs[:, 8 * bno:8 * bno + 8]), waits)
                u = dve.put(lambda e: e.tensor_tensor(r_, r_, gv[:, :, bno], ALU.mult), u, comp["g"])
                ov = ob.ap.rearrange("p (h d) -> p h d", h=8)
                if first:
                    u = dve.put(lambda e: e.tensor_tensor(yc.ap.rearrange("p (h d) -> p h d", h=8), ov, bc(r_, 2, 64), ALU.mult),
                                u, ob.ready, yc.refill())
                    ob.free = [u]
                else:
                    tm = TM.take()
                    u = dve.put(lambda e: e.tensor_tensor(tm.ap.rearrange("p (h d) -> p h d", h=8), ov, bc(r_, 2, 64), ALU.mult),
                                u, ob.ready, tm.refill())
                    ob.free = [u]
                    u = dve.put(lambda e: e.tensor_tensor(yc.ap, yc.ap, tm.ap, ALU.add), u, yc.ready)
                    tm.free = [u]
                yc.ready = [u]

            def compressed(i):
                rs, rc = rss[i]
                er = ER.take()
                ev = er.ap[:, 0:120].rearrange("p (h n) -> p h n", h=8)
                w = er.refill()
                for hh in range(2):
                    b = AB.take()

                    def go(e, hh=hh, b=b):
                        for j in range(4):
                            ins = e.matmul(b.ap[:, j * 15:(j + 1) * 15], Q.ap[64 * hh:64 * hh + 64, j, i * 128:(i + 1) * 128],
                                           kcs[64 * hh:64 * hh + 64, :], start=True, stop=True)
                        return ins
                    t = pe.put(go, b.refill(), Q.ready, comp[0])
                    Q.free.append(t)
                    v = dve.put(lambda e, hh=hh, b=b: e.tensor_tensor(
                        ev[:, 4 * hh:4 * hh + 4, :], b.ap[:, 0:60].rearrange("p (h n) -> p h n", h=4),
                        bc(C("am")[:, 15 * i:15 * i + 15], 1, 4), ALU.add), t, w)
                    w = []
                    b.free = [v]
                mx = P.small(8)
                v = dve.put(lambda e: e.tensor_reduce(mx, ev, AX, ALU.max), v)
                v = dve.put(lambda e: e.tensor_tensor(ev, ev, bc(mx, 2, 15), ALU.subtract), v)
                a = act.put(lambda e: e.activation(er.ap[:, 0:120], er.ap[:, 0:120], ACT.Exp), v)
                v1_ = dve.put(lambda e: e.tensor_reduce(rs[:, 0:8], ev, AX, ALU.add), a)
                v = dve.put(lambda e: e.tensor_tensor(ev, ev, bc(C("mm")[:, 15 * i:15 * i + 15], 1, 8), ALU.mult), a, v1_)
                yield
                etv = []
                for half in range(2):
                    tb = AB.take()

                    def go(e, half=half, tb=tb):
                        for h in range(4):
                            x = 4 * half + h
                            ins = e.transpose(tb.ap[0:15, h * 128:(h + 1) * 128], er.ap[:, x * 15:(x + 1) * 15], ident)
                        return ins
                    t = pe.put(go, v, tb.refill(), consts)
                    et = ET.take()
                    a = act.put(lambda e, et=et, tb=tb: e.activation(et.ap[0:15, :], tb.ap[0:15, :], ACT.Copy), t, et.refill())
                    tb.free = [a]
                    etv.append((et, a))
                er.free = [t]
                yield
                ob = AB.take()

                def go(e):
                    for h in range(8):
                        g = h // 4
                        ins = e.matmul(ob.ap[:, h * 64:(h + 1) * 64], etv[g][0].ap[0:15, (h % 4) * 128:(h % 4 + 1) * 128],
                                       vcs[:, g * 64:(g + 1) * 64], start=True, stop=True)
                    return ins
                t = pe.put(go, ob.refill(), etv[0][1], etv[1][1], comp[1])
                etv[0][0].free = [t]
                etv[1][0].free = [t]
                P.vcs_free = [t]
                ob.ready = [t]
                collect(i, 0, ob, [v1_], False)
                yield

            def full(i, bno):
                rs, rc = rss[i]
                ob = AB.take()
                ob.wait, ob.vready = ob.refill(), VS.ready
                ends = []

                def K(hh, j, rdy=False):
                    return KS.ready if rdy else KS.ap[64 * hh:64 * hh + 64, bno - 1, :]

                def vof(mt, vs):
                    return VS.ap[:, mt, (bno - 1) * 128 + vs * 64:(bno - 1) * 128 + (vs + 1) * 64]

                def heads(jp, hh):
                    js = (2 * jp, 2 * jp + 1)
                    hs = [hh * 4 + j for j in js]
                    er, t = scores(Q, K, js, hh, i, extra, [rs[:, 8 * bno + h:8 * bno + h + 1] for h in hs])
                    KS.free.append(t)
                    ends.append(er.ready)
                    yield
                    yield
                    VS.free.append(weigh(er, [(h, hh) for h in hs], i, ob, vof, 64))
                    yield
                yield from weave([heads(jp, hh) for jp in range(2) for hh in range(2)], 2)
                collect(i, bno, ob, ends, bno == 1)
                yield

            def finish(i):
                yc = YC[i]
                tt, lp_ = to_T(AB, yc.ap, 4, O1.ap, 4, [yc.ready, frO], i)
                yc.free = lp_
                O1.ready += tt
                yield
            return chain(full(0, 1), full(0, 2), full(1, 1), full(1, 2), compressed(0), compressed(1), finish(0), finish(1))

        for _ in lin_kv():
            pass
        def tail():
            P.flush()
            acc_.append(out_begin())
            out_part(I["w_out_2"][l], acc_[0], 0)
            yield
        acc_ = []
        mix(chain(lin_cmp(), lin_rest(), tail()), nsa(), 3)
        acc = acc_[0]
        out_part(I["w_out_2"][l], acc, 4)
        layer_norm(acc, cols[:, 28:44], cols_t, AB)
        if l == DEPTH - 1:
            load_gb(I["ln3_g_2"][l], I["ln3_b_2"][l])
        acc = swiglu(l, 2)
        return layer_norm(acc, cols[:, 44:60], cols_t, LB, final=l == DEPTH - 1)

    for l in range(DEPTH):
        outs = second(l)
    sp.items.append((lambda e: None, outs, Tok(), None))


def build(nc, I, out_ap):
    with ExitStack() as ctx:
        def sb(name, shape, dt=F):
            return ctx.enter_context(nc.sbuf_tensor(name, shape, dt))

        m = {
            "raw": sb("raw", [128, NRAW, UNIT]), "hl": sb("hl", [128, NHL, 2, UNIT], R),
            "const": sb("cst", [128, NCONST]), "maskb": sb("maskb", [128, 3, 128], BF),
            "x": sb("xs", [128, 2, D]), "xt": sb("xt", [128, 2, 8, S], R),
            "o1": sb("o1", [128, 2, 8, S], R), "o2": sb("o2", [128, 2, 4, S], R), "gb": sb("gb", [128, 2, D]),
            "th": sb("th", [128, 2, 512]), "tm": sb("tm", [128, 5, 512]), "rt": sb("rt", [128, 2, 512]), "er": sb("er", [128, 5, 512]),
            "ai": sb("ai", [128, 2, 128], R), "et": sb("et", [128, 3, 512]), "mhalf": sb("mhalf", [128, 8]), "small": sb("small", [128, 1340]),
            "stage": sb("stage", [64, 128]), "stage2": sb("stage2", [32, 2, 128]), "gn": sb("gn", [128, 512]),
            "vcs": sb("vcs", [15, 128]), "zb": sb("zb", [128, 2, 258]),
            "q1": sb("q1", [128, 4, S]), "k1": sb("k1", [128, 4, S]), "sg": sb("sg", [128, 2, 1024]),
            "w2": sb("w2", [128, 2, 64]),
            "psum": ctx.enter_context(nc.psum_tensor("ps", [128, 8, 512], F)),
        }
        m = {k: v[:] for k, v in m.items()}
        qkv, v1 = sb("qkv", [128, 4096])[:], sb("v1", [128, 1024])[:]
        m["q0"] = qkv[:, 0:1024].rearrange("p (j t) -> p j t", j=4)
        m["k0"] = qkv[:, 1024:2048].rearrange("p (j t) -> p j t", j=4)
        m["v0"] = qkv[:, 2048:4096].rearrange("p (i c) -> p i c", i=2)
        m["w1"] = qkv.rearrange("p (n c) -> p n c", n=2)
        m["v1"] = v1.rearrange("p (i c) -> p i c", i=2)
        m["vs"] = v1[:, 0:512].rearrange("p (i c) -> p i c", i=2)
        m["wt"] = v1[:, 512:1024]
        m["ka"] = m["k1"].rearrange("p j t -> p (j t)")[:, 512:992]
        sems = {k: ctx.enter_context(nc.semaphore("s_" + k)) for k in
                ["pe", "act", "dve", "pool", "sp", "const", "x", "gb", "stage", "gn", "lv", "pes", "w2", "w1", "gw",
                 "out0", "out1"] + [f"raw{i}" for i in range(NRAW)]}
        units = None
        for _ in range(2):
            P = Program(m, sems, units)
            P.pe_free, P.vcs_free = [], []
            script(P, I, out_ap)
            units = P.units
        for q in (P.pe, P.act, P.dve, P.pool, P.sp):
            q.number()
        block = ctx.enter_context(nc.Block())
        block.sync(P.sp.emit)
        block.tensor(P.pe.emit)
        block.vector(P.dve.emit)
        block.scalar(P.act.emit)
        block.gpsimd(P.pool.emit)


_INS = ["x", "w_in", "ret_norm_g", "ca_rel_bias", "da_lambda_q1", "da_lambda_k1", "da_lambda_q2", "da_lambda_k2",
        "da_norm_g", "w_branch_a", "w_branch_b", "w_branch_c", "b_merge", "w_out", "ln1_g", "ln1_b", "w_ffn_in",
        "w_ffn_out", "ln2_g", "ln2_b", "ffn1_gate_2", "ffn1_up_2", "ffn1_down_2", "ln1_g_2", "ln1_b_2", "w_in_2",
        "conv_w_2", "gmlp_ln_g_2", "gmlp_ln_b_2", "gmlp_w_2", "gmlp_b_2", "ck_pe_2", "ck_w1_2", "ck_b1_2", "ck_w2_2",
        "cv_pe_2", "cv_w1_2", "cv_b1_2", "cv_w2_2", "w_out_2", "ln2_g_2", "ln2_b_2", "ffn2_gate_2", "ffn2_up_2",
        "ffn2_down_2", "ln3_g_2", "ln3_b_2"]


def kernel(**inputs):
    import concourse.bacc as bacc
    from concourse.bass_utils import run_bass_kernel_spmd

    nc = bacc.Bacc("TRN2", target_bir_lowering=False, num_devices=1, dynamic_dma_scratch_size=256)
    arrays, aps = {}, {}
    for name in _INS:
        a = np.ascontiguousarray(inputs[name])
        arrays["in_" + name] = a
        aps[name] = nc.dram_tensor("in_" + name, a.shape, mybir.dt.from_np(a.dtype), kind="ExternalInput").ap()
    arrays["in_const"] = constants()
    aps["const"] = nc.dram_tensor("in_const", (128, NCONST), F, kind="ExternalInput").ap()
    out = nc.dram_tensor("out", (1, S, D), F, kind="ExternalOutput").ap()
    build(nc, aps, out)
    r = run_bass_kernel_spmd(nc, [arrays], core_ids=[0])
    return r.results[0]["out"]
```

```python
from contextlib import ExitStack
import math

import numpy as np
import concourse.bass as bass
from concourse import mybir
from concourse.alu_op_type import AluOpType as ALU

F = mybir.dt.float32
R = mybir.dt.float32r
BF = mybir.dt.bfloat16
ACT = mybir.ActivationFunctionType
AX = mybir.AxisListType.X

DEPTH = 2
D = 1024
S = 256
FF = 2816
ALPHA = (2.0 * DEPTH) ** 0.25
EPS = 1e-5
NEG = -1e30
GC = 0.044715
GS = math.sqrt(2.0 / math.pi)

UNIT = 2048
RATIO1 = 2.5
RATIO2 = 3.0
WIDTH = 2
NRAW = 3
NHL = 3

CO = {}
_at = 0
for _n, _w in (("ident", 128), ("flip", 128), ("cosR", 128), ("sinR", 256), ("cosD", 64), ("sinD", 128), ("decay", 1024),
               ("chunk", 128), ("causal", 128), ("tril", 128), ("am", 30), ("mm", 30)):
    CO[_n] = (_at, _at + _w)
    _at += _w
NCONST = _at


def constants():
    c = np.zeros((128, NCONST), np.float32)
    p = np.arange(128)

    def put(name, a):
        c[:, CO[name][0]:CO[name][1]] = a.reshape(128, -1)

    put("ident", np.eye(128))
    put("flip", np.eye(128)[:, ::-1])
    for name, d in (("R", 128), ("D", 64)):
        inv = (np.float32(10000.0) ** (-np.arange(0, d, 2, dtype=np.float32) / np.float32(d))).astype(np.float32)
        ang = (np.arange(S, dtype=np.float32)[:, None] * inv[None, :]).astype(np.float32)
        cos = np.cos(ang).astype(np.float32).reshape(2, 128, d // 2).transpose(1, 0, 2)
        sin = np.sin(ang).astype(np.float32).reshape(2, 128, d // 2).transpose(1, 0, 2)
        put("cos" + name, cos)
        put("sin" + name, np.stack([-sin, sin], axis=2))
    lg = np.log1p(-np.exp2(-5.0 - np.arange(4)))
    n = np.arange(S)
    cn, cm = n[None, :] // 64, p[:, None] // 64
    diff = n[None, :] - p[:, None]
    dec = np.zeros((128, 4, S))
    for h in range(4):
        dec[:, h] = np.where(cn >= cm, np.exp(lg[h] * np.where(cn == cm, np.abs(diff), diff)), 0.0)
    put("decay", dec * 128 ** -0.5)
    put("chunk", np.where((p[:, None] >= 64) & (p[None, :] < 64), NEG, 0.0))
    put("causal", np.where(p[:, None] > p[None, :], NEG, 0.0))
    put("tril", np.where(p[None, :] <= p[:, None], 1.0, 0.0))
    t = p[:, None, None] + 128 * np.arange(2)[None, :, None]
    ok = 16 * np.arange(15)[None, None, :] + 31 <= t
    put("am", np.where(ok, 0.0, NEG))
    put("mm", np.where(ok, 1.0, 0.0))
    return c


class Tok:

    def __init__(self, sem=None, value=0):
        self.sem, self.value, self.need = sem, value, False


def flat(ws):
    for w in ws:
        if w is None:
            continue
        if isinstance(w, Tok):
            yield w
        else:
            yield from flat(w)


class Queue:

    def __init__(self, sem):
        self.sem, self.items = sem, []

    def put(self, fn, *waits):
        tok = Tok(self.sem)
        ws = list(flat(waits))
        for w in ws:
            w.need = True
        self.items.append((fn, ws, tok, None))
        return tok

    def dma(self, fn, sem, value, *waits):
        tok = Tok(sem, value)
        ws = list(flat(waits))
        for w in ws:
            w.need = True
        self.items.append((fn, ws, tok, sem))
        return tok

    def number(self):
        n = 0
        for _, _, tok, dsem in self.items:
            if dsem is None and tok.need:
                n += 1
                tok.value = n

    def emit(self, e):
        seen = {}
        for fn, ws, tok, dsem in self.items:
            need = {}
            for w in ws:
                need[w.sem] = max(need.get(w.sem, 0), w.value)
            for s, v in need.items():
                if seen.get(s, 0) < v:
                    e.wait_ge(s, v)
                    seen[s] = v
            ins = fn(e)
            if dsem is not None:
                ins.then_inc(dsem, 16)
            elif tok.need:
                ins.then_inc(self.sem, 1)


class Buf:

    def __init__(self, ap, free=()):
        self.ap, self.ready, self._free, self.held = ap, [], list(free), False
        self.wait, self.vready, self.halves = [], [], [[], []]

    @property
    def free(self):
        return self._free

    @free.setter
    def free(self, toks):
        self._free, self.held = toks, False

    def refill(self):
        f, self._free, self.ready = self._free, [], []
        return f


class Ring:

    def __init__(self, bufs):
        self.bufs = list(bufs)

    def take(self):
        b = next(b for b in self.bufs if not b.held)
        self.bufs.remove(b)
        self.bufs.append(b)
        b.held = True
        return b


class Program:
    def __init__(self, mem, sems, units):
        self.m = mem
        self.pe, self.act, self.dve, self.pool, self.sp = (Queue(sems[k]) for k in ("pe", "act", "dve", "pool", "sp"))
        self.sems = sems
        self.planned, self.units, self.prepped = units, [], []
        self.got = 0
        self.raw = [Buf(mem["raw"][:, i, :]) for i in range(NRAW)]
        self.rawn = [0] * NRAW
        self.hl = [Buf(mem["hl"][:, i, :, :]) for i in range(NHL)]
        self.small_at = self.small_end = 0
        self.nstage = 0
        self.dman = {}
        self.pending = []
        self.ahead = NHL

    def small_turn(self):
        half = self.m["small"].shape[1] // 2
        self.small_end = half if self.small_end != half else 2 * half
        self.small_at = self.small_end - half

    def small(self, n):
        a = self.small_at
        self.small_at += n
        assert self.small_at <= self.small_end, self.small_at
        return self.m["small"][:, a:a + n]

    def load(self, q, name, out, src, *waits):
        n = self.dman[name] = self.dman.get(name, 0) + 1
        return q.dma(lambda e: e.dma_start(out, src), self.sems[name], 16 * n, *waits)

    def prep(self, k):
        segs, n = self.planned[k]
        r = k % NRAW
        raw, hl = self.raw[r], self.hl[k % NHL]
        waits = raw.refill()
        for view, src in segs:
            self.rawn[r] += 1
            out = view(raw.ap)
            dma = self.sp.dma(lambda e, o=out, s=src: e.dma_start(o, s), self.sems[f"raw{r}"], 16 * self.rawn[r], waits)
            waits = []
        src, hi, lo = raw.ap[:, 0:n], hl.ap[:, 0, 0:n], hl.ap[:, 1, 0:n]
        a = self.act.put(lambda e: e.activation(hi, src, ACT.Copy), dma, hl.refill())
        self.prepped.append(hl)

        hl.halves = []

        def low(parts=1):
            h = len(hl.halves)
            s = slice(h * n // parts, (h + 1) * n // parts)
            v = self.dve.put(lambda e: e.tensor_tensor(lo[:, s], src[:, s], hi[:, s].bitcast(F), ALU.subtract), a)
            raw.free = [v]
            hl.halves.append([a, v])
            if len(hl.halves) == parts:
                hl.halves = (hl.halves * 2)[:2]
                hl.ready = [*hl.halves]
        return low

    def prep_next(self):
        if self.planned is None or len(self.prepped) >= len(self.planned):
            return lambda parts=1: None
        return self.prep(len(self.prepped))

    def later(self, units, fn):
        self.pending.append([units, fn])

    def tick(self):
        for p in list(self.pending):
            p[0] -= 1
            if p[0] <= 0:
                self.pending.remove(p)
                p[1]()

    def flush(self):
        while self.pending:
            self.pending.pop(0)[1]()

    def unit(self, segs, n):
        self.units.append((segs, n))
        if self.planned is None:
            b = Buf(self.m["hl"][:, 0, :, :])
        else:
            while len(self.prepped) < min(len(self.planned), self.got + self.ahead):
                self.prep_next()()
            b = self.prepped[self.got]
        self.got += 1
        return b.ap[:, 0, 0:n], b.ap[:, 1, 0:n], b


def bc(ap, axis, n):
    a = ap.unsqueeze(axis)
    shape = list(a.shape)
    shape[axis] = n
    return a.to_broadcast(shape)


def mm3(e, out, l, r, start, stop):
    e.matmul(out, l[0], r[0], start=start, stop=False)
    e.matmul(out, l[0], r[1], start=False, stop=False)
    return e.matmul(out, l[1], r[0], start=False, stop=stop)


IDLE = "idle"


class Line(set):

    def until(self, *names):
        while not all(n in self for n in names):
            yield IDLE

    def mark(self, name):
        self.add(name)
        return iter(())


def mix(a, b, ratio=1.0):
    b = iter(b)
    due = 0.0
    for _ in a:
        due += ratio
        while due >= 1.0:
            due -= 1.0
            next(b, None)
    for _ in b:
        pass


def weave(tasks, width):
    tasks = iter(tasks)
    live = []
    while True:
        while len(live) < width:
            t = next(tasks, None)
            if t is None:
                break
            live.append(t)
        if not live:
            return
        idle = True
        for t in list(live):
            try:
                r = next(t)
            except StopIteration:
                live.remove(t)
                continue
            if r is not IDLE:
                idle = False
                yield
        if idle:
            yield IDLE


def tiles(parts, width):
    for tasks, last in parts:
        yield from weave(tasks, width)
        yield from last


def chain(*gens):
    for g in gens:
        if callable(g):
            g = g() or ()
        yield from g


def script(P, I, out_ap):
    m = P.m
    pe, act, dve, pool, sp = P.pe, P.act, P.dve, P.pool, P.sp
    cst = m["const"]

    def C(name, *dims):
        a = cst[:, CO[name][0]:CO[name][1]]
        return a

    ident, flip = C("ident"), C("flip")
    X = m["x"]
    xload = P.load(sp, "x", X[:, :, :], I["x"][0].rearrange("(i p) d -> p i d", p=128))
    iload = P.load(sp, "ident", ident, I["const"][:, 0:128])

    LB = Ring([Buf(m["psum"][:, i, :]) for i in range(4)])
    AB = Ring([Buf(m["psum"][:, 4 + i, :]) for i in range(4)])
    TH = Ring([Buf(m["th"][:, i, :]) for i in range(2)])
    TM = Ring([Buf(m["tm"][:, i, :]) for i in range(5)])
    RT = Ring([Buf(m["rt"][:, i, :]) for i in range(2)])
    ER = Ring([Buf(m["er"][:, i, :]) for i in range(5)])
    ET = Ring([Buf(m["et"][:, i, :]) for i in range(3)])
    XT = Buf(m["xt"])
    O1 = Buf(m["o1"])
    O2 = Buf(m["o2"])
    GB = Buf(m["gb"])
    BT = GB
    BTap = m["gb"].rearrange("p a (b c) -> p (a b) c", c=S)

    def split(dst, sl, src, waits, scale=1.0):
        hi, lo = sl(dst[:, 0]), sl(dst[:, 1])
        a = act.put(lambda e: e.activation(hi, src, ACT.Copy, scale=scale), waits)
        if scale == 1.0:
            v = dve.put(lambda e: e.tensor_tensor(lo, src, hi.bitcast(F), ALU.subtract), a)
        else:
            v = dve.put(lambda e: e.scalar_tensor_tensor(lo, src, scale, hi.bitcast(F), ALU.mult, ALU.subtract), a)
        return [a, v]

    def transposes(ring, blocks, waits):
        b = ring.take()

        def go(e):
            for k, x in enumerate(blocks):
                i = e.transpose(b.ap[:, k * 128:(k + 1) * 128], x, ident)
            return i
        b.ready = [pe.put(go, b.refill(), waits, iload)]
        return b

    def to_T(ring, src, nk, dst, k0, waits, i, scale=1.0):
        toks = []
        for g in range(0, nk, 4):
            n = min(4, nk - g)
            b = transposes(ring, [src[:, (g + k) * 128:(g + k + 1) * 128] for k in range(n)], waits)
            t = split(dst, lambda x, g=g, n=n: x[:, k0 + g:k0 + g + n, i * 128:(i + 1) * 128],
                      b.ap[:, 0:n * 128].rearrange("p (k t) -> p k t", k=n), b.ready, scale)
            b.free = t
            toks += t
            last = b.ready
        return toks, last

    def wk(w, r0, kt, c0, nc):
        src = w[r0:r0 + kt * 128, c0:c0 + nc].rearrange("(k p) c -> p k c", p=128)
        return [(lambda a: a[:, 0:kt * nc].rearrange("p (k c) -> p k c", k=kt), src)], kt * nc

    def n_unit(w, r, c0, src, b, fr, first, last, per=4):
        segs, n = wk(w, r * 128, per, c0, 512)
        hi, lo, ub = P.unit(segs, n)
        hi, lo = (x.rearrange("p (k c) -> p k c", k=per) for x in (hi, lo))
        for i in range(2):
            def go(e, i=i):
                for k in range(per):
                    ins = mm3(e, b[i].ap, [src.ap[:, z, r + k, i * 128:(i + 1) * 128] for z in (0, 1)],
                              [hi[:, k, :], lo[:, k, :]], first and k == 0, last and k == per - 1)
                return ins
            t = pe.put(go, ub.ready, fr[i], src.ready)
            fr[i] = []
            b[i].ready = [t]
        ub.free = [t]
        src.free.append(t)
        P.tick()

    def proj_N(w, c0, src, nk=8):
        b = [LB.take(), LB.take()]
        fr = [x.refill() for x in b]
        if src.half:
            P.ahead = 1
            us = []
            for r in (0, 4):
                segs, n = wk(w, r * 128, 4, c0, 512)
                hi, lo, ub = P.unit(segs, n)
                us.append((*(x.rearrange("p (k c) -> p k c", k=4) for x in (hi, lo)), ub))

            def pieces(n, i, parts):
                hi, lo, ub = us[n]
                for p in parts:
                    def go(e, p=p):
                        for k in (2 * p, 2 * p + 1):
                            ins = mm3(e, b[i].ap, [src.ap[:, z, 4 * n + k, i * 128:(i + 1) * 128] for z in (0, 1)],
                                      [hi[:, k, :], lo[:, k, :]], n == 0 and k == 0, n == 1 and k == 3)
                        return ins
                    t = pe.put(go, ub.halves[p], fr[i], src.kt[i][4 * n + 2 * p])
                b[i].ready = [t]
                if i == 1:
                    ub.free = [t]
                    src.free.append(t)
            in_halves(src, pieces)
            yield
            P.res = b
            return
        for r in range(0, nk, 4):
            n_unit(w, r, c0, src, b, fr, r == 0, r + 4 == nk)
            yield
        P.res = b

    def t_unit(src, nk, view, n_el, segs, ncols, ring):
        hi, lo, ub = P.unit(segs, n_el)
        banks = []
        for c in range(0, ncols, 2):
            b = ring.take()
            fr = b.refill()
            for cc in range(c, min(c + 2, ncols)):
                def go(e, cc=cc, b=b, c=c):
                    for k in range(nk):
                        ins = mm3(e, b.ap[:, (cc - c) * 256:(cc - c) * 256 + 256], [view(hi, k, cc), view(lo, k, cc)],
                                  [src.ap[:, z, k, :] for z in (0, 1)], k == 0, k == nk - 1)
                    return ins
                t = pe.put(go, ub.ready, fr, src.ready)
                fr = []
            b.ready = [t]
            banks.append(b)
        ub.free = [t]
        src.free.append(t)
        P.tick()
        return banks

    def first_units(two, more):
        P.ahead = 1
        us = [P.unit(segs, UNIT) for segs in two]
        bs = [LB.take() for _ in two]
        frs = [b.refill() for b in bs]

        def pieces(n, i, parts):
            hi, lo, ub = us[n]
            hi, lo = (x.rearrange("p (k c) -> p k c", k=8) for x in (hi, lo))

            for p in [q for p in parts for q in (2 * p, 2 * p + 1)]:
                def go(e, p=p):
                    for k in range(2 * p, 2 * p + 2):
                        ins = mm3(e, bs[n].ap[:, i * 256:(i + 1) * 256], [XT.ap[:, z, k, i * 128:(i + 1) * 128] for z in (0, 1)],
                                  [hi[:, k, :], lo[:, k, :]], k == 0, k == 7)
                    return ins
                t = pe.put(go, ub.halves[p // 2], frs[n], XT.kt[i][2 * p])
            bs[n].ready = [t]
            if i == 1:
                ub.free = [t]
                XT.free.append(t)
        in_halves(XT, pieces, more)
        return bs

    def proj_T(w, c0, src, nk=8, cols=256, ring=None, srck=0):
        segs, n = wk(w, 0, nk, c0, cols)
        return t_unit(src, nk, lambda a, k, c: a.rearrange("p (k c) -> p k c", k=nk)[:, k, c * 128:(c + 1) * 128],
                      n, segs, cols // 128, ring or LB)

    def pow_m05(dst, src, waits, scale, n, eps=EPS):
        a = pool.put(lambda e: e.tensor_scalar(src, src, scale, eps, ALU.mult, ALU.add), waits)
        return pool.put(lambda e: e.tensor_tensor(dst, src, m["mhalf"][:, 0:n], ALU.pow), a, half_ready)

    half_ready = dve.put(lambda e: e.memset(m["mhalf"][:, :], -0.5))
    zpad = dve.put(lambda e: e.memset(m["zb"][:, :, 0:2], 0.0))

    def load_gb(g, b):
        w = GB.refill()
        P.load(sp, "gb", GB.ap[:, 0, :], g.partition_broadcast(128), w)
        GB.ready = [P.load(sp, "gb", GB.ap[:, 1, :], b.partition_broadcast(128))]

    def residual(b, i, c, waits, kt=None):
        def go(e):
            for k in range(4):
                for z in (0, 1):
                    ins = e.matmul(b.ap[:, k * 128:(k + 1) * 128], XT.ap[:, z, 4 * c + k, i * 128:(i + 1) * 128], ai,
                                   start=k == 0 and z == 0, stop=False)
            return ins
        t = pe.put(go, waits, kt or XT.ready, ai_ready)
        XT.free.append(t)

    def layer_norm(acc, gb, gb_t, rings, tail, final=False):
        X_ready, banks, fr, kt = [None, None], [None, None], XT.refill(), [[], []]

        def last(i):
            st, mv, rs = P.small(12), P.small(2), P.small(1)
            for c in range(2):
                b = acc[i][c]
                v = dve.put(lambda e, b=b, c=c: e.bn_stats(st[:, 6 * c:6 * c + 6], b.ap), b.ready)
            g = dve.put(lambda e: e.bn_aggr(mv, st), v)
            p = pow_m05(rs, mv[:, 1:2], g, 1.0, 1, EPS / ALPHA ** 2)
            for c in range(2):
                b, xs, gs = acc[i][c], X[:, i, c * 512:(c + 1) * 512], GB.ap[:, 0, c * 512:(c + 1) * 512]
                v = dve.put(lambda e, b=b, xs=xs, gs=gs: e.scalar_tensor_tensor(xs, b.ap, mv[:, 0:1], gs, ALU.subtract, ALU.mult),
                            g, X_free[i], GB.ready)
            for c in range(2):
                xs, bs = X[:, i, c * 512:(c + 1) * 512], GB.ap[:, 1, c * 512:(c + 1) * 512]
                v = dve.put(lambda e, xs=xs, bs=bs: e.scalar_tensor_tensor(xs, xs, rs, bs, ALU.mult, ALU.add), p, v)
                t = P.load(sp, f"out{i}", out_ap[0, i * 128:(i + 1) * 128, c * 512:(c + 1) * 512], xs, v)
            return t

        def stats(i, between=lambda: None):
            st, mv, rs, nb = P.small(12), P.small(2), P.small(1), P.small(1)
            for c in range(2):
                b = acc[i][c]
                v = dve.put(lambda e, b=b, c=c: e.bn_stats(st[:, 6 * c:6 * c + 6], b.ap), b.ready)
            g = dve.put(lambda e: e.bn_aggr(mv, st), v)
            p = pow_m05(rs, mv[:, 1:2], g, 1.0, 1, EPS / ALPHA ** 2)
            between()
            v = dve.put(lambda e: e.scalar_tensor_tensor(nb, mv[:, 0:1], -1.0, rs, ALU.mult, ALU.mult), p)
            b0, b1 = acc[i]
            a = act.put(lambda e: e.activation(X[:, i, 0:512], b0.ap, ACT.Identity, bias=nb, scale=rs), v, X_free[i])
            b0.free = [a]
            v = dve.put(lambda e: e.tensor_scalar(X[:, i, 512:1024], b1.ap, mv[:, 0:1], rs, ALU.subtract, ALU.mult), p, X_free[i])
            b1.free = [v]
            X_ready[i] = [a, v]

        def turn(i):
            banks[i] = [rings[i].take() for _ in range(2)]
            for q, b in enumerate(banks[i]):
                def go(e, b=b, q=q):
                    for k in range(4):
                        ins = e.transpose(b.ap[:, k * 128:(k + 1) * 128], X[:, i, (4 * q + k) * 128:(4 * q + k + 1) * 128], ident)
                    return ins
                b.ready = [pe.put(go, b.refill(), X_ready[i][q], consts)]
            X_free[i] = [*b.ready]

        def affine(i, between=lambda: None):
            tms = [TM.take() for _ in range(2)]
            ws = [tm.refill() for tm in tms]

            def full(c):
                for k in range(2 * (c % 2), 2 * (c % 2) + 2):
                    q, kk = c // 2, 4 * (c // 2) + k
                    b = banks[i][q]
                    o, src, g, h = tms[q].ap[:, k * 128:(k + 1) * 128], b.ap[:, k * 128:(k + 1) * 128], gb[:, kk:kk + 1], gb[:, 8 + kk:9 + kk]
                    if q:
                        v = act.put(lambda e, o=o, src=src, g=g, h=h: e.activation(o, src, ACT.Identity, bias=h, scale=g),
                                    b.ready, ws[q], gb_t)
                    else:
                        v = dve.put(lambda e, o=o, src=src, g=g, h=h: e.tensor_scalar(o, src, g, h, ALU.mult, ALU.add),
                                    b.ready, ws[q], gb_t)
                if c % 2:
                    b.free = [v]
                return v

            def parts(c):
                hi, lo = (XT.ap[:, z, 2 * c:2 * c + 2, i * 128:(i + 1) * 128] for z in (0, 1))
                return hi, lo, tms[c // 2].ap[:, 256 * (c % 2):256 * (c % 2) + 256].rearrange("p (k t) -> p k t", k=2)

            def high(c, t):
                hi, lo, f = parts(c)
                return act.put(lambda e: e.activation(hi, f, ACT.Copy), t, fr)

            def low(c, a):
                hi, lo, f = parts(c)
                v = dve.put(lambda e: e.tensor_tensor(lo, f, hi.bitcast(F), ALU.subtract), a)
                tms[c // 2].free = [v]
                kt[i].extend([[a, v]] * 2)
            f2, f0 = full(2), full(0)
            h0 = high(0, f0)
            f3, f1 = full(3), full(1)
            h1 = high(1, f1)
            between()
            h2, h3 = high(2, f2), high(3, f3)
            for c, h in enumerate((h0, h1, h2, h3)):
                low(c, h)

        if final:
            outs = [last(0)]
            for t in tail:
                t()
            return [*outs, last(1)]
        stats(0)
        for t in tail[:3]:
            t()
        low = P.prep_next()
        turn(0)
        tail[3]()
        affine(0, lambda: low(2))
        stats(1, lambda: low(2))
        XT.kt = kt
        XT.half = (lambda: turn(1), lambda: affine(1))

    def in_halves(src, pieces, more=lambda: None):
        turn, affine = src.half
        src.half = None
        pieces(0, 0, (0, 1))
        more()
        pieces(1, 0, (0,))
        turn()
        pieces(1, 0, (1,))
        affine()
        P.prep_next()()
        src.ready = [src.kt[i][k] for i in (0, 1) for k in (0, 2, 4, 6)]
        pieces(0, 1, (0, 1))
        pieces(1, 1, (0, 1))
        P.ahead = NHL
        P.tick()
        P.tick()

    X_free = [[], []]
    XT.half = O1.half = O2.half = None
    toks = []
    for i in range(2):
        t, lastpe = to_T(AB, X[:, i, :], 8, XT.ap, 0, xload, i)
        toks += t
        X_free[i] = lastpe
    XT.ready = toks
    for _ in range(2):
        P.prep_next()()
    cload = P.load(sp, "const", cst[:, 128:], I["const"][:, 128:])
    identb, chunkb, causalb = m["maskb"][:, 0, :], m["maskb"][:, 1, :], m["maskb"][:, 2, :]
    dve.put(lambda e: e.tensor_copy(identb, ident), iload, cload)
    dve.put(lambda e: e.tensor_copy(chunkb, C("chunk")))
    mask_ready = dve.put(lambda e: e.tensor_copy(causalb, C("causal")))
    ai = m["ai"]
    ai_ready = act.put(lambda e: e.activation(ai, ident, ACT.Copy), iload)
    consts = [iload, cload, mask_ready]

    def out_begin():
        acc = [[LB.take(), LB.take()] for _ in range(2)]
        for i in range(2):
            for c in range(2):
                residual(acc[i][c], i, c, acc[i][c].refill())
        return acc

    def out_part(w, acc, r):
        for c in range(2):
            n_unit(w, r, c * 512, O1, [acc[0][c], acc[1][c]], [[], []], False, False)

    def out_end(w, acc):
        us = []
        for c in range(2):
            segs, n = wk(w, 512, 4, c * 512, 512)
            P.ahead = NHL - c
            hi, lo, ub = P.unit(segs, n)
            us.append((*(x.rearrange("p (k c) -> p k c", k=4) for x in (hi, lo)), ub))

        def part(c, i, ks):
            hi, lo, ub = us[c]

            def go(e):
                for k in ks:
                    ins = mm3(e, acc[i][c].ap, [O1.ap[:, z, 4 + k, i * 128:(i + 1) * 128] for z in (0, 1)],
                              [hi[:, k, :], lo[:, k, :]], False, k == 3)
                return ins
            t = pe.put(go, ub.ready, O1.ready)
            acc[i][c].ready = [t]
            if i == 1 and ks[-1] == 3:
                ub.free = [t]
                O1.free.append(t)
        for c in range(2):
            part(c, 0, range(4))
        return [lambda c=c, ks=ks: part(c, 1, ks) for c in range(2) for ks in ((0, 1), (2, 3))]

    def ffn(gate_up, down, scale, setup=iter(())):
        o2_free = O2.refill()
        HT = [Buf(m["o2"][:, :, i, :], o2_free) for i in range(4)]

        view = lambda a, k, c: a.rearrange("p (k g c) -> p k g c", k=8, g=2)[:, k, c, :]

        def up(j, b=None):
            N = b is not None
            if not N:
                b, = t_unit(XT, 8, view, UNIT, gate_up(j), 2, LB)
            h, th, tm = HT[j % 4], TH.take(), TM.take()
            ga, up_ = b.ap[:, 0:256], b.ap[:, 256:512]
            tha, tma = th.ap[:, 0:256], tm.ap[:, 0:256]
            if N:
                ga, up_ = (b.ap.rearrange("p (i g c) -> p i g c", i=2, g=2)[:, :, g, :] for g in (0, 1))
                tha, tma = (x.rearrange("p (i c) -> p i c", i=2) for x in (tha, tma))
            a = act.put(lambda e: e.activation(tha, ga, ACT.Tanh, scale=0.5), b.ready, th.refill())
            v = dve.put(lambda e: e.scalar_tensor_tensor(tma, tha, 1.0, ga, ALU.add, ALU.mult), a, tm.refill())
            th.free = [v]
            v = dve.put(lambda e: e.scalar_tensor_tensor(tma, tma, 0.5 * scale / ALPHA, up_, ALU.mult, ALU.mult), v)
            b.free = [v]
            if N:
                def turn():
                    tb = transposes(LB, [tm.ap[:, i * 128:(i + 1) * 128] for i in (0, 1)], v)
                    tm.free = [*tb.ready]
                    h.ready = tb.free = split(h.ap, lambda x: x, tb.ap[:, 0:256], [tb.ready, h.refill()])
                P.later(1, turn)
                return
            t = split(h.ap, lambda x: x, tma, [v, h.refill()])
            h.ready = t
            tm.free = t

        def dn_unit(d):
            segs, n = wk(down, d * 256, 2, 0, 1024)
            hi, lo, ub = P.unit(segs, n)
            return (*(x.rearrange("p (k c) -> p k c", k=2) for x in (hi, lo)), ub)

        def dn(d, unit, i, c):
            hi, lo, ub = unit
            hs = [HT[(2 * d + k) % 4] for k in range(2)]

            def go(e):
                for k in range(2):
                    ins = mm3(e, acc[i][c].ap, [hs[k].ap[:, z, i * 128:(i + 1) * 128] for z in (0, 1)],
                              [hi[:, k, c * 512:(c + 1) * 512], lo[:, k, c * 512:(c + 1) * 512]],
                              False, d == 10 and k == 1)
                return ins
            t = pe.put(go, ub.ready, hs[0].ready, hs[1].ready)
            acc[i][c].ready = [t]
            if i == 1 and c == 1:
                for h in hs:
                    h.free = [t]
                ub.free = [t]
                P.tick()

        acc = []

        def begin(i):
            acc.append([AB.take(), AB.take()])
            for c in range(2):
                residual(acc[i][c], i, c, acc[i][c].refill(), [XT.kt[i][4 * c], XT.kt[i][4 * c + 2]])
        for j, b in enumerate(first_units([gate_up(0), gate_up(1)], lambda: begin(0))):
            up(j, b)
        begin(1)
        up(2)
        for d in range(9):
            u = dn_unit(d)
            for i in range(2):
                for c in range(2):
                    dn(d, u, i, c)
            for j in (2 * d + 3, 2 * d + 4):
                up(j)
            next(setup, None)
        for _ in setup:
            pass
        up(21)
        us = [dn_unit(9)]
        P.ahead = 2
        us.append(dn_unit(10))
        for d in (9, 10):
            for c in range(2):
                dn(d, us[d - 9], 0, c)
        O2.free = []

        def step(d, c):
            dn(d, us[d - 9], 1, c)
            O2.free = [h.free for h in HT]
        return acc, [lambda d=d, c=c: step(d, c) for d in (9, 10) for c in range(2)]

    def scores(q, k, js, hh, i, extra, mul=None):
        K = 128 * (i + 1)
        b = AB.take()
        fr = b.refill()

        def go(e):
            for n, j in enumerate(js):
                so = b.ap[:, n * K:(n + 1) * K]
                e.matmul(so, q.ap[64 * hh:64 * hh + 64, j, i * 128:(i + 1) * 128], k(hh, j)[:, 0:K],
                         start=True, stop=False)
                ex = extra(j, hh, i)
                for x, (c, l, r) in enumerate(ex):
                    ins = e.matmul(so[:, c:c + 128], l, r, start=False, stop=x == len(ex) - 1)
            return ins
        t = pe.put(go, fr, q.ready, k(0, 0, True), consts, P.bias)
        q.free.append(t)
        nj = len(js)
        nm = P.small(nj)
        v = dve.put(lambda e: e.tensor_reduce(nm, b.ap[:, 0:nj * K].rearrange("p (n k) -> p n k", n=nj), AX, ALU.max,
                                              negate=True), t)
        er = ER.take()
        w = [v, er.refill()]
        rs = []
        for n, j in enumerate(js):
            def ex_(e, n=n, r=None):
                return e.activation(er.ap[:, n * K:(n + 1) * K], b.ap[:, n * K:(n + 1) * K], ACT.Exp,
                                    bias=nm[:, n:n + 1], accum_out=mul[n])
            a = act.put(ex_, w)
            w = []
        b.free = [a]
        er.ready = [a]
        return er, t

    def weigh(er, heads, i, ob, v_of, odim, vfree):
        K = 128 * (i + 1)
        T = i + 1
        blocks = [er.ap[:, n * K + mt * 128:n * K + mt * 128 + 128] for n in range(len(heads)) for mt in range(T)]
        tb = transposes(AB, blocks, er.ready)
        er.free = [*tb.ready]
        et = ET.take()
        w = len(blocks) * 128
        if P.flip:
            a = act.put(lambda e: e.activation(et.ap[:, 0:w], tb.ap[:, 0:w], ACT.Copy), tb.ready, et.refill())
        else:
            a = dve.put(lambda e: e.tensor_copy(et.ap[:, 0:w], tb.ap[:, 0:w]), tb.ready, et.refill())
        P.flip = not P.flip
        tb.free = [a]
        yield

        def go(e):
            for n, (o, vs) in enumerate(heads):
                for mt in range(T):
                    x = n * T + mt
                    ins = e.matmul(ob.ap[:, o * odim:(o + 1) * odim], et.ap[:, x * 128:(x + 1) * 128], v_of(mt, vs),
                                   start=mt == 0, stop=mt == T - 1)
            return ins
        t = pe.put(go, a, ob.wait, ob.vready)
        ob.wait = []
        et.free = [t]
        ob.ready = [t]
        vfree.append(t)

    P.flip = True

    def sums(o, v):
        if not o:
            b = AB.take()
            b.wait, b.vready = b.refill(), v.ready
            o.append(b)
        return o[0]

    def rot(w, c0, nh, dh, dst, scale):
        yield from proj_N(w, c0, XT)
        b = P.res
        cos, sin = ("cosR", "sinR") if dh == 128 else ("cosD", "sinD")
        hd = dh // 2
        fr = dst.refill()
        for i in range(2):
            pv = b[i].ap.rearrange("p (h s d) -> p h s d", h=nh, s=2)
            cv = bc(bc(C(cos).rearrange("p (i d) -> p i d", i=2)[:, i, :], 1, 2), 1, nh)
            sv = C(sin).rearrange("p (i s d) -> p i s d", i=2, s=2)
            t1, t2 = RT.take(), TM.take()
            a1 = t1.ap.rearrange("p (h s d) -> p h s d", h=nh, s=2)
            a2 = t2.ap.rearrange("p (h s d) -> p h s d", h=nh, s=2)
            u1 = dve.put(lambda e, a1=a1, pv=pv, cv=cv: e.tensor_tensor(a1, pv, cv, ALU.mult), b[i].ready, t1.refill(), consts)
            w2 = t2.refill()
            for s in range(2):
                u2 = dve.put(lambda e, s=s, a2=a2, pv=pv, sv=sv, i=i: e.tensor_tensor(
                    a2[:, :, s, :], pv[:, :, 1 - s, :], bc(sv[:, i, s, :], 1, nh), ALU.mult), w2)
                w2 = []
            b[i].free = [u2]
            u = dve.put(lambda e, t1=t1, t2=t2: e.tensor_tensor(t1.ap, t1.ap, t2.ap, ALU.add), u1, u2)
            t2.free = [u]

            def turn(i=i, t1=t1, u=u):
                tb = transposes(AB, [t1.ap[:, k * 128:(k + 1) * 128] for k in range(4)], u)
                t1.free = [*tb.ready]
                a = act.put(lambda e: e.activation(dst.ap[:, :, i * 128:(i + 1) * 128],
                                                   tb.ap.rearrange("p (k t) -> p k t", k=4), ACT.Copy, scale=scale),
                            tb.ready, fr)
                tb.free = [a]
                dst.ready.append(a)
            P.later(1 + i, turn)

    def copy_N(w, c0, dst, sl):
        yield from proj_N(w, c0, XT)
        b = P.res
        for i in range(2):
            a = act.put(lambda e, i=i: e.activation(sl(dst.ap, i), b[i].ap, ACT.Copy), b[i].ready, dst.wait)
            dst.wait = []
            b[i].free = [a]
            dst.ready.append(a)
            yield

    def copy_T(banks, dst, t0, scale, waits=()):
        for k, b in enumerate(banks):
            a = act.put(lambda e, k=k, b=b: e.activation(dst.ap[:, t0 + 2 * k:t0 + 2 * k + 2, :],
                                                         b.ap.rearrange("p (c t) -> p c t", c=2), ACT.Copy, scale=scale),
                        b.ready, waits)
            b.free = [a]
            dst.ready.append(a)

    def staging(rows, n):
        w = P.stage_free
        for name_src, r0, r1 in rows:
            t = P.load(sp, "stage", m["stage"][r0:r1, :], name_src, w)
            w = []

        def turn():
            b = LB.take()
            tp = pe.put(lambda e: e.transpose(b.ap[:, 0:n], m["stage"][0:n, :], ident[0:n, 0:n]), t, b.refill(), consts)
            P.stage_free = [tp]
            col = P.small(n)
            a = dve.put(lambda e: e.tensor_copy(col, b.ap[:, 0:n]), tp)
            b.free = [a]
            return col, a
        return turn

    P.stage_free = []
    P.bias = []
    B = {k: Buf(m[k]) for k in ("q0", "k0", "q1", "k1", "v0", "v1", "sg", "gn", "w2")}

    def first_setup(l, o):
        P.small_turn()
        lam_init = 0.8 - 0.6 * math.exp(-0.3 * l)

        def rows(name):
            return I[name][l].rearrange("(r c) -> r c", c=128)
        turn = staging([(rows("b_merge"), 0, 24)] +
                       [(rows(nme), 24 + 8 * n, 32 + 8 * n) for n, nme in enumerate(("ln1_g", "ln1_b", "ln2_g", "ln2_b"))], 56)
        gn = B["gn"]
        w = gn.refill()
        P.load(sp, "gn", gn.ap[:, 0:256], I["ret_norm_g"][l].partition_broadcast(128), w)
        gl = P.load(sp, "gn", gn.ap[:, 256:384], I["da_norm_g"][l].partition_broadcast(128))
        lv = TM.take()
        w = lv.refill()
        for n, nme in enumerate(("da_lambda_q1", "da_lambda_k1", "da_lambda_q2", "da_lambda_k2")):
            tl = P.load(sp, "lv", lv.ap[:, n * 64:(n + 1) * 64], I[nme][l].partition_broadcast(128), w)
            w = []
        rb = I["ca_rel_bias"]
        src = bass.AP(rb.tensor, l * 8 * 513 + 129, [[1, 128], [513, 8], [1, 256]])
        tb = P.load(sp, "gb", BTap[:, :, :], src, BT.refill())
        yield
        yield
        bm, bm_t = turn()
        bmh = P.small(24)
        bmh_t = dve.put(lambda e: e.tensor_scalar(bmh, bm[:, 0:24], 0.5, None, ALU.mult), bm_t)
        a = dve.put(lambda e: e.tensor_scalar(gn.ap[:, 0:256], gn.ap[:, 0:256], 0.5, None, ALU.mult), gl)
        gn.ready = [a, dve.put(lambda e: e.tensor_scalar(gn.ap[:, 256:384], gn.ap[:, 256:384], 1.0 - lam_init, None, ALU.mult), gl)]
        yield
        lp, le, nlam = P.small(2), P.small(2), P.small(1)
        lvv = lv.ap[:, 0:256].rearrange("p (a b d) -> p a b d", a=2, b=2)
        a = dve.put(lambda e: e.tensor_tensor(lvv[:, :, 0, :], lvv[:, :, 0, :], lvv[:, :, 1, :], ALU.mult), tl)
        a = dve.put(lambda e: e.tensor_reduce(lp, lvv[:, :, 0, :], AX, ALU.add), a)
        lv.free = [a]
        a = act.put(lambda e: e.activation(le, lp, ACT.Exp), a)
        a = dve.put(lambda e: e.tensor_tensor(nlam, le[:, 1:2], le[:, 0:1], ALU.subtract), a)
        nlam_t = dve.put(lambda e: e.tensor_scalar(nlam, nlam, lam_init, None, ALU.subtract), a)
        yield
        BT.ready = [dve.put(lambda e: e.memset(BTap[0:64, :, 0:64], NEG), tb)]
        o.update(bm=bm, bmh=bmh, cols_t=bm_t, bm_t=bmh_t, nlam=nlam, nlam_t=nlam_t)

    def first(l, o, now, nxt):
        w_in = I["w_in"][l]
        gn = B["gn"]

        V0, V1, SG = B["v0"], B["v1"], B["sg"]

        def silu_gate(c0, c):
            yield from proj_N(w_in, c0, XT)
            b = P.res
            for i in range(2):
                th, tm = TH.take(), TM.take()
                a = act.put(lambda e, i=i, th=th: e.activation(th.ap, b[i].ap, ACT.Tanh, scale=0.5), b[i].ready, th.refill())
                v = dve.put(lambda e, i=i, th=th, tm=tm: e.scalar_tensor_tensor(tm.ap, th.ap, 1.0, b[i].ap, ALU.add, ALU.mult),
                            a, tm.refill())
                th.free = [v]
                b[i].free = [v]
                v = dve.put(lambda e, i=i, tm=tm: e.tensor_tensor(
                    SG.ap[:, i, c * 512:(c + 1) * 512].rearrange("p (h d) -> p h d", h=2),
                    tm.ap.rearrange("p (h d) -> p h d", h=2), bc(gn.ap[:, 0:256], 1, 2), ALU.mult), v, gn.ready, SG.wait)
                SG.wait = []
                tm.free = [v]
                SG.ready.append(v)
                gn.free.append(v)
                yield

        def linear_a():
            yield from rot(w_in, 0, 4, 128, B["q0"], 1.0)
            yield from rot(w_in, 512, 4, 128, B["k0"], 1.0)
            V0.wait = V0.refill()
            for c in range(2):
                yield from copy_N(w_in, 1024 + 512 * c, V0, lambda a, i, c=c: a[:, i, c * 512:(c + 1) * 512])
            SG.wait = SG.refill()
            for c in range(2):
                yield from silu_gate(2048 + 512 * c, c)

        def linear_b():
            for dst, c0, sc in ((B["q1"], 3072, 0.125), (B["k1"], 3584, 1.0)):
                fr = dst.refill()
                for u in range(2):
                    copy_T(proj_T(w_in, c0 + 256 * u, XT), dst, 2 * u, sc, fr)
                    yield
            V1.wait = V1.refill()
            yield from copy_N(w_in, 4096, V1, lambda a, i: a[:, i, :])

        def linear_c():
            yield from rot(w_in, 4608, 8, 64, B["q0"], 0.125)
            yield from rot(w_in, 5120, 8, 64, B["k0"], 1.0)
            V0.wait = V0.refill()
            yield from copy_N(w_in, 5632, V0, lambda a, i: a[:, i, 0:512])

        MT = Buf(m["sg"])

        def merge(br, w_br, src, nk):
            per = 1 if nk == 8 else 2
            for u in range(4):
                gb_, = proj_T(w_in, 6144 + br * 1024 + u * 256, XT)
                th = TH.take()
                w = th.refill()
                for c in range(2):
                    col = br * 8 + u * 2 + c
                    a = act.put(lambda e, c=c, col=col, th=th, gb_=gb_: e.activation(
                        th.ap[:, c * 256:(c + 1) * 256], gb_.ap[:, c * 256:(c + 1) * 256], ACT.Tanh,
                        bias=bmh[:, col:col + 1], scale=0.5), gb_.ready, w, bm_t)
                    w = []
                gb_.free = [a]
                yield
                if nk == 8:
                    bb, = proj_T(w_br, u * 256, src)
                elif u % 2 == 0:
                    bb, nxt = proj_T(w_br, u * 256, src, nk=4, cols=512)
                else:
                    bb = nxt
                mt = MT.ap.rearrange("p a b -> p (a b)")[:, u * 512:(u + 1) * 512]
                if br == 0:
                    v = dve.put(lambda e, mt=mt, th=th, bb=bb: e.scalar_tensor_tensor(mt, th.ap, 1.0, bb.ap, ALU.add, ALU.mult),
                                bb.ready, a, MT.wait)
                    MT.ready.append(v)
                else:
                    v = dve.put(lambda e, th=th, bb=bb: e.scalar_tensor_tensor(th.ap, th.ap, 1.0, bb.ap, ALU.add, ALU.mult),
                                bb.ready, a)
                    bb.free = [v]
                    v = dve.put(lambda e, mt=mt, th=th: e.tensor_tensor(mt, mt, th.ap, ALU.add), v, MT.ready)
                    MT.ready[u] = v
                if br == 0:
                    bb.free = [v]
                th.free = [v]
                yield

        def retention():
            q, k = B["q0"], B["k0"]
            fr1 = O1.refill()

            def head(h):
                b = AB.take()

                def go(e, h=h, b=b):
                    e.matmul(b.ap[:, 0:256], k.ap[:, h, 0:128], q.ap[:, h, :], start=True, stop=True)
                    return e.matmul(b.ap[:, 256:384], k.ap[:, h, 128:256], q.ap[:, h, 128:256], start=True, stop=True)
                t = pe.put(go, b.refill(), q.ready, k.ready)
                q.free.append(t)
                k.free.append(t)
                er = ER.take()
                dh = C("decay")[:, h * 256:(h + 1) * 256]
                dve.put(lambda e, er=er, b=b, dh=dh: e.tensor_tensor(er.ap[:, 0:256], b.ap[:, 0:256], dh, ALU.mult), t, er.refill(), consts)
                v = dve.put(lambda e, er=er, b=b, dh=dh: e.tensor_tensor(er.ap[:, 256:384], b.ap[:, 256:384], dh[:, 0:128], ALU.mult))
                b.free = [v]
                yield
                ob = AB.take()

                def go2(e, h=h, er=er, ob=ob):
                    vs = [V0.ap[:, i, h * 256:(h + 1) * 256] for i in range(2)]
                    e.matmul(ob.ap[:, 0:256], er.ap[:, 0:128], vs[0], start=True, stop=True)
                    e.matmul(ob.ap[:, 256:512], er.ap[:, 128:256], vs[0], start=True, stop=False)
                    return e.matmul(ob.ap[:, 256:512], er.ap[:, 256:384], vs[1], start=False, stop=True)
                t = pe.put(go2, ob.refill(), v, V0.ready)
                er.free = [t]
                V0.free.append(t)
                ss, rs = P.small(2), P.small(2)
                tm = TM.take()
                w = tm.refill()
                for i in range(2):
                    a = act.put(lambda e, i=i, tm=tm, ob=ob, ss=ss: e.activation(
                        tm.ap[:, 0:256], ob.ap[:, i * 256:(i + 1) * 256], ACT.Square, accum_out=ss[:, i:i + 1]), t, w, a if i else None)
                    w = []
                p = pow_m05(rs, ss, a, 1.0 / 256, 2)
                for i in range(2):
                    v = dve.put(lambda e, i=i, tm=tm, ob=ob, rs=rs, h=h: e.scalar_tensor_tensor(
                        tm.ap[:, i * 256:(i + 1) * 256], ob.ap[:, i * 256:(i + 1) * 256], rs[:, i:i + 1],
                        SG.ap[:, i, h * 256:(h + 1) * 256], ALU.mult, ALU.mult), p, a, SG.ready)
                ob.free = [v]
                SG.free.append(v)
                yield
                tb = transposes(AB, [tm.ap[:, i * 256 + c * 128:i * 256 + (c + 1) * 128] for c in range(2) for i in range(2)], v)
                tm.free = [*tb.ready]
                tt = split(O1.ap, lambda x, h=h: x[:, 2 * h:2 * h + 2, :], tb.ap.rearrange("p (c t) -> p c t", c=2),
                           [tb.ready, fr1])
                tb.free = tt
                O1.ready += tt
                yield
            return weave([head(h) for h in range(4)], 2)

        def ca_attention():
            q, kk, v = B["q1"], B["k1"], V1
            fr = O2.refill()

            def K(hh, j, rdy=False):
                return kk.ready if rdy else kk.ap[64 * hh:64 * hh + 64, j, :]

            def extra(j, hh, i):
                h = 2 * j + hh
                if i == 0:
                    return [(0, BTap[:, h, 0:128], flip)]
                return [(0, BTap[:, h, 128:256], flip), (128, BTap[:, h, 0:128], flip)]
            vof = lambda mt, vs: v.ap[:, mt, vs * 64:(vs + 1) * 64]

            def tile(i):
                rs, rc = P.small(8), P.small(8)
                o, ends = [], []

                def heads(jp, hh):
                    js = (2 * jp, 2 * jp + 1)
                    hs = [2 * j + hh for j in js]
                    ob = sums(o, v)
                    er, t = scores(q, K, js, hh, i, extra, [rs[:, h:h + 1] for h in hs])
                    kk.free.append(t)
                    BT.free.append(t)
                    ends.append(er.ready)
                    yield
                    yield
                    yield from weigh(er, [(h, h) for h in hs], i, ob, vof, 64, v.free)
                    yield

                def last():
                  ob = o[0]
                  u = dve.put(lambda e: e.reciprocal(rc, rs), ends)
                  tm = TM.take()
                  u = dve.put(lambda e: e.tensor_tensor(
                      tm.ap.rearrange("p (h d) -> p h d", h=8), ob.ap.rearrange("p (h d) -> p h d", h=8),
                      bc(rc, 2, 64), ALU.mult), ob.ready, u, tm.refill())
                  ob.free = [u]
                  yield
                  tt, lp_ = to_T(AB, tm.ap, 4, O2.ap, 0, [u, fr], i)
                  tm.free = lp_
                  O2.ready += tt
                  yield
                return [heads(jp, hh) for jp in range(2) for hh in range(2)], last()
            return tiles([tile(0), tile(1)], WIDTH)

        def da_attention():
            q, kk, v = B["q0"], B["k0"], V0
            fr = O3.refill()

            def K(hh, j, rdy=False):
                return kk.ready if rdy else kk.ap[64 * hh:64 * hh + 64, j, :]

            def extra(j, hh, i):
                return [(128 * i, chunkb, identb)]
            vof = lambda mt, vs: v.ap[:, mt, vs * 128:(vs + 1) * 128]

            def tile(i):
                o = []
                KK = 128 * (i + 1)

                def heads(jp):
                    js = (2 * jp, 2 * jp + 1)
                    ob = sums(o, v)
                    rs, rc = P.small(4), P.small(4)
                    e0, t = scores(q, K, js, 0, i, extra, [rs[:, n:n + 1] for n in range(2)])
                    yield
                    e1, t = scores(q, K, js, 1, i, extra, [rs[:, 2 + n:3 + n] for n in range(2)])
                    kk.free.append(t)
                    yield
                    u = dve.put(lambda e: e.reciprocal(rc, rs), e1.ready, e0.ready)
                    u = dve.put(lambda e: e.tensor_scalar(rc[:, 2:4], rc[:, 2:4], nlam, None, ALU.mult), u, nlam_t)
                    for n in range(2):
                        s1 = e1.ap[:, n * KK:(n + 1) * KK]
                        u1 = dve.put(lambda e, s1=s1, n=n: e.tensor_scalar(s1, s1, rc[:, 2 + n:3 + n], None, ALU.mult), u)
                    for n in range(2):
                        s0, s1 = (x.ap[:, n * KK:(n + 1) * KK] for x in (e0, e1))
                        u2 = dve.put(lambda e, s0=s0, s1=s1, n=n: e.scalar_tensor_tensor(
                            s0, s0, rc[:, n:n + 1], s1, ALU.mult, ALU.add), u1)
                    e1.free = [u2]
                    e0.ready = [u2]
                    yield
                    yield from weigh(e0, [(j, j) for j in js], i, ob, vof, 128, v.free)
                    yield

                def last():
                  ob = o[0]
                  ss, rs = P.small(4), P.small(4)
                  tm = TM.take()
                  w = tm.refill()
                  for j in range(4):
                      a = act.put(lambda e, j=j: e.activation(
                          tm.ap[:, 0:128], ob.ap[:, j * 128:(j + 1) * 128], ACT.Square, accum_out=ss[:, j:j + 1]), ob.ready, w,
                          a if j else None)
                      w = []
                  p = pow_m05(rs, ss, a, 1.0 / 128, 4)
                  tv, ov = (x.rearrange("p (h d) -> p h d", h=4) for x in (tm.ap, ob.ap))
                  u = dve.put(lambda e: e.tensor_tensor(tv, ov, bc(rs, 2, 128), ALU.mult), p, a)
                  ob.free = [u]
                  u = dve.put(lambda e: e.tensor_tensor(tv, tv, bc(gn.ap[:, 256:384], 1, 4), ALU.mult), u, gn.ready)
                  gn.free.append(u)
                  yield
                  tt, lp_ = to_T(AB, tm.ap, 4, O3.ap, 0, [u, fr], i)
                  tm.free = lp_
                  O3.ready += tt
                  yield
                return [heads(0), heads(1)], last()
            return tiles([tile(0), tile(1)], WIDTH)

        O3 = O1
        mix(linear_a(), now, 1.0)
        bm, bmh, cols_t, bm_t, nlam, nlam_t = (o[k] for k in ("bm", "bmh", "cols_t", "bm_t", "nlam", "nlam_t"))
        P.flush()
        at = Line()

        def merged_begin():
            MT.free = SG.free
            MT.wait = MT.refill()

        def bias(x):
            P.bias = x
        mix(chain(linear_b(), lambda: at.mark("B"), at.until("retention"), linear_c(), P.flush, lambda: at.mark("C"),
                  merged_begin, merge(0, I["w_branch_a"][l], O1, 8), lambda: at.mark("a"),
                  at.until("ca"), merge(1, I["w_branch_b"][l], O2, 4), at.until("da"),
                  merge(2, I["w_branch_c"][l], O3, 4)),
            chain(retention, lambda: at.mark("retention"), at.until("B"), lambda: bias(BT.ready), ca_attention,
                  lambda: bias([]), lambda: at.mark("ca"), at.until("C", "a"), da_attention, lambda: at.mark("da")), RATIO1)
        fr = O1.refill()
        for u in range(4):
            mt = MT.ap.rearrange("p a b -> p (a b)")[:, u * 512:(u + 1) * 512]
            t = split(O1.ap, lambda x, u=u: x[:, 2 * u:2 * u + 2, :], mt.rearrange("p (c t) -> p c t", c=2),
                      [MT.ready[u], fr], scale=0.5 / ALPHA)
            O1.ready += t
        SG.free = [t]
        acc = out_begin()
        out_part(I["w_out"][l], acc, 0)
        layer_norm(acc, bm[:, 24:40], cols_t, [AB, AB], out_end(I["w_out"][l], acc))

        wf = I["w_ffn_in"][l].rearrange("(k p) (g f) -> p k g f", p=128, g=2)

        def gate_up(j):
            src = wf[:, :, :, j * 128:(j + 1) * 128]
            return [(lambda a, g=g: a.rearrange("p (k g c) -> p k g c", k=8, g=2)[:, :, g, :], src[:, :, g, :])
                    for g in range(2)]
        acc, tail = ffn(gate_up, I["w_ffn_out"][l], 1.0, nxt)
        layer_norm(acc, bm[:, 40:56], cols_t, [LB, AB], tail)

    YC = []

    def shared():
        B["w1"] = Buf(m["w1"], B["q0"].free + B["k0"].free + B["v0"].free)
        B["wt"] = Buf(m["wt"], B["v1"].free)
        B["vs"] = Buf(m["vs"], B["v1"].free)
        B["ka"] = Buf(m["ka"], B["k1"].free)
        YC.extend(Buf(m["sg"][:, 1, i * 512:(i + 1) * 512], B["sg"].free) for i in range(2))
        yield

    def swiglu(l, which, setup=iter(())):
        def gate_up(j):
            return [(lambda a, g=g: a.rearrange("p (k g c) -> p k g c", k=8, g=2)[:, :, g, :],
                     I[f"ffn{which}_{nme}_2"][l][:, j * 128:(j + 1) * 128].rearrange("(k p) f -> p k f", p=128))
                    for g, nme in enumerate(("gate", "up"))]
        return ffn(gate_up, I[f"ffn{which}_down_2"][l], 0.5, setup)

    def second_setup(l, o):
        P.small_turn()

        def rows(name):
            return I[name][l].rearrange("(r c) -> r c", c=128)
        lns = ("ln1_g_2", "ln1_b_2", "ln2_g_2", "ln2_b_2", "ln3_g_2", "ln3_b_2")
        turn = staging([(rows(nme), 12 + 8 * n, 20 + 8 * n) for n, nme in enumerate(lns)] +
                       [(I["conv_w_2"][l].rearrange("k (c p) -> (k c) p", p=128), 0, 6), (I["gmlp_b_2"][l], 6, 10),
                        (I["ck_b1_2"][l:l + 1, :], 10, 11), (I["cv_b1_2"][l:l + 1, :], 11, 12)], 60)
        pes = m["stage2"]
        w = P.pe_free
        for n, nme in enumerate(("ck_pe_2", "cv_pe_2")):
            for r in range(2):
                tq = P.load(sp, "pes", pes[0:32, n, r * 64:(r + 1) * 64], I[nme][l], w)
                w = []
        gn = B["gn"]
        w = gn.refill()
        P.load(sp, "gn", gn.ap[:, 0:256], I["gmlp_ln_g_2"][l].partition_broadcast(128), w)
        gn.ready = [P.load(sp, "gn", gn.ap[:, 256:512], I["gmlp_ln_b_2"][l].partition_broadcast(128))]
        w2 = B["w2"]
        w = w2.refill()
        P.load(sp, "w2", w2.ap[:, 0, :], I["ck_w2_2"][l], w)
        w2.ready = [P.load(sp, "w2", w2.ap[:, 1, :], I["cv_w2_2"][l])]
        gw = RT.take()
        tg = P.load(sp, "gw", gw.ap[:, :].rearrange("p (h q) -> p h q", h=4),
                    I["gmlp_w_2"][l].rearrange("h p q -> p h q"), gw.refill())
        yield
        w1 = B["w1"]
        w = w1.refill()
        for n, nme in enumerate(("ck_w1_2", "cv_w1_2")):
            t = P.load(sp, "w1", w1.ap[:, n, :].rearrange("p (j f) -> p j f", j=16),
                       I[nme][l].rearrange("(j l) d f -> (l d) j f", l=2), w)
            w = []
            w1.ready = [t]
            yield
        cols, cols_t = turn()
        b = LB.take()

        def go(e):
            e.transpose(b.ap[:, 0:32], pes[0:32, 0, :], ident[0:32, 0:32])
            return e.transpose(b.ap[:, 32:64], pes[0:32, 1, :], ident[0:32, 0:32])
        tp = pe.put(go, tq, b.refill(), consts)
        P.pe_free = [tp]
        pet = P.small(64)
        pet_t = dve.put(lambda e: e.tensor_copy(pet, b.ap[:, 0:64]), tp)
        b.free = [pet_t]
        t = dve.put(lambda e: e.tensor_tensor(gw.ap.rearrange("p (h q) -> p h q", h=4),
                                              gw.ap.rearrange("p (h q) -> p h q", h=4), bc(C("tril"), 1, 4), ALU.mult), tg, consts)
        yield
        wt = B["wt"]
        tb = transposes(LB, [gw.ap[:, h * 128:(h + 1) * 128] for h in range(4)], t)
        gw.free = [*tb.ready]
        t = act.put(lambda e: e.activation(wt.ap, tb.ap, ACT.Copy), tb.ready, wt.refill())
        tb.free = [t]
        wt.ready = [t]
        o.update(cols=cols, cols_t=cols_t, pet=pet, pet_t=pet_t)

    def second(l, o, nxt):
        cols, cols_t, pet, pet_t = (o[k] for k in ("cols", "cols_t", "pet", "pet_t"))
        gn, w1, w2, wt = (B[k] for k in ("gn", "w1", "w2", "wt"))
        acc, tail = swiglu(l, 1)
        layer_norm(acc, cols[:, 12:28], cols_t, [LB, AB], tail)

        w_in = I["w_in_2"][l]
        frO = O1.refill()

        kcs = P.small(15)
        vcs = m["vcs"]
        ka = B["ka"]
        comp = {}

        def compress(n, bank):
            src = bank.ap[:, 256 * n:256 * n + 256].rearrange("p (t s) -> p s t", s=16)
            w = ka.refill()
            kv = ka.ap.rearrange("p (j g n) -> p j g n", j=16, g=2)
            for g in range(2):
                for par in range(2):
                    for a_ in range(2):
                        u = dve.put(lambda e, g=g, par=par, a_=a_, n=n: e.tensor_tensor(
                            kv[64 * par:64 * par + 64, 8 * a_:8 * a_ + 8, g, :],
                            src[64 * g:64 * g + 64, par::2, a_:a_ + 15],
                            bc(pet[64 * g:64 * g + 64, 32 * n + par + 16 * a_:32 * n + 16 * a_ + 16:2], 2, 15),
                            ALU.add), w, bank.ready, pet_t)
                        w = []
            if n:
                bank.free = [u]
            yield
            hb = AB.take()

            def go(e):
                for j in range(16):
                    ins = e.matmul(hb.ap[0:30, 0:128], ka.ap[:, j * 30:(j + 1) * 30], w1.ap[:, n, j * 128:(j + 1) * 128],
                                   start=j == 0, stop=j == 15)
                return ins
            t = pe.put(go, u, w1.ready, hb.refill())
            ka.free = [t]
            w1.free.append(t)
            tm = TM.take()
            a = act.put(lambda e: e.activation(tm.ap[0:30, 0:128], hb.ap[0:30, 0:128], ACT.Copy), t, tm.refill())
            hb.free = [a]
            yield
            hb2 = AB.take()
            t = pe.put(lambda e: e.transpose(hb2.ap[:, 0:30], tm.ap[0:30, 0:128], ident[0:30, 0:30]), a, hb2.refill(), consts)
            tm.free = [t]
            x, y, z = P.small(30), P.small(30), P.small(30)
            v = dve.put(lambda e: e.tensor_scalar(x, hb2.ap[:, 0:30], cols[:, 10 + n:11 + n], None, ALU.add), t, cols_t)
            hb2.free = [v]
            v = dve.put(lambda e: e.tensor_tensor(y, x, x, ALU.mult), v)
            v = dve.put(lambda e: e.tensor_scalar(y, y, GC, 1.0, ALU.mult, ALU.add), v)
            v = dve.put(lambda e: e.tensor_tensor(y, y, x, ALU.mult), v)
            a = act.put(lambda e: e.activation(z, y, ACT.Tanh, scale=GS), v)
            v = dve.put(lambda e: e.scalar_tensor_tensor(y, z, 1.0, x, ALU.add, ALU.mult), a)
            yield
            ob = AB.take()
            if n == 0:
                def go2(e):
                    e.matmul(ob.ap[0:64, 0:15], w2.ap[:, 0, :], y[:, 0:15], start=True, stop=True)
                    return e.matmul(ob.ap[64:128, 0:15], w2.ap[:, 0, :], y[:, 15:30], start=True, stop=True)
            else:
                def go2(e):
                    e.matmul(ob.ap[0:15, 0:64], y[:, 0:15], w2.ap[:, 1, :], start=True, stop=True)
                    return e.matmul(ob.ap[0:15, 64:128], y[:, 15:30], w2.ap[:, 1, :], start=True, stop=True)
            t = pe.put(go2, v, w2.ready, ob.refill())
            w2.free.append(t)
            if n == 0:
                a = act.put(lambda e: e.activation(kcs, ob.ap[:, 0:15], ACT.Copy, scale=0.5), t)
            else:
                a = act.put(lambda e: e.activation(vcs[:, :], ob.ap[0:15, 0:128], ACT.Copy, scale=0.5), t, P.vcs_free)
            ob.free = [a]
            comp[n] = a
            yield

        KS, VS, Q = B["k1"], B["vs"], B["q1"]

        def lin_cmp():
            b, = proj_T(w_in, 1792, XT)
            comp["b"] = b
            at.mark("kc")
            yield
            segs, n = wk(w_in, 0, 8, 2560, 24)
            ghi, glo, gub = P.unit(segs, n)
            ghi, glo = (x.rearrange("p (k c) -> p k c", k=8) for x in (ghi, glo))
            gbk = LB.take()

            def go(e):
                for k in range(8):
                    ins = mm3(e, gbk.ap[0:24, 0:256], [ghi[:, k, :], glo[:, k, :]],
                              [XT.ap[:, z, k, :] for z in (0, 1)], k == 0, k == 7)
                return ins
            t = pe.put(go, gub.ready, gbk.refill(), XT.ready)
            gub.free = [t]
            XT.free.append(t)
            tm = TM.take()
            a = act.put(lambda e: e.activation(tm.ap[0:24, 0:256], gbk.ap[0:24, 0:256], ACT.Tanh, scale=0.5), t, tm.refill())
            gbk.free = [a]
            yield
            gbk2 = LB.take()

            def go(e):
                e.transpose(gbk2.ap[:, 0:24], tm.ap[0:24, 0:128], ident[0:24, 0:24])
                return e.transpose(gbk2.ap[:, 24:48], tm.ap[0:24, 128:256], ident[0:24, 0:24])
            t = pe.put(go, a, gbk2.refill(), consts)
            tm.free = [t]
            comp["g"] = dve.put(lambda e: e.tensor_scalar(gts, gbk2.ap[:, 0:48], 0.5, 0.5, ALU.mult, ALU.add), t)
            gbk2.free = [comp["g"]]
            at.mark("g")
            yield

        def lin_kv():
            fr = Q.refill()
            yield from proj_N(w_in, 768, XT)
            bk = P.res
            SGb = B["sg"]
            w = SGb.refill()
            comp["uv"] = (bk, SGb.ap[:, 0, :].rearrange("p (i c) -> p i c", i=2), SGb, w)
            at.mark("uv")
            two = [[(lambda a, g=g, c=c: a.rearrange("p (k c g d) -> p k c g d", k=8, g=2, c=2)[:, :, c, g, :],
                     w_in[:, 1280 + g * 256 + u * 128 + c * 64:1280 + g * 256 + u * 128 + c * 64 + 64]
                     .rearrange("(k p) d -> p k d", p=128))
                    for g in range(2) for c in range(2)] for u in range(2)]
            for u in range(2):
                bk = t_unit(XT, 8, lambda a, k, c: a.rearrange("p (k c) -> p k c", k=8)[:, k, c * 128:(c + 1) * 128],
                            UNIT, two[u], 2, LB)
                copy_T(bk, Q, 2 * u, 0.125, fr)
                yield
            fr = KS.refill()
            segs = [(lambda a, g=g: a.rearrange("p (k g c) -> p k g c", k=8, g=2)[:, :, g, :],
                     w_in[:, 2048 + g * 256:2048 + g * 256 + 128].rearrange("(k p) c -> p k c", p=128)) for g in range(2)]
            bk = t_unit(XT, 8, lambda a, k, c: a.rearrange("p (k g c) -> p k g c", k=8, g=2)[:, k, c, :],
                        UNIT, segs, 2, LB)
            copy_T(bk, KS, 0, 1.0, fr)
            yield
            fr = VS.refill()
            segs = [(lambda a, g=g: a.rearrange("p (k g c) -> p k g c", k=8, g=2)[:, :, g, :],
                     w_in[:, 2176 + g * 256:2176 + g * 256 + 128].rearrange("(k p) c -> p k c", p=128)) for g in range(2)]
            hi, lo, ub = P.unit(segs, UNIT)
            hi, lo = (x.rearrange("p (k c) -> p k c", k=8) for x in (hi, lo))
            bk = LB.take()

            def go(e):
                for i in range(2):
                    for k in range(8):
                        ins = mm3(e, bk.ap[:, i * 256:(i + 1) * 256], [XT.ap[:, z, k, i * 128:(i + 1) * 128] for z in (0, 1)],
                                  [hi[:, k, :], lo[:, k, :]], k == 0, k == 7)
                return ins
            t = pe.put(go, ub.ready, bk.refill(), XT.ready)
            ub.free = [t]
            XT.free.append(t)
            a = act.put(lambda e: e.activation(VS.ap[:, :, 0:256], bk.ap.rearrange("p (i c) -> p i c", i=2), ACT.Copy), t, fr)
            bk.free = [a]
            VS.ready = [a]
            yield
        gts = P.small(48)

        def lin_rest():
            bh, = proj_T(w_in, 0, XT)
            hs = TH.take()
            a = act.put(lambda e: e.activation(hs.ap, bh.ap, ACT.Copy), bh.ready, hs.refill())
            bh.free = [a]
            yield
            bb, = proj_T(w_in, 256, XT)
            yield
            bcg, = proj_T(w_in, 512, XT)
            z = m["zb"]
            v = dve.put(lambda e: e.tensor_tensor(z[:, :, 2:258], hs.ap.rearrange("p (c t) -> p c t", c=2),
                                                  bcg.ap.rearrange("p (c t) -> p c t", c=2), ALU.mult), a, bcg.ready)
            bcg.free = [v]
            hs.free = [v]
            yt = TM.take()
            w = yt.refill()
            for c in range(2):
                ya = yt.ap[:, c * 256:(c + 1) * 256]
                u = dve.put(lambda e, c=c, ya=ya: e.tensor_scalar(ya, z[:, c, 2:258], cols[:, 4 + c:5 + c], None, ALU.mult), v, w, cols_t)
                w = []
                for k in (1, 0):
                    u = dve.put(lambda e, c=c, ya=ya, k=k: e.scalar_tensor_tensor(
                        ya, z[:, c, k:k + 256], cols[:, 2 * k + c:2 * k + c + 1], ya, ALU.mult, ALU.add), u)
            u = dve.put(lambda e: e.tensor_tensor(yt.ap, yt.ap, bb.ap, ALU.mult), u, bb.ready)
            bb.free = [u]
            t = split(O1.ap, lambda x: x[:, 0:2, :], yt.ap.rearrange("p (c t) -> p c t", c=2), [u, frO], 1.0 / ALPHA)
            yt.free = t
            O1.ready += t
            yield

        def gmlp(i):
                bk, zz, SGb, w = comp["uv"]
                t1, th = TM.take(), TH.take()
                a = act.put(lambda e, i=i, t1=t1: e.activation(t1.ap, bk[i].ap, ACT.Square), bk[i].ready, t1.refill())
                v = dve.put(lambda e, t1=t1: e.tensor_scalar(t1.ap, t1.ap, GC, 1.0, ALU.mult, ALU.add), a)
                v = dve.put(lambda e, i=i, t1=t1: e.tensor_tensor(t1.ap, t1.ap, bk[i].ap, ALU.mult), v)
                a = act.put(lambda e, t1=t1, th=th: e.activation(th.ap, t1.ap, ACT.Tanh, scale=GS), v, th.refill())
                a = act.put(lambda e, i=i, t1=t1: e.activation(t1.ap, bk[i].ap, ACT.Copy, scale=0.5), a)
                bk[i].free = [a]
                v = dve.put(lambda e, i=i, t1=t1, th=th: e.scalar_tensor_tensor(zz[:, i, :], th.ap, 1.0, t1.ap, ALU.add, ALU.mult), a, w)
                w = []
                t1.free = [v]
                th.free = [v]
                st, mv, rs = P.small(6), P.small(2), P.small(1)
                vi = zz[:, i, 256:512]
                v = dve.put(lambda e, vi=vi, st=st: e.bn_stats(st, vi), v)
                v = dve.put(lambda e, st=st, mv=mv: e.bn_aggr(mv, st), v)
                p = pow_m05(rs, mv[:, 1:2], v, 1.0, 1)
                v = dve.put(lambda e, vi=vi, mv=mv, rs=rs: e.tensor_scalar(vi, vi, mv[:, 0:1], rs, ALU.subtract, ALU.mult), p)
                v = dve.put(lambda e, vi=vi: e.tensor_tensor(vi, vi, gn.ap[:, 0:256], ALU.mult), v, gn.ready)
                v = dve.put(lambda e, vi=vi: e.tensor_tensor(vi, vi, gn.ap[:, 256:512], ALU.add), v)
                gn.free = [v]
                yield
                sb_ = AB.take()

                def go(e, i=i, sb_=sb_):
                    for h in range(4):
                        ins = e.matmul(sb_.ap[:, h * 64:(h + 1) * 64], wt.ap[:, h * 128:(h + 1) * 128],
                                       zz[:, i, 256 + h * 64:256 + (h + 1) * 64], start=True, stop=True)
                    return ins
                t = pe.put(go, v, wt.ready, sb_.refill())
                wt.free.append(t)
                for h in range(4):
                    us = zz[:, i, h * 64:(h + 1) * 64]
                    v = dve.put(lambda e, us=us, h=h, sb_=sb_: e.scalar_tensor_tensor(
                        us, sb_.ap[:, h * 64:(h + 1) * 64], cols[:, 6 + h:7 + h], us, ALU.add, ALU.mult), t, cols_t)
                sb_.free = [v]
                yield
                tt, lp_ = to_T(AB, zz[:, i, 0:256], 2, O1.ap, 2, [v, frO], i, 1.0 / ALPHA)
                SGb.free += lp_ + [t]
                O1.ready += tt
                yield

        at = Line()

        def nsa():
            def extra(j, hh, i):
                return [(128 * i, causalb, identb)]
            rss = [(P.small(24), P.small(24)) for _ in range(2)]

            def collect(i, bno, ob, waits, first):
                yc, (rs, rc) = YC[i], rss[i]
                gv = gts[:, 24 * i:24 * i + 24].rearrange("p (h b) -> p h b", b=3)
                r_ = rc[:, 8 * bno:8 * bno + 8]
                u = dve.put(lambda e: e.reciprocal(r_, rs[:, 8 * bno:8 * bno + 8]), waits)
                u = dve.put(lambda e: e.tensor_tensor(r_, r_, gv[:, :, bno], ALU.mult), u, comp["g"])
                ov = ob.ap.rearrange("p (h d) -> p h d", h=8)
                if first:
                    u = dve.put(lambda e: e.tensor_tensor(yc.ap.rearrange("p (h d) -> p h d", h=8), ov, bc(r_, 2, 64), ALU.mult),
                                u, ob.ready, yc.refill())
                    ob.free = [u]
                else:
                    tm = TM.take()
                    u = dve.put(lambda e: e.tensor_tensor(tm.ap.rearrange("p (h d) -> p h d", h=8), ov, bc(r_, 2, 64), ALU.mult),
                                u, ob.ready, tm.refill())
                    ob.free = [u]
                    u = dve.put(lambda e: e.tensor_tensor(yc.ap, yc.ap, tm.ap, ALU.add), u, yc.ready)
                    tm.free = [u]
                yc.ready = [u]

            def compressed(i):
                rs, rc = rss[i]
                er = ER.take()
                ev = er.ap[:, 0:120].rearrange("p (h n) -> p h n", h=8)
                w = er.refill()
                for hh in range(2):
                    b = AB.take()

                    def go(e, hh=hh, b=b):
                        for j in range(4):
                            ins = e.matmul(b.ap[:, j * 15:(j + 1) * 15], Q.ap[64 * hh:64 * hh + 64, j, i * 128:(i + 1) * 128],
                                           kcs[64 * hh:64 * hh + 64, :], start=True, stop=True)
                        return ins
                    t = pe.put(go, b.refill(), Q.ready, comp[0])
                    Q.free.append(t)
                    v = dve.put(lambda e, hh=hh, b=b: e.tensor_tensor(
                        ev[:, 4 * hh:4 * hh + 4, :], b.ap[:, 0:60].rearrange("p (h n) -> p h n", h=4),
                        bc(C("am")[:, 15 * i:15 * i + 15], 1, 4), ALU.add), t, w)
                    w = []
                    b.free = [v]
                mx = P.small(8)
                v = dve.put(lambda e: e.tensor_reduce(mx, ev, AX, ALU.max), v)
                v = dve.put(lambda e: e.tensor_tensor(ev, ev, bc(mx, 2, 15), ALU.subtract), v)
                a = act.put(lambda e: e.activation(er.ap[:, 0:120], er.ap[:, 0:120], ACT.Exp), v)
                v1_ = dve.put(lambda e: e.tensor_reduce(rs[:, 0:8], ev, AX, ALU.add), a)
                v = dve.put(lambda e: e.tensor_tensor(ev, ev, bc(C("mm")[:, 15 * i:15 * i + 15], 1, 8), ALU.mult), a, v1_)
                yield
                etv = []
                for half in range(2):
                    tb = AB.take()

                    def go(e, half=half, tb=tb):
                        for h in range(4):
                            x = 4 * half + h
                            ins = e.transpose(tb.ap[0:15, h * 128:(h + 1) * 128], er.ap[:, x * 15:(x + 1) * 15], ident)
                        return ins
                    t = pe.put(go, v, tb.refill(), consts)
                    et = ET.take()
                    a = act.put(lambda e, et=et, tb=tb: e.activation(et.ap[0:15, :], tb.ap[0:15, :], ACT.Copy), t, et.refill())
                    tb.free = [a]
                    etv.append((et, a))
                er.free = [t]
                yield
                ob = AB.take()

                def go(e):
                    for h in range(8):
                        g = h // 4
                        ins = e.matmul(ob.ap[:, h * 64:(h + 1) * 64], etv[g][0].ap[0:15, (h % 4) * 128:(h % 4 + 1) * 128],
                                       vcs[:, g * 64:(g + 1) * 64], start=True, stop=True)
                    return ins
                t = pe.put(go, ob.refill(), etv[0][1], etv[1][1], comp[1])
                etv[0][0].free = [t]
                etv[1][0].free = [t]
                P.vcs_free = [t]
                ob.ready = [t]
                collect(i, 0, ob, [v1_], False)
                yield

            def full(i, bno):
                rs, rc = rss[i]
                o, ends = [], []

                def K(hh, j, rdy=False):
                    return KS.ready if rdy else KS.ap[64 * hh:64 * hh + 64, bno - 1, :]

                def vof(mt, vs):
                    return VS.ap[:, mt, (bno - 1) * 128 + vs * 64:(bno - 1) * 128 + (vs + 1) * 64]

                def heads(jp, hh):
                    js = (2 * jp, 2 * jp + 1)
                    hs = [hh * 4 + j for j in js]
                    ob = sums(o, VS)
                    er, t = scores(Q, K, js, hh, i, extra, [rs[:, 8 * bno + h:8 * bno + h + 1] for h in hs])
                    KS.free.append(t)
                    ends.append(er.ready)
                    yield
                    yield
                    yield from weigh(er, [(h, hh) for h in hs], i, ob, vof, 64, VS.free)
                    yield

                def last():
                    yield from at.until("g")
                    collect(i, bno, o[0], ends, bno == 1)
                    at.mark(f"full{i}{bno}")
                    yield
                return [heads(jp, hh) for jp in range(2) for hh in range(2)], last()

            def finish(i):
                yc = YC[i]
                tt, lp_ = to_T(AB, yc.ap, 4, O1.ap, 4, [yc.ready, frO], i, 1.0 / ALPHA)
                yc.free = lp_
                O1.ready += tt
                yield
            return chain(weave([tiles([full(0, 1), full(0, 2), full(1, 1), full(1, 2)], WIDTH),
                          chain(at.until("kc"), lambda: compress(0, comp["b"]), lambda: compress(1, comp["b"]),
                                at.until("full11"), compressed(0), lambda: at.mark("comp0"), at.until("full11"),
                                compressed(1), lambda: at.mark("comp1"))                          ], 3), finish(0), finish(1))

        mix(lin_kv(), chain(at.until("uv"), lambda: weave([gmlp(0), gmlp(1)], 2)), 1.5)

        def tail():
            P.flush()
            acc_.append(out_begin())
            out_part(I["w_out_2"][l], acc_[0], 0)
            yield
        acc_ = []
        mix(chain(lin_cmp(), lin_rest(), tail()), nsa(), RATIO2)
        acc = acc_[0]
        layer_norm(acc, cols[:, 28:44], cols_t, [AB, AB], out_end(I["w_out_2"][l], acc))
        if l == DEPTH - 1:
            load_gb(I["ln3_g_2"][l], I["ln3_b_2"][l])
        acc, tail = swiglu(l, 2, nxt)
        return layer_norm(acc, cols[:, 44:60], cols_t, [LB, AB], tail, final=l == DEPTH - 1)

    os_ = [{} for _ in range(2 * DEPTH)]
    for l in range(DEPTH):
        first(l, os_[l], iter(()) if l else first_setup(0, os_[0]), first_setup(l + 1, os_[l + 1]) if l + 1 < DEPTH else chain(shared, lambda: second_setup(0, os_[DEPTH])))
    for l in range(DEPTH):
        outs = second(l, os_[DEPTH + l], second_setup(l + 1, os_[DEPTH + l + 1]) if l + 1 < DEPTH else iter(()))
    sp.items.append((lambda e: None, outs, Tok(), None))


def build(nc, I, out_ap):
    with ExitStack() as ctx:
        def sb(name, shape, dt=F):
            return ctx.enter_context(nc.sbuf_tensor(name, shape, dt))

        m = {
            "raw": sb("raw", [128, NRAW, UNIT]), "hl": sb("hl", [128, NHL, 2, UNIT], R),
            "const": sb("cst", [128, NCONST]), "maskb": sb("maskb", [128, 3, 128], BF),
            "x": sb("xs", [128, 2, D]), "xt": sb("xt", [128, 2, 8, S], R),
            "o1": sb("o1", [128, 2, 8, S], R), "o2": sb("o2", [128, 2, 4, S], R), "gb": sb("gb", [128, 2, D]),
            "th": sb("th", [128, 2, 512]), "tm": sb("tm", [128, 5, 512]), "rt": sb("rt", [128, 2, 512]), "er": sb("er", [128, 5, 512]),
            "ai": sb("ai", [128, 128], R), "et": sb("et", [128, 3, 512]), "mhalf": sb("mhalf", [128, 8]), "small": sb("small", [128, 1340]),
            "stage": sb("stage", [64, 128]), "stage2": sb("stage2", [32, 2, 128]), "gn": sb("gn", [128, 512]),
            "vcs": sb("vcs", [15, 128]), "zb": sb("zb", [128, 2, 258]),
            "q1": sb("q1", [128, 4, S]), "k1": sb("k1", [128, 4, S]), "sg": sb("sg", [128, 2, 1024]),
            "w2": sb("w2", [128, 2, 64]),
            "psum": ctx.enter_context(nc.psum_tensor("ps", [128, 8, 512], F)),
        }
        m = {k: v[:] for k, v in m.items()}
        qkv, v1 = sb("qkv", [128, 4096])[:], sb("v1", [128, 1024])[:]
        m["q0"] = qkv[:, 0:1024].rearrange("p (j t) -> p j t", j=4)
        m["k0"] = qkv[:, 1024:2048].rearrange("p (j t) -> p j t", j=4)
        m["v0"] = qkv[:, 2048:4096].rearrange("p (i c) -> p i c", i=2)
        m["w1"] = qkv.rearrange("p (n c) -> p n c", n=2)
        m["v1"] = v1.rearrange("p (i c) -> p i c", i=2)
        m["vs"] = v1[:, 0:512].rearrange("p (i c) -> p i c", i=2)
        m["wt"] = v1[:, 512:1024]
        m["ka"] = m["k1"].rearrange("p j t -> p (j t)")[:, 512:992]
        sems = {k: ctx.enter_context(nc.semaphore("s_" + k)) for k in
                ["pe", "act", "dve", "pool", "sp", "const", "ident", "x", "gb", "stage", "gn", "lv", "pes", "w2", "w1", "gw",
                 "out0", "out1"] + [f"raw{i}" for i in range(NRAW)]}
        units = None
        for _ in range(2):
            P = Program(m, sems, units)
            P.pe_free, P.vcs_free = [], []
            script(P, I, out_ap)
            units = P.units
        for q in (P.pe, P.act, P.dve, P.pool, P.sp):
            q.number()
        block = ctx.enter_context(nc.Block())
        block.sync(P.sp.emit)
        block.tensor(P.pe.emit)
        block.vector(P.dve.emit)
        block.scalar(P.act.emit)
        block.gpsimd(P.pool.emit)


_INS = ["x", "w_in", "ret_norm_g", "ca_rel_bias", "da_lambda_q1", "da_lambda_k1", "da_lambda_q2", "da_lambda_k2",
        "da_norm_g", "w_branch_a", "w_branch_b", "w_branch_c", "b_merge", "w_out", "ln1_g", "ln1_b", "w_ffn_in",
        "w_ffn_out", "ln2_g", "ln2_b", "ffn1_gate_2", "ffn1_up_2", "ffn1_down_2", "ln1_g_2", "ln1_b_2", "w_in_2",
        "conv_w_2", "gmlp_ln_g_2", "gmlp_ln_b_2", "gmlp_w_2", "gmlp_b_2", "ck_pe_2", "ck_w1_2", "ck_b1_2", "ck_w2_2",
        "cv_pe_2", "cv_w1_2", "cv_b1_2", "cv_w2_2", "w_out_2", "ln2_g_2", "ln2_b_2", "ffn2_gate_2", "ffn2_up_2",
        "ffn2_down_2", "ln3_g_2", "ln3_b_2"]


def kernel(**inputs):
    import concourse.bacc as bacc
    from concourse.bass_utils import run_bass_kernel_spmd

    nc = bacc.Bacc("TRN2", target_bir_lowering=False, num_devices=1, dynamic_dma_scratch_size=256)
    arrays, aps = {}, {}
    for name in _INS:
        a = np.ascontiguousarray(inputs[name])
        arrays["in_" + name] = a
        aps[name] = nc.dram_tensor("in_" + name, a.shape, mybir.dt.from_np(a.dtype), kind="ExternalInput").ap()
    arrays["in_const"] = constants()
    aps["const"] = nc.dram_tensor("in_const", (128, NCONST), F, kind="ExternalInput").ap()
    out = nc.dram_tensor("out", (1, S, D), F, kind="ExternalOutput").ap()
    build(nc, aps, out)
    r = run_bass_kernel_spmd(nc, [arrays], core_ids=[0])
    return r.results[0]["out"]
```
